# Optimizing a Trainium2 kernel written in Bass

```python
import math
import jax, jax.numpy as jnp
from jax import lax
import numpy as np

D_MODEL = 1024
BATCH = 1
SEQ = 512
DEPTH = 1

D_MIX = D_MODEL
ATTN_WIDTH = D_MIX // 2
HEAD_DIM = 64
N_HEADS = ATTN_WIDTH // HEAD_DIM
CONV_WIDTH = D_MIX - ATTN_WIDTH
CONV_GROUPS = CONV_WIDTH // HEAD_DIM
CONV_K = 31
D_IN = 3 * ATTN_WIDTH + N_HEADS + 2 * CONV_WIDTH
D_FF = int(math.ceil((8 * D_MODEL / 3) / 256) * 256)
Q_BLOCK = 128
N_MOD = 6
EPS = 1e-6


def rms_norm(x, g):
    xf = x.astype(jnp.float32)
    y = xf * lax.rsqrt(jnp.mean(xf * xf, axis=-1, keepdims=True) + EPS)
    return (y * g.astype(jnp.float32)).astype(x.dtype)

def layer_norm(x, g, b):
    xf = x.astype(jnp.float32)
    mu = jnp.mean(xf, axis=-1, keepdims=True)
    var = jnp.mean(jnp.square(xf - mu), axis=-1, keepdims=True)
    y = (xf - mu) * lax.rsqrt(var + EPS)
    return (y * g.astype(jnp.float32) + b.astype(jnp.float32)).astype(x.dtype)

def fox_attention(q, k, v, log_f):
    B, S, H, Dh = q.shape
    nb = S // Q_BLOCK
    scale = Dh ** -0.5
    cum = jnp.cumsum(log_f, axis=1)
    cum_k = jnp.transpose(cum, (0, 2, 1))[:, :, None, :]
    q_blocks = jnp.transpose(q.reshape(B, nb, Q_BLOCK, H, Dh), (1, 0, 2, 3, 4))
    c_blocks = jnp.transpose(cum.reshape(B, nb, Q_BLOCK, H), (1, 0, 3, 2))
    k_pos = jnp.arange(S, dtype=jnp.int32)

    def one_block(args):
        i, q_blk, c_blk = args
        s = jnp.einsum('bqhd,bkhd->bhqk', q_blk, k).astype(jnp.float32) * scale
        s = s + c_blk[..., None] - cum_k
        q_pos = i * Q_BLOCK + jnp.arange(Q_BLOCK, dtype=jnp.int32)
        mask = k_pos[None, :] <= q_pos[:, None]
        s = jnp.where(mask[None, None], s, -jnp.inf)
        p = jax.nn.softmax(s, axis=-1)
        return jnp.einsum('bhqk,bkhd->bqhd', p.astype(v.dtype), v)

    outs = lax.map(one_block, (jnp.arange(nb, dtype=jnp.int32), q_blocks, c_blocks))
    return jnp.transpose(outs, (1, 0, 2, 3, 4)).reshape(B, S, H * Dh)

def causal_depthwise_conv(u, w, b):
    C = u.shape[-1]
    out = lax.conv_general_dilated(
        u, w[:, None, :].astype(u.dtype), window_strides=(1,), padding=((CONV_K - 1, 0),),
        dimension_numbers=('NWC', 'WIO', 'NWC'), feature_group_count=C)
    return out + b.astype(u.dtype)

def hybrid_mixer(h, w_in, b_f, conv_w, conv_b, conv_ln_g, conv_ln_b, w_o):
    B, S, _ = h.shape
    proj = h @ w_in
    splits = [ATTN_WIDTH, 2 * ATTN_WIDTH, 3 * ATTN_WIDTH, 3 * ATTN_WIDTH + N_HEADS,
              3 * ATTN_WIDTH + N_HEADS + CONV_WIDTH]
    q, k, v, f_logit, conv_val, conv_gate = jnp.split(proj, splits, axis=-1)
    q = q.reshape(B, S, N_HEADS, HEAD_DIM)
    k = k.reshape(B, S, N_HEADS, HEAD_DIM)
    v = v.reshape(B, S, N_HEADS, HEAD_DIM)
    log_f = jax.nn.log_sigmoid((f_logit + b_f).astype(jnp.float32))
    attn = fox_attention(q, k, v, log_f)
    u = conv_val * jax.nn.sigmoid(conv_gate)
    u = causal_depthwise_conv(u, conv_w, conv_b)
    u = jax.nn.silu(layer_norm(u, conv_ln_g, conv_ln_b))
    return jnp.concatenate([attn, u], axis=-1) @ w_o

def swiglu_ffn(h, w_ffn_in, w_ffn_out):
    g, u = jnp.split(h @ w_ffn_in, 2, axis=-1)
    return (jax.nn.silu(g) * u) @ w_ffn_out

def first_inputs(seed: int = 0) -> dict:
    key = jax.random.key(seed)
    ks = jax.random.split(key, 24)
    f32 = jnp.float32
    L, D = DEPTH, D_MODEL

    def nrm(k, shape, s):
        return jax.random.normal(k, shape, f32) * s

    x = jax.random.normal(ks[0], (BATCH, SEQ, D), f32)
    c = jax.random.normal(ks[1], (BATCH, D), f32)
    w_in = jnp.concatenate([
        nrm(ks[2], (L, D, 3 * ATTN_WIDTH), D ** -0.5),
        nrm(ks[3], (L, D, N_HEADS), 0.5 * D ** -0.5),
        nrm(ks[4], (L, D, 2 * CONV_WIDTH), D ** -0.5),
    ], axis=-1)
    b_f = 2.5 + 0.5 * jax.random.normal(ks[5], (L, N_HEADS), f32)
    conv_w = nrm(ks[6], (L, CONV_K, CONV_WIDTH), CONV_K ** -0.5)
    conv_b = nrm(ks[7], (L, CONV_WIDTH), 0.01)
    conv_ln_g = 1.0 + nrm(ks[8], (L, CONV_WIDTH), 0.05)
    conv_ln_b = nrm(ks[9], (L, CONV_WIDTH), 0.01)
    w_o = nrm(ks[10], (L, D_MIX, D), D_MIX ** -0.5)
    w_ffn_in = nrm(ks[11], (L, D, 2 * D_FF), D ** -0.5)
    w_ffn_out = nrm(ks[12], (L, D_FF, D), D_FF ** -0.5)
    mix_pre_g = 1.0 + nrm(ks[13], (L, D), 0.05)
    mix_post_g = 1.0 + nrm(ks[14], (L, D), 0.05)
    ffn_pre_g = 1.0 + nrm(ks[15], (L, D), 0.05)
    ffn_post_g = 1.0 + nrm(ks[16], (L, D), 0.05)
    ada_w = nrm(ks[17], (L, D, N_MOD * D), 0.5 * D ** -0.5)
    ada_b = nrm(ks[18], (L, N_MOD * D), 0.01)
    return {"x": x, "c": c, "w_in": w_in, "b_f": b_f, "conv_w": conv_w, "conv_b": conv_b,
            "conv_ln_g": conv_ln_g, "conv_ln_b": conv_ln_b, "w_o": w_o,
            "w_ffn_in": w_ffn_in, "w_ffn_out": w_ffn_out,
            "mix_pre_g": mix_pre_g, "mix_post_g": mix_post_g,
            "ffn_pre_g": ffn_pre_g, "ffn_post_g": ffn_post_g,
            "ada_w": ada_w, "ada_b": ada_b}

def first_block(x, c, w_in, b_f, conv_w, conv_b, conv_ln_g, conv_ln_b, w_o,
              w_ffn_in, w_ffn_out, mix_pre_g, mix_post_g, ffn_pre_g, ffn_post_g,
              ada_w, ada_b):
    c_act = jax.nn.silu(c)
    for i in range(DEPTH):
        mod = c_act @ ada_w[i] + ada_b[i]
        sh1, sc1, g1, sh2, sc2, g2 = [m[:, None, :] for m in jnp.split(mod, N_MOD, axis=-1)]
        h = rms_norm(x, mix_pre_g[i]) * (1.0 + sc1) + sh1
        y = hybrid_mixer(h, w_in[i], b_f[i], conv_w[i], conv_b[i], conv_ln_g[i], conv_ln_b[i], w_o[i])
        x = x + g1 * rms_norm(y, mix_post_g[i])
        h = rms_norm(x, ffn_pre_g[i]) * (1.0 + sc2) + sh2
        y = swiglu_ffn(h, w_ffn_in[i], w_ffn_out[i])
        x = x + g2 * rms_norm(y, ffn_post_g[i])
    return x


DEPTH_2 = 2

N_A_LAYERS = DEPTH_2 // 2
N_B_LAYERS = DEPTH_2 - N_A_LAYERS

M_EXPAND = 2
M_D_INNER = M_EXPAND * D_MODEL
M_HEADDIM = 64
M_HEADS = M_D_INNER // M_HEADDIM
M_GROUPS = 4
M_D_STATE = 128
M_D_CONV = 4
M_CHUNK = 128
M_CONV_DIM = M_D_INNER + 2 * M_GROUPS * M_D_STATE
M_IN_DIM = 2 * M_D_INNER + 2 * M_GROUPS * M_D_STATE + M_HEADS

SB_HEAD_DIM = 64
SB_HEADS = D_MODEL // SB_HEAD_DIM
SB_WIDTH = SB_HEADS * SB_HEAD_DIM
SB_BLOCK = 128


def _rmsnorm(x, g):
    xf = x.astype(jnp.float32)
    xf = xf * lax.rsqrt(jnp.mean(xf * xf, axis=-1, keepdims=True) + EPS)
    return (xf * g.astype(jnp.float32)).astype(x.dtype)

def _modulate(x, g, shift, scale):
    return _rmsnorm(x, g) * (1.0 + scale[:, None, :]) + shift[:, None, :]

def _causal_dwconv(u, w, b):
    k = w.shape[0]
    out = lax.conv_general_dilated(
        u, w[:, None, :].astype(u.dtype), window_strides=(1,), padding=[(k - 1, 0)],
        dimension_numbers=('NWC', 'WIO', 'NWC'), feature_group_count=u.shape[-1])
    return out + b

def _ssd_chunked(xs, dt, a_neg, bm, cm):
    b, s, h, p = xs.shape
    g, n = bm.shape[2], bm.shape[3]
    hg = h // g
    nc = s // M_CHUNK
    xdt = (xs.astype(jnp.float32) * dt[..., None]).reshape(b, s, g, hg, p)
    a = (dt * a_neg).reshape(b, s, g, hg)

    def chunks(t):
        return jnp.moveaxis(t.reshape((b, nc, M_CHUNK) + t.shape[2:]), 1, 0)

    causal = jnp.tril(jnp.ones((M_CHUNK, M_CHUNK), dtype=bool))[None, :, :, None, None]

    def step(state, inp):
        xc, ac, bc, cc = inp
        acum = jnp.cumsum(ac, axis=1)
        seg = jnp.where(causal, acum[:, :, None] - acum[:, None, :], -jnp.inf)
        scores = jnp.einsum('btgn,bsgn->btsg', cc, bc)[..., None] * jnp.exp(seg)
        y_diag = jnp.einsum('btsgh,bsghp->btghp', scores, xc)
        y_off = jnp.einsum('btgn,bghpn->btghp', cc, state) * jnp.exp(acum)[..., None]
        w_end = jnp.exp(acum[:, -1:] - acum)
        new_state = (state * jnp.exp(acum[:, -1])[..., None, None]
                     + jnp.einsum('bsgn,bsghp->bghpn', bc, xc * w_end[..., None]))
        return new_state, y_diag + y_off

    state0 = jnp.zeros((b, g, hg, p, n), jnp.float32)
    _, ys = lax.scan(step, state0, (chunks(xdt), chunks(a),
                                    chunks(bm.astype(jnp.float32)), chunks(cm.astype(jnp.float32))))
    return jnp.moveaxis(ys, 0, 1).reshape(b, s, h, p)

def _mamba2_mixer(h, in_w, conv_w, conv_b, dt_bias, a_log, d_skip, norm_g, out_w):
    b, s, _ = h.shape
    zxbcdt = h @ in_w
    z = zxbcdt[..., :M_D_INNER]
    xbc = zxbcdt[..., M_D_INNER:M_D_INNER + M_CONV_DIM]
    dt = zxbcdt[..., M_D_INNER + M_CONV_DIM:]
    xbc = jax.nn.silu(_causal_dwconv(xbc, conv_w, conv_b))
    gn = M_GROUPS * M_D_STATE
    xs = xbc[..., :M_D_INNER].reshape(b, s, M_HEADS, M_HEADDIM)
    bm = xbc[..., M_D_INNER:M_D_INNER + gn].reshape(b, s, M_GROUPS, M_D_STATE)
    cm = xbc[..., M_D_INNER + gn:].reshape(b, s, M_GROUPS, M_D_STATE)
    dt = jax.nn.softplus(dt.astype(jnp.float32) + dt_bias.astype(jnp.float32))
    a_neg = -jnp.exp(a_log.astype(jnp.float32))
    y = _ssd_chunked(xs, dt, a_neg, bm, cm)
    y = y + d_skip.astype(jnp.float32)[:, None] * xs.astype(jnp.float32)
    y = y.reshape(b, s, M_D_INNER) * jax.nn.silu(z.astype(jnp.float32))
    yg = y.reshape(b, s, M_GROUPS, M_D_INNER // M_GROUPS)
    yg = yg * lax.rsqrt(jnp.mean(yg * yg, axis=-1, keepdims=True) + EPS)
    y = yg.reshape(b, s, M_D_INNER) * norm_g.astype(jnp.float32)
    return y.astype(h.dtype) @ out_w

def _stick_breaking(q, k, v):
    s_len = q.shape[1]
    scale = SB_HEAD_DIM ** -0.5
    outs = []
    for i in range(s_len // SB_BLOCK):
        lo, hi = i * SB_BLOCK, (i + 1) * SB_BLOCK
        z = jnp.einsum('bthd,bshd->bhts', q[:, lo:hi], k[:, :hi]).astype(jnp.float32) * scale
        mask = ((lo + jnp.arange(SB_BLOCK))[:, None] > jnp.arange(hi)[None, :])[None, None]
        log_keep = jnp.where(mask, jax.nn.log_sigmoid(-z), 0.0)
        after = lax.cumsum(log_keep, axis=3, reverse=True) - log_keep
        log_a = jnp.where(mask, jax.nn.log_sigmoid(z) + after, -jnp.inf)
        a = jnp.exp(log_a).astype(v.dtype)
        outs.append(jnp.einsum('bhts,bshd->bthd', a, v[:, :hi]))
    return jnp.concatenate(outs, axis=1)

def _sb_mixer(h, k, v, in_w, out_w):
    b, s, _ = h.shape
    qz = h @ in_w
    q = qz[..., :SB_WIDTH].reshape(b, s, SB_HEADS, SB_HEAD_DIM)
    z = qz[..., SB_WIDTH:]
    o = _stick_breaking(q, k, v).reshape(b, s, SB_WIDTH)
    return (o * jax.nn.silu(z)) @ out_w

def second_inputs(seed: int = 0) -> dict:
    key = jax.random.key(seed)
    ks = jax.random.split(key, 24)
    f32 = jnp.float32

    def nrm(k, shape, fan_in, mult=1.0):
        return jax.random.normal(k, shape, f32) * (mult * fan_in ** -0.5)

    def gain(k, shape):
        return 1.0 + 0.05 * jax.random.normal(k, shape, f32)

    def small(k, shape):
        return 0.01 * jax.random.normal(k, shape, f32)

    x = jax.random.normal(ks[0], (BATCH, SEQ, D_MODEL), f32)
    c = jax.random.normal(ks[1], (BATCH, D_MODEL), f32)
    ada_w = nrm(ks[2], (DEPTH_2, D_MODEL, 3 * D_MODEL), D_MODEL, 0.5)
    ada_b = small(ks[3], (DEPTH_2, 3 * D_MODEL))
    norm_g = gain(ks[4], (DEPTH_2, D_MODEL))
    m_in_w = nrm(ks[5], (N_A_LAYERS, D_MODEL, M_IN_DIM), D_MODEL)
    m_conv_w = nrm(ks[6], (N_A_LAYERS, M_D_CONV, M_CONV_DIM), M_D_CONV)
    m_conv_b = small(ks[7], (N_A_LAYERS, M_CONV_DIM))
    dt0 = jnp.exp(jax.random.uniform(ks[8], (N_A_LAYERS, M_HEADS), f32,
                                     np.log(1e-3).astype(np.float32), np.log(1e-1).astype(np.float32)))
    m_dt_bias = dt0 + jnp.log(-jnp.expm1(-dt0))
    m_a_log = jnp.log(jax.random.uniform(ks[9], (N_A_LAYERS, M_HEADS), f32, 1.0, 16.0))
    m_d = 1.0 + 0.1 * jax.random.normal(ks[10], (N_A_LAYERS, M_HEADS), f32)
    m_norm_g = gain(ks[11], (N_A_LAYERS, M_D_INNER))
    m_out_w = nrm(ks[12], (N_A_LAYERS, M_D_INNER, D_MODEL), M_D_INNER)
    kv_ada_w = nrm(ks[13], (D_MODEL, 2 * D_MODEL), D_MODEL, 0.5)
    kv_ada_b = small(ks[14], (2 * D_MODEL,))
    kv_norm_g = gain(ks[15], (D_MODEL,))
    kv_w = nrm(ks[16], (D_MODEL, 2 * SB_WIDTH), D_MODEL)
    sb_in_w = nrm(ks[17], (N_B_LAYERS, D_MODEL, 2 * SB_WIDTH), D_MODEL)
    sb_out_w = nrm(ks[18], (N_B_LAYERS, SB_WIDTH, D_MODEL), SB_WIDTH)
    final_g = gain(ks[19], (D_MODEL,))
    return {'x': x, 'c': c, 'ada_w': ada_w, 'ada_b': ada_b, 'norm_g': norm_g,
            'm_in_w': m_in_w, 'm_conv_w': m_conv_w, 'm_conv_b': m_conv_b,
            'm_dt_bias': m_dt_bias, 'm_a_log': m_a_log, 'm_d': m_d,
            'm_norm_g': m_norm_g, 'm_out_w': m_out_w,
            'kv_ada_w': kv_ada_w, 'kv_ada_b': kv_ada_b, 'kv_norm_g': kv_norm_g, 'kv_w': kv_w,
            'sb_in_w': sb_in_w, 'sb_out_w': sb_out_w, 'final_g': final_g}

def second_block(x, c, ada_w, ada_b, norm_g, m_in_w, m_conv_w, m_conv_b, m_dt_bias, m_a_log,
              m_d, m_norm_g, m_out_w, kv_ada_w, kv_ada_b, kv_norm_g, kv_w,
              sb_in_w, sb_out_w, final_g):
    b, s, _ = x.shape
    c_act = jax.nn.silu(c)

    for i in range(N_A_LAYERS):
        shift, scale, gate = jnp.split(c_act @ ada_w[i] + ada_b[i], 3, axis=-1)
        h = _modulate(x, norm_g[i], shift, scale)
        y = _mamba2_mixer(h, m_in_w[i], m_conv_w[i], m_conv_b[i], m_dt_bias[i], m_a_log[i],
                          m_d[i], m_norm_g[i], m_out_w[i])
        x = x + gate[:, None, :] * y

    kv_shift, kv_scale = jnp.split(c_act @ kv_ada_w + kv_ada_b, 2, axis=-1)
    hk = _modulate(x, kv_norm_g, kv_shift, kv_scale)
    kv = hk @ kv_w
    k = kv[..., :SB_WIDTH].reshape(b, s, SB_HEADS, SB_HEAD_DIM)
    v = kv[..., SB_WIDTH:].reshape(b, s, SB_HEADS, SB_HEAD_DIM)

    for j in range(N_B_LAYERS):
        i = N_A_LAYERS + j
        shift, scale, gate = jnp.split(c_act @ ada_w[i] + ada_b[i], 3, axis=-1)
        h = _modulate(x, norm_g[i], shift, scale)
        y = _sb_mixer(h, k, v, sb_in_w[j], sb_out_w[j])
        x = x + gate[:, None, :] * y

    return _rmsnorm(x, final_g)


def setup_inputs(seed=0):
    out = dict(first_inputs(seed))
    for name, value in second_inputs(seed + 1).items():
        if name != "x":
            out[name + "_2"] = value
    return out


def reference(
    x, c, w_in, b_f, conv_w, conv_b, conv_ln_g, conv_ln_b, w_o, w_ffn_in, w_ffn_out, mix_pre_g,
    mix_post_g, ffn_pre_g, ffn_post_g, ada_w, ada_b, c_2, ada_w_2, ada_b_2, norm_g_2, m_in_w_2,
    m_conv_w_2, m_conv_b_2, m_dt_bias_2, m_a_log_2, m_d_2, m_norm_g_2, m_out_w_2, kv_ada_w_2,
    kv_ada_b_2, kv_norm_g_2, kv_w_2, sb_in_w_2, sb_out_w_2, final_g_2,
):
    x = first_block(
        x, c, w_in, b_f, conv_w, conv_b, conv_ln_g, conv_ln_b, w_o, w_ffn_in, w_ffn_out,
        mix_pre_g, mix_post_g, ffn_pre_g, ffn_post_g, ada_w, ada_b,
    )
    return second_block(
        x, c_2, ada_w_2, ada_b_2, norm_g_2, m_in_w_2, m_conv_w_2, m_conv_b_2, m_dt_bias_2,
        m_a_log_2, m_d_2, m_norm_g_2, m_out_w_2, kv_ada_w_2, kv_ada_b_2, kv_norm_g_2, kv_w_2,
        sb_in_w_2, sb_out_w_2, final_g_2,
    )


_drawn_inputs = setup_inputs


def setup_inputs(seed=0):
    import zlib

    import numpy as np

    out = dict(_drawn_inputs(seed))
    spreads = {}
    factors = {'conv_b': 8.0,
     'conv_ln_g': 3.706,
     'conv_ln_b': 8.0,
     'mix_pre_g': 2.847,
     'mix_post_g': 3.576,
     'ffn_pre_g': 2.721,
     'ffn_post_g': 4.053,
     'ada_b': 3.491,
     'ada_b_2': 4.789,
     'norm_g_2': 2.669,
     'm_conv_b_2': 8.0,
     'm_d_2': 11.914,
     'm_norm_g_2': 4.145,
     'kv_ada_b_2': 8.0,
     'kv_norm_g_2': 8.0}
    for name, (base, spread) in spreads.items():
        noise = np.random.default_rng([zlib.crc32(name.encode()), seed]).standard_normal(out[name].shape)
        drawn = base * np.exp(spread * noise) if base else spread * noise
        out[name] = __import__('jax').numpy.asarray(drawn.astype(out[name].dtype))
    for name, factor in factors.items():
        out[name] = (out[name] * factor).astype(out[name].dtype)
    return out
```

```python
from contextlib import ExitStack

import numpy as np

import concourse.bass as bass
from concourse import mybir

F32 = mybir.dt.float32
F32R = mybir.dt.float32r
ALU = mybir.AluOpType
ACT = mybir.ActivationFunctionType
AX = mybir.AxisListType

P = 128
S = 512
TB = S // P
D = 1024
KT = D // P
EPS = 1e-6
NEG = -1.0e30

AW = D // 2
HD = 64
H1 = AW // HD
CT = AW // P
CK = 31
DFF = 2816
FT = DFF // P

MI = 2 * D
MT = MI // P
MH = MI // HD
MG = 4
MN = 128
XT = (MI + 2 * MG * MN) // P
MK = 4

H2 = D // HD

SEGS = [("conv", CT), ("q1", AW // 256), ("k1", AW // 256), ("v1", AW // 256), ("wo", KT // 2),
        ("ffn_in", FT), ("ffn_out", FT // 2), ("xbc", XT // 2), ("z", MT // 2), ("m_out", MT // 2),
        ("k2", KT // 2), ("v2", KT // 2), ("q2", KT // 2), ("z2", KT // 2), ("sb_out", KT // 2)]
FIRST = {}
NPAN = 0
for _name, _n in SEGS:
    FIRST[_name] = NPAN
    NPAN += _n
COUNT = dict(SEGS)

MOD = dict(sh1=0, sc1=8, g1=16, sh2=24, sc2=32, g2=40, msh=48, msc=56, mg=64, kvsh=72, kvsc=80, ssh=88,
           ssc=96, sg=104)
NMOD = 112
NADA = NMOD // 2
ADA_C2 = 24
ADA_FIRST = 10

VEC = {}
NVEC = 0
for _name, _n in [("c", KT), ("c2", KT), ("ada_b", NMOD), ("mix_pre", KT), ("mix_post", KT), ("ffn_pre", KT),
                  ("ffn_post", KT), ("conv_w", CT * CK), ("conv_b", CT), ("ln_g", CT), ("ln_b", CT),
                  ("norm2", 2 * KT), ("mconv_w", XT * MK), ("mconv_b", XT), ("m_norm", MT), ("m_d", MT),
                  ("kv_norm", KT), ("final", KT), ("b_f", 1), ("dt_bias", 1), ("a_log", 1)]:
    VEC[_name] = (NVEC, _n)
    NVEC += _n
CST = dict(ident=0, upper=1, neg_after=2, neg_from=3, ones=4)


def at(c, i):
    return c + 2 * i


def pairs(e, n, body):
    if n // 2 >= 2:
        with e.Fori(0, n // 2) as i:
            for u in range(2):
                body(i, u)
    else:
        for i in range(n // 2):
            for u in range(2):
                body(i, u)
    if n % 2:
        body(n // 2, 0)


def build(nc, x_in, panels, ada, vecs, cst, w_f, w_dt, out):
    ctx = ExitStack()
    with ctx:
        def sem(name):
            return ctx.enter_context(nc.semaphore(name))

        def sbuf(scope, name, shape, dt=F32):
            return scope.enter_context(nc.sbuf_tensor(name, shape, dt))

        x = sbuf(ctx, "x", [P, KT, S])
        hhi = sbuf(ctx, "hhi", [P, KT, S], F32R)
        hlo = sbuf(ctx, "hlo", [P, KT, S], F32R)
        raw = sbuf(ctx, "raw", [P, 2, 16, P])
        whi = sbuf(ctx, "whi", [P, 2, 16, P], F32R)
        wlo = sbuf(ctx, "wlo", [P, 2, 16, P], F32R)
        ada_raw = sbuf(ctx, "ada_raw", [P, 2, KT, 256])
        ada_acc = sbuf(ctx, "ada_acc", [P, 2, 256])
        vec = sbuf(ctx, "vec", [P, NVEC])
        consts = sbuf(ctx, "consts", [P, 5, P])
        mod = sbuf(ctx, "mod", [P, NMOD])
        cs = sbuf(ctx, "cs", [P, 2, KT])
        coef = sbuf(ctx, "coef", [P, 3, KT])
        eps = sbuf(ctx, "eps", [P, 1])
        ps = ctx.enter_context(nc.psum_tensor("ps", [P, 8, S], F32))
        MODB = 4
        ident = consts[:, CST["ident"], :]
        ones = consts[:, CST["ones"], :]

        def v(name, i=None, n=None):
            a, w = VEC[name]
            if i is None:
                return vec[:, a:a + w]
            return vec[:, a + i:a + i + (n or 1)]

        def m(name, n=KT):
            return mod[:, MOD[name]:MOD[name] + n]

        w_landed = [sem("w_landed0"), sem("w_landed1")]
        hi_split = sem("hi_split")
        lo_split = sem("lo_split")
        panels_used = sem("panels_used")
        pair_free = [sem("pair_free0"), sem("pair_free1")]
        ada_landed = [sem("ada_landed0"), sem("ada_landed1")]
        ada_mul = sem("ada_mul")
        acc_ready = sem("acc_ready")
        mod_done = sem("mod_done")
        ada_chain = sem("ada_chain")
        sg_ready = sem("sg_ready")
        small_landed = sem("small_landed")
        setup = sem("setup")
        ws_ready = sem("ws_ready")
        small_done = sem("small_done")
        mod_read = sem("mod_read")

        def load_panel(e, c, i):
            if c + (0 if isinstance(i, int) else 0) >= 2 or not isinstance(i, int):
                e.wait_ge(lo_split, at(c - 1, i))
            e.dma_start(raw[:, c % 2, :, :].rearrange("p t n -> p (t n)"),
                        panels[at(c, i)]).then_inc(w_landed[c % 2], 16)

        def load_ada(e, c, i):
            if c >= 2:
                e.wait_ge(acc_ready, at(c - 1, i))
            e.dma_start(ada_raw[:, c % 2, :, :].rearrange("p k n -> p (k n)"),
                        ada[at(c, i)]).then_inc(ada_landed[c % 2], 16)

        def split_hi(e, c, i):
            e.wait_ge(w_landed[c % 2], (c // 2 + i + 1) * 16)
            if c >= 2 or not isinstance(i, int):
                e.wait_ge(panels_used, at(c - 1, i))
            e.activation(whi[:, c % 2, :, :], raw[:, c % 2, :, :], ACT.Copy).then_inc(hi_split, 1)

        def split_lo(e, c, i):
            e.wait_ge(hi_split, at(c + 1, i))
            e.tensor_tensor(wlo[:, c % 2, :, :], raw[:, c % 2, :, :], whi[:, c % 2, :, :].bitcast(F32),
                            ALU.subtract).then_inc(lo_split, 1)

        def ada_multiply(e, c, i):
            e.wait_ge(ada_landed[c % 2], (c // 2 + i + 1) * 16)
            which = 0 if c < ADA_C2 else 1
            e.tensor_tensor(ada_raw[:, c % 2, :, :], ada_raw[:, c % 2, :, :],
                            cs[:, which, :].unsqueeze(2).to_broadcast([P, KT, 256]),
                            ALU.mult).then_inc(ada_mul, 1)

        def ada_sum(e, c, i):
            e.wait_ge(ada_mul, at(c + 1 - ADA_FIRST, i))
            e.wait_ge(mod_done, at(c - 1, i))
            e.tensor_reduce(ada_acc[:, c % 2, :], ada_raw[:, c % 2, :, :].rearrange("p k n -> p n k"),
                            AX.X, ALU.add).then_inc(acc_ready, 1)

        def ada_columns(e, c, i):
            e.wait_ge(acc_ready, at(c + 1, i))
            for b in range(2):
                col = c * 2 + i * 4 + b
                mm = e.matmul(ps[:, MODB, col:col + 1] if isinstance(i, int) else ps[:, MODB, bass.ds(col, 1)],
                              ada_acc[:, c % 2, b * P:(b + 1) * P], ones[:, 0:1], start=True, stop=True)
            mm.then_inc(mod_done, 1)

        def read_mod(e, a0, a1):
            e.wait_ge(mod_done, a1)
            lo, hi = 2 * a0, 2 * a1
            e.tensor_tensor(mod[:, lo:hi], ps[:, MODB, lo:hi], v("ada_b")[:, lo:hi], ALU.add).then_inc(mod_read, 1)

        PASSES = ((whi, 0), (whi, 1), (wlo, 0))

        def in_panel(e, c, qc, i, src, by_token):
            e.wait_ge(lo_split, at(c + 1, i))
            e.wait_ge(pair_free[qc % 2], qc // 2 + 1 + i)
            for b in range(TB if by_token else 2):
                for k in range(KT):
                    for n, (w, part) in enumerate(PASSES):
                        flags = dict(start=(k == 0 and n == 0), stop=(k == KT - 1 and n == 2))
                        if by_token:
                            o = ps[:, 2 * (qc % 2) + b // 2, (b % 2) * 256:(b % 2) * 256 + 256]
                            mm = e.matmul(o, src[part][:, k, b * P:(b + 1) * P],
                                          w[:, c % 2, 2 * k:2 * k + 2, :], **flags)
                        else:
                            mm = e.matmul(ps[:, 2 * (qc % 2) + b, :], w[:, c % 2, 2 * k + b, :],
                                          src[part][:, k, :], **flags)
            mm.then_inc(panels_used, 1)

        def out_projection(e, name, parts):
            c0, n = FIRST[name], COUNT[name]
            per = n // len(parts)

            def panel(c, i, src, k0, first, last):
                e.wait_ge(lo_split, at(c + 1, i))
                for k2 in range(2):
                    for b in range(8):
                        for j, (w, part) in enumerate(PASSES):
                            rhs = (src[part][:, k0 + k2, :] if isinstance(i, int) else
                                   src[part][:, bass.ds(k0 + k2 + i * 4, 1), :])
                            mm = e.matmul(ps[:, b, :], w[:, c % 2, k2 * 8 + b, :], rhs,
                                          start=(first and k2 == 0 and j == 0),
                                          stop=(last and k2 == 1 and j == 2), skip_group_check=True)
                mm.then_inc(panels_used, 1)

            for s, src in enumerate(parts):
                lo = 1 if s == 0 else 0
                hi = per - 1 if s == len(parts) - 1 else per
                base = c0 + s * per
                if s == 0:
                    panel(base, 0, src, 0, True, False)
                mid = hi - lo
                if mid >= 4:
                    with e.Fori(0, mid // 2) as i:
                        for u in range(2):
                            panel(base + lo + u, i, src, 2 * (lo + u), False, False)
                    rest = range(lo + mid // 2 * 2, hi)
                else:
                    rest = range(lo, hi)
                for k in rest:
                    panel(base + k, 0, src, 2 * k, False, False)
                if s == len(parts) - 1:
                    panel(base + per - 1, 0, src, 2 * (per - 1), False, True)

        def stream(e, name, *, load=False, hi=False, lo=False):
            c0, n = FIRST[name], COUNT[name]

            def step(i, u):
                if load:
                    load_panel(e, c0 + u + 2, i)
                if hi:
                    split_hi(e, c0 + u + 1, i)
                if lo:
                    split_lo(e, c0 + u + 1, i)
            ahead = 2 if load else 1
            whole = min(n, NPAN - ahead - c0)
            if whole == n:
                pairs(e, n, step)
            else:
                for k in range(whole):
                    step(k // 2, k % 2)

        def out_block(name, parts):
            with nc.Block() as block:
                @block.sync
                def _(sp):
                    stream(sp, name, load=True)

                @block.scalar
                def _(act):
                    stream(act, name, hi=True)

                @block.vector
                def _(dve):
                    stream(dve, name, lo=True)

                @block.tensor
                def _(pe):
                    out_projection(pe, name, parts)

        nsem = {k: sem(k) for k in ("y_ready", "ysq_ready", "ss_used", "std_ready", "rs_ready", "scaled",
                                    "x_new0", "x_new1", "sq_ready", "h0_ready", "hi_ready", "lo_ready", "coef_ready",
                                    "out_ready", "out_stored")}
        done = {k: 0 for k in nsem}

        def boundary(post, gate, targets, final=False, mods=None, room=None):
            base = dict(done)
            N = nsem
            rows = 8
            with ExitStack() as tmp:
                y = sbuf(tmp, f"y{base['coef_ready']}_{base['sq_ready']}", [P, KT, S]) if post not in (None, "none") or final else None
                if room is None:
                    room = sbuf(tmp, f"room{base['coef_ready']}_{base['sq_ready']}", [P, 6, S])
                sq, h0 = room[:, 0:2, :], room[:, 2:4, :]
                std, rs = room[:, 4, :], room[:, 5, :]
                normed = post not in (None, "none")
                fresh = post != "none"
                nt = len(targets)
                ss0 = base["ss_used"]
                ss1 = ss0 + (rows if normed else 0)
                st0 = base["std_ready"]
                with nc.Block() as block:
                    @block.scalar
                    def _(act):
                        if normed:
                            for k in range(KT):
                                act.activation(y[:, k, :], ps[:, k, :], ACT.Copy).then_inc(N["y_ready"], 1)
                            act.wait_ge(N["ss_used"], ss0 + rows)
                            act.activation(std, ps[:, 0, :], ACT.Sqrt, bias=eps[:, 0:1],
                                           scale=1.0 / D).then_inc(N["std_ready"], 1)
                        for k in range(KT):
                            if fresh:
                                act.wait_ge(N[f"x_new{k % 2}"], base[f"x_new{k % 2}"] + k // 2 + 1)
                            if k >= 2:
                                act.wait_ge(N["ss_used"], ss1 + k - 1)
                            elif normed:
                                act.wait_ge(N["ss_used"], ss1)
                            act.activation(sq[:, k % 2, :], x[:, k, :], ACT.Square).then_inc(N["sq_ready"], 1)
                        act.wait_ge(N["ss_used"], ss1 + rows)
                        if normed:
                            act.wait_ge(N["rs_ready"], base["rs_ready"] + 1)
                        act.activation(std, ps[:, int(normed), :], ACT.Sqrt, bias=eps[:, 0:1],
                                       scale=1.0 / D).then_inc(N["std_ready"], 1)
                        for t in range(nt):
                            gain, sc, sh, thi, tlo = targets[t]
                            for k in range(KT):
                                act.wait_ge(N["h0_ready"], base["h0_ready"] + t * KT + k + 1)
                                act.activation(thi[:, k, :], h0[:, k % 2, :], ACT.Identity,
                                               bias=m(sh)[:, k:k + 1]).then_inc(N["hi_ready"], 1)

                    @block.tensor
                    def _(pe):
                        if normed:
                            for k in range(KT):
                                pe.wait_ge(N["ysq_ready"], base["ysq_ready"] + k + 1)
                                pe.matmul(ps[:, 0, :], ones, sq[:, k % 2, :], start=k == 0,
                                          stop=k == KT - 1).then_inc(N["ss_used"], 1)
                        for k in range(KT):
                            pe.wait_ge(N["sq_ready"], base["sq_ready"] + k + 1)
                            pe.matmul(ps[:, int(normed), :], ones, sq[:, k % 2, :], start=k == 0,
                                      stop=k == KT - 1).then_inc(N["ss_used"], 1)

                    @block.vector
                    def _(dve):
                        if mods:
                            read_mod(dve, *mods)
                            dve.wait_ge(mod_read, read_counts[mods])
                        if normed:
                            dve.tensor_tensor(coef[:, 0, :], v(post), m(gate), ALU.mult).then_inc(N["coef_ready"], 1)
                            for k in range(KT):
                                dve.wait_ge(N["y_ready"], base["y_ready"] + k + 1)
                                if k >= 2:
                                    dve.wait_ge(N["ss_used"], ss0 + k - 1)
                                dve.tensor_tensor(sq[:, k % 2, :], y[:, k, :], y[:, k, :],
                                                  ALU.mult).then_inc(N["ysq_ready"], 1)
                            dve.wait_ge(N["std_ready"], st0 + 1)
                            dve.reciprocal(rs, std).then_inc(N["rs_ready"], 1)
                            dve.wait_ge(N["rs_ready"], base["rs_ready"] + 1)
                            dve.wait_ge(N["coef_ready"], base["coef_ready"] + 1)
                            for k in range(KT):
                                dve.scalar_tensor_tensor(out=y[:, k, :], in0=y[:, k, :], scalar=coef[:, 0, k:k + 1],
                                                         in1=rs, op0=ALU.mult,
                                                         op1=ALU.mult).then_inc(N["scaled"], 1)
                                if k % 2:
                                    dve.wait_ge(N["scaled"], base["scaled"] + k + 1)
                                    dve.tensor_tensor(x[:, k, :], x[:, k, :], y[:, k, :],
                                                      ALU.add).then_inc(N["x_new1"], 1)
                        elif fresh:
                            for k in range(KT):
                                dve.scalar_tensor_tensor(out=x[:, k, :], in0=ps[:, k, :], scalar=m(gate)[:, k:k + 1],
                                                         in1=x[:, k, :], op0=ALU.mult,
                                                         op1=ALU.add).then_inc(N[f"x_new{k % 2}"], 1)
                        if fresh:
                            for r in range(2):
                                dve.wait_ge(N[f"x_new{r}"], base[f"x_new{r}"] + KT // 2)
                        dve.wait_ge(N["std_ready"], st0 + (2 if normed else 1))
                        if normed:
                            dve.wait_ge(N["scaled"], base["scaled"] + KT)
                        dve.reciprocal(rs, std).then_inc(N["rs_ready"], 1)
                        dve.wait_ge(N["rs_ready"], base["rs_ready"] + (2 if normed else 1))
                        if final:
                            for k in range(KT):
                                dve.scalar_tensor_tensor(out=y[:, k, :], in0=x[:, k, :], scalar=v("final", k),
                                                         in1=rs, op0=ALU.mult,
                                                         op1=ALU.mult).then_inc(N["out_ready"], 1)
                        for t in range(nt):
                            gain, sc, sh, thi, tlo = targets[t]
                            dve.scalar_tensor_tensor(out=coef[:, 1 + t, :], in0=m(sc), scalar=1.0, in1=gain,
                                                     op0=ALU.add, op1=ALU.mult).then_inc(N["coef_ready"], 1)
                            dve.wait_ge(N["coef_ready"], base["coef_ready"] + (1 if normed else 0) + t + 1)

                            def lo(k):
                                n = t * KT + k
                                dve.wait_ge(N["hi_ready"], base["hi_ready"] + n + 1)
                                dve.scalar_tensor_tensor(out=tlo[:, k, :], in0=h0[:, k % 2, :],
                                                         scalar=m(sh)[:, k:k + 1], in1=thi[:, k, :].bitcast(F32),
                                                         op0=ALU.add, op1=ALU.subtract).then_inc(N["lo_ready"], 1)
                            for k in range(KT):
                                n = t * KT + k
                                if n >= 2:
                                    dve.wait_ge(N["lo_ready"], base["lo_ready"] + n - 1)
                                dve.scalar_tensor_tensor(out=h0[:, k % 2, :], in0=x[:, k, :],
                                                         scalar=coef[:, 1 + t, k:k + 1], in1=rs,
                                                         op0=ALU.mult, op1=ALU.mult).then_inc(N["h0_ready"], 1)
                                if k:
                                    lo(k - 1)
                            lo(KT - 1)

                    if normed:
                        @block.gpsimd
                        def _(pool):
                            for k in range(0, KT, 2):
                                pool.wait_ge(N["scaled"], base["scaled"] + k + 1)
                                pool.tensor_tensor(x[:, k, :], x[:, k, :], y[:, k, :],
                                                   ALU.add).then_inc(N["x_new0"], 1)

                    if final:
                        @block.sync
                        def _(sp):
                            for k in range(KT):
                                sp.wait_ge(N["out_ready"], base["out_ready"] + k + 1)
                                sp.dma_start(out[k], y[:, k, :]).then_inc(N["out_stored"], 16)
                            sp.wait_ge(N["out_stored"], 16 * KT)

            done["y_ready"] += KT * normed
            done["ysq_ready"] += KT * normed
            done["ss_used"] = ss1 + rows
            done["std_ready"] += 1 + normed
            done["rs_ready"] += 1 + normed
            done["scaled"] += KT * normed
            done["x_new0"] += KT // 2 * fresh
            done["x_new1"] += KT // 2 * fresh
            done["sq_ready"] += KT
            done["h0_ready"] += KT * nt
            done["hi_ready"] += KT * nt
            done["lo_ready"] += KT * nt
            done["coef_ready"] += nt + normed

        read_counts = {(0, ADA_FIRST): 1, (10, 20): 2, (20, 42): 3, (42, 54): 4, (54, 56): 5}

        def split_small(dve, whi_s, wlo_s, raw_s, n, base):
            for w in (whi_s, wlo_s):
                dve.memset(w[:].bitcast(F32), 0.0).then_inc(ws_ready, 1)
            dve.wait_ge(ws_ready, base + 2)
            dve.tensor_copy(whi_s[:, :, 0:n], raw_s[:, :, 0:n]).then_inc(ws_ready, 1)
            dve.wait_ge(ws_ready, base + 3)
            dve.tensor_tensor(wlo_s[:, :, 0:n], raw_s[:, :, 0:n], whi_s[:, :, 0:n].bitcast(F32),
                              ALU.subtract).then_inc(ws_ready, 1)

        def small_projection(pe, whi_s, wlo_s, ready):
            pe.wait_ge(ws_ready, ready)
            for k in range(KT):
                for n, (w, part) in enumerate(((whi_s, hhi), (whi_s, hlo), (wlo_s, hhi))):
                    mm = pe.matmul(ps[:, 5, :], w[:, k, :], part[:, k, :], start=(k == 0 and n == 0),
                                   stop=(k == KT - 1 and n == 2))
            mm.then_inc(small_done, 1)

        sp_step = sem("sp_step")
        sp_exp = sem("sp_exp")

        def log1p_exp(dve, t, rows, bias, base, ready):
            r = slice(0, rows)
            n = [base]

            def then(ins):
                n[0] += 1
                ins.then_inc(sp_step, 1)
                dve.wait_ge(sp_step, n[0])
            dve.wait_ge(small_done, ready)
            then(dve.tensor_scalar(t[r, 0, :], ps[r, 5, :], bias, None, ALU.add))
            then(dve.tensor_scalar(t[r, 1, :], t[r, 0, :], -1.0, None, ALU.mult))
            then(dve.tensor_tensor(t[r, 2, :], t[r, 0, :], t[r, 1, :], ALU.min))
            dve.wait_ge(sp_exp, ready)
            then(dve.tensor_scalar(t[r, 2, :], t[r, 1, :], 2.0, None, ALU.add))
            then(dve.reciprocal(t[r, 3, :], t[r, 2, :]))
            then(dve.tensor_tensor(t[r, 1, :], t[r, 1, :], t[r, 3, :], ALU.mult))
            then(dve.tensor_tensor(t[r, 2, :], t[r, 1, :], t[r, 1, :], ALU.mult))
            then(dve.tensor_scalar(t[r, 3, :], t[r, 2, :], 1.0 / 17, None, ALU.mult))
            for k in range(7, 0, -1):
                then(dve.scalar_tensor_tensor(out=t[r, 3, :], in0=t[r, 3, :], scalar=1.0 / (2 * k + 1),
                                              in1=t[r, 2, :], op0=ALU.add, op1=ALU.mult))
            then(dve.scalar_tensor_tensor(out=t[r, 3, :], in0=t[r, 3, :], scalar=1.0, in1=t[r, 1, :],
                                          op0=ALU.add, op1=ALU.mult))
            then(dve.tensor_scalar(t[r, 1, :], t[r, 3, :], 2.0, None, ALU.mult))
            return n[0], then

        def small_exp(act, t, rows, step, use):
            act.wait_ge(sp_step, step)
            act.activation(t[0:rows, 1, :], t[0:rows, 2, :], ACT.Exp).then_inc(sp_exp, 1)

        with nc.Block() as block:
            @block.sync
            def _(sp):
                sp.dma_start(vec[:], vecs).then_inc(setup, 16)
                sp.dma_start(consts[:].rearrange("p a b -> p (a b)"), cst).then_inc(setup, 16)
                for c in range(2):
                    load_ada(sp, c, 0)
                sp.dma_start(x[:], x_in).then_inc(small_landed, 16)
                for c in range(2):
                    load_panel(sp, c, 0)
                for c in range(2, ADA_FIRST + 2):
                    load_ada(sp, c, 0)

            @block.scalar
            def _(act):
                act.wait_ge(setup, 32)
                act.activation(cs[:].rearrange("p a b -> p (a b)"), vec[:, 0:2 * KT], ACT.Silu).then_inc(ada_chain, 1)
                split_hi(act, 0, 0)

            @block.vector
            def _(dve):
                dve.memset(eps[:], EPS).then_inc(pair_free[0], 1)
                dve.memset(coef[:], 0.0).then_inc(pair_free[1], 1)
                dve.wait_ge(ada_chain, 1)
                n = 1
                for c in range(ADA_FIRST):
                    dve.wait_ge(ada_landed[c % 2], 16 * (c // 2 + 1))
                    if c >= 2:
                        dve.wait_ge(mod_done, c - 1)
                    for k in range(KT):
                        if k == 0:
                            ins = dve.tensor_scalar(ada_acc[:, c % 2, :], ada_raw[:, c % 2, k, :], cs[:, 0, k:k + 1],
                                                    None, ALU.mult)
                        else:
                            dve.wait_ge(ada_chain, n)
                            ins = dve.scalar_tensor_tensor(out=ada_acc[:, c % 2, :], in0=ada_raw[:, c % 2, k, :],
                                                           scalar=cs[:, 0, k:k + 1], in1=ada_acc[:, c % 2, :],
                                                           op0=ALU.mult, op1=ALU.add)
                        if k < KT - 1:
                            ins.then_inc(ada_chain, 1)
                            n += 1
                        else:
                            ins.then_inc(acc_ready, 1)
                split_lo(dve, 0, 0)
                dve.wait_ge(small_landed, 16)

            @block.tensor
            def _(pe):
                pe.wait_ge(setup, 32)
                for c in range(ADA_FIRST):
                    ada_columns(pe, c, 0)

        boundary("none", None, [(v("mix_pre"), "sc1", "sh1", hhi, hlo)], mods=(0, ADA_FIRST))

        with ExitStack() as seg:
            qk = sbuf(seg, "qk", [P, 2 * CT, S])
            vt = sbuf(seg, "vt", [P, TB, AW])
            u = sbuf(seg, "u", [P, CT, CK - 1 + S])
            cv = sbuf(seg, "cv", [P, CT, S])
            ncum = sbuf(seg, "ncum", [H1, S])
            sg = sbuf(seg, "sg", [P, 2, S])
            conv_step = sem("conv_step")
            lf_ready = sem("lf_ready")
            pad_ready = sem("pad_ready")

            def conv_taps(dve, n0, n1):
                for n in range(n0, n1):
                    j, tap = n % CT, n // CT
                    w = v("conv_w", j * CK + tap)
                    src = u[:, j, tap:tap + S]
                    if tap == 0:
                        dve.tensor_scalar(cv[:, j, :], src, w, v("conv_b", j), ALU.mult,
                                          ALU.add).then_inc(conv_step, 1)
                    else:
                        dve.wait_ge(conv_step, n - CT + 1)
                        dve.scalar_tensor_tensor(out=cv[:, j, :], in0=src, scalar=w, in1=cv[:, j, :],
                                                 op0=ALU.mult, op1=ALU.add).then_inc(conv_step, 1)
            TAPS_EARLY = 54

            with ExitStack() as tmp:
                wf_raw = sbuf(tmp, "wf_raw", [P, KT, H1])
                wf_hi = sbuf(tmp, "wf_hi", [P, KT, P], F32R)
                wf_lo = sbuf(tmp, "wf_lo", [P, KT, P], F32R)
                ft = sbuf(tmp, "ft", [H1, 4, S])
                one_row = sbuf(tmp, "one_row", [H1, S])
                c0, q0, a0 = 0, 0, ADA_FIRST
                segs = [("conv", 4), ("q1", 2), ("k1", 2), ("v1", 2)]
                with nc.Block() as block:
                    @block.sync
                    def _(sp):
                        sp.dma_start(wf_raw[:].rearrange("p k n -> p (k n)"), w_f).then_inc(small_landed, 16)

                        def step(i, r):
                            load_panel(sp, c0 + r + 2, i)
                            load_ada(sp, a0 + r + 2, i)
                        pairs(sp, 10, step)

                    @block.gpsimd
                    def _(pool):
                        pairs(pool, 10, lambda i, r: ada_multiply(pool, a0 + r, i))

                    @block.scalar
                    def _(act):
                        at0 = 0
                        for name, n in segs:
                            def step(i, r, name=name, at0=at0):
                                c = at0 + r
                                pair = c % 2
                                split_hi(act, c + 1, i)
                                act.wait_ge(panels_used, at(c + 1, i))
                                bank = ps[:, 2 * pair:2 * pair + 2, :]
                                if name == "conv":
                                    act.activation(sg[:, pair, :], ps[:, 2 * pair + 1, :],
                                                   ACT.Sigmoid).then_inc(sg_ready, 1)
                                elif name == "v1":
                                    act.activation(vt[:, :, r * 256:(r + 1) * 256],
                                                   bank.rearrange("p a (b c) -> p (a b) c", b=2),
                                                   ACT.Copy).then_inc(pair_free[pair], 1)
                                else:
                                    t = 2 * r + (CT if name == "k1" else 0)
                                    act.activation(qk[:, t:t + 2, :], bank, ACT.Copy,
                                                   scale=HD ** -0.5 if name == "q1" else 1.0
                                                   ).then_inc(pair_free[pair], 1)
                            pairs(act, n, step)
                            at0 += n
                            if name == "conv":
                                small_exp(act, ft, H1, 3, 1)

                    @block.vector
                    def _(dve):
                        dve.memset(u[:, :, 0:CK - 1], 0.0).then_inc(pad_ready, 1)
                        dve.memset(one_row[:], 1.0).then_inc(pad_ready, 1)
                        dve.wait_ge(small_landed, 32)
                        split_small(dve, wf_hi, wf_lo, wf_raw, H1, 0)

                        def conv(i, r):
                            c = r
                            split_lo(dve, c + 1, i)
                            dve.wait_ge(sg_ready, at(c + 1, i))
                            j = r + i * 2
                            dst = u[:, j, CK - 1:] if isinstance(i, int) else u[:, bass.ds(j, 1), CK - 1:]
                            dve.tensor_tensor(dst, ps[:, 2 * r, :], sg[:, r, :], ALU.mult).then_inc(pair_free[r], 1)
                            ada_sum(dve, a0 + c, i)
                        pairs(dve, 4, conv)
                        last, then = log1p_exp(dve, ft, H1, v("b_f")[0:H1, :], 0, 1)
                        dve.tensor_scalar(ft[:, 2, :], ft[:, 0, :], 0.0, -1.0, ALU.min,
                                          ALU.mult).then_inc(lf_ready, 1)
                        dve.wait_ge(lf_ready, 1)
                        dve.tensor_tensor(ft[:, 3, :], ft[:, 2, :], ft[:, 1, :], ALU.add).then_inc(lf_ready, 1)
                        dve.wait_ge(lf_ready, 2)
                        dve.tensor_tensor_scan(ncum[:], one_row[:], ft[:, 3, :], 0.0, ALU.mult,
                                               ALU.add).then_inc(lf_ready, 1)
                        dve.wait_ge(pair_free[0], 3)
                        dve.wait_ge(pair_free[1], 3)
                        for k in range(4, 10):
                            split_lo(dve, k + 1, 0)
                            conv_taps(dve, (k - 4) * TAPS_EARLY // 6, (k - 3) * TAPS_EARLY // 6)
                            ada_sum(dve, a0 + k, 0)

                    @block.tensor
                    def _(pe):
                        def step(i, r):
                            in_panel(pe, r, r, i, (hhi, hlo), False)
                            ada_columns(pe, a0 + r, i)
                        pairs(pe, 4, step)
                        small_projection(pe, wf_hi, wf_lo, 4)
                        pairs(pe, 4, lambda i, r: (in_panel(pe, 4 + r, 4 + r, i, (hhi, hlo), False),
                                                   ada_columns(pe, a0 + 4 + r, i)))
                        for r in range(2):
                            in_panel(pe, 8 + r, 8 + r, 0, (hhi, hlo), True)
                            ada_columns(pe, a0 + 8 + r, 0)

            NU = TB * H1
            with ExitStack() as tmp:
                pm = sbuf(tmp, "pm", [P, 2, S])
                pt = sbuf(tmp, "pt", [P, 2, S])
                mx = sbuf(tmp, "mx", [P, NU])
                nmx = sbuf(tmp, "nmx", [P, NU])
                rsum = sbuf(tmp, "rsum", [P, NU])
                rinv = sbuf(tmp, "rinv", [P, NU])
                o1 = sbuf(tmp, "o1", [P, 2, AW])
                lsq = sbuf(tmp, "lsq", [P, CT, S])
                lstd = sbuf(tmp, "lstd", [P, S])
                lrs = sbuf(tmp, "lrs", [P, S])
                A = {k: sem("a1_" + k) for k in ("s_done", "max", "nmax", "exp", "t_done", "pt_ready", "pv_done",
                                                 "rinv", "o_ready", "ot_done", "ohi", "olo", "mean", "centred",
                                                 "sq", "var", "std", "rstd", "scaled", "silu", "chi", "clo")}
                units = [(qb, h) for qb in range(TB) for h in range(H1)]
                with nc.Block() as block:
                    @block.tensor
                    def _(pe):
                        def logits(n):
                            qb, h = units[n]
                            nk = (qb + 1) * P
                            r0 = HD * (h % 2)
                            if n >= 2:
                                pe.wait_ge(A["exp"], n - 1)
                            o = ps[:, n % 2, 0:nk]
                            pe.matmul(o, qk[r0:r0 + HD, h // 2, qb * P:(qb + 1) * P],
                                      qk[r0:r0 + HD, CT + h // 2, 0:nk], start=True, stop=False)
                            pe.matmul(o, ident[0:H1, h:h + 1].to_broadcast([H1, P]), ncum[:, 0:nk],
                                      start=False, stop=False)
                            pe.matmul(ps[:, n % 2, qb * P:nk], ident, consts[:, CST["neg_after"], :],
                                      start=False, stop=True).then_inc(A["s_done"], 1)

                        def turn(n):
                            qb, h = units[n]
                            pe.wait_ge(A["exp"], n + 1)
                            if n >= 2:
                                pe.wait_ge(A["pt_ready"], n - 1)
                            for kb in range(qb + 1):
                                mm = pe.transpose(ps[:, 2 + n % 2, kb * P:(kb + 1) * P],
                                                  pm[:, n % 2, kb * P:(kb + 1) * P], ident)
                            mm.then_inc(A["t_done"], 1)

                        def values(n):
                            qb, h = units[n]
                            pe.wait_ge(A["pt_ready"], n + 1)
                            if h == 0 and qb >= 2:
                                pe.wait_ge(A["o_ready"], qb - 1)
                            for kb in range(qb + 1):
                                mm = pe.matmul(ps[:, 6 + qb % 2, h * HD:(h + 1) * HD],
                                               pt[:, n % 2, kb * P:(kb + 1) * P],
                                               vt[:, kb, h * HD:(h + 1) * HD], start=kb == 0, stop=kb == qb)
                            mm.then_inc(A["pv_done"], 1)

                        def turn_out(qb):
                            pe.wait_ge(A["o_ready"], qb + 1)
                            if qb:
                                pe.wait_ge(A["olo"], qb)
                            for t in range(CT):
                                mm = pe.transpose(ps[:, 5, t * P:(t + 1) * P], o1[:, qb % 2, t * P:(t + 1) * P],
                                                  ident)
                            mm.then_inc(A["ot_done"], 1)

                        for n in range(NU + 4):
                            if n < NU:
                                logits(n)
                            if 1 <= n <= NU:
                                turn(n - 1)
                            if 2 <= n <= NU + 1:
                                values(n - 2)
                            if n >= H1 + 3 and (n - 3) % H1 == 0:
                                turn_out((n - 3) // H1 - 1)
                        for j in range(CT):
                            pe.wait_ge(conv_step, CK * CT - CT + j + 1)
                            mm = pe.matmul(ps[:, 4, :], ones, cv[:, j, :], start=j == 0, stop=j == CT - 1)
                        mm.then_inc(A["mean"], 1)
                        for j in range(CT):
                            pe.wait_ge(A["sq"], j + 1)
                            mm = pe.matmul(ps[:, 0, :], ones, lsq[:, j, :], start=j == 0, stop=j == CT - 1)
                        mm.then_inc(A["var"], 1)

                    @block.scalar
                    def _(act):
                        def out_hi(qb):
                            act.wait_ge(A["ot_done"], qb + 1)
                            act.activation(hhi[:, 0:CT, qb * P:(qb + 1) * P],
                                           ps[:, 5, :].rearrange("p (t q) -> p t q", t=CT),
                                           ACT.Copy).then_inc(A["ohi"], 1)
                        for n, (qb, h) in enumerate(units):
                            nk = (qb + 1) * P
                            act.wait_ge(A["nmax"], n + 1)
                            if n >= 2:
                                act.wait_ge(A["t_done"], n - 1)
                            act.activation(pm[:, n % 2, 0:nk], ps[:, n % 2, 0:nk], ACT.Exp, bias=nmx[:, n:n + 1],
                                           accum_out=rsum[:, n:n + 1]).then_inc(A["exp"], 1)
                            if n >= H1 + 3 and (n - 3) % H1 == 0:
                                out_hi((n - 3) // H1 - 1)
                        out_hi(TB - 1)
                        for j in range(CT):
                            act.wait_ge(A["centred"], j + 1)
                            act.activation(lsq[:, j, :], cv[:, j, :], ACT.Square).then_inc(A["sq"], 1)
                        act.wait_ge(A["var"], 1)
                        act.activation(lstd[:], ps[:, 0, :], ACT.Sqrt, bias=eps[:, 0:1],
                                       scale=1.0 / AW).then_inc(A["std"], 1)
                        for j in range(CT):
                            act.wait_ge(A["scaled"], j + 1)
                            act.activation(lsq[:, j, :], cv[:, j, :], ACT.Silu,
                                           bias=v("ln_b", j)).then_inc(A["silu"], 1)

                    @block.vector
                    def _(dve):
                        read_mod(dve, 10, 20)

                        def neg_max(n):
                            qb, h = units[n]
                            dve.wait_ge(A["s_done"], n + 1)
                            dve.tensor_reduce(mx[:, n:n + 1], ps[:, n % 2, 0:(qb + 1) * P], AX.X,
                                              ALU.max).then_inc(A["max"], 1)
                            dve.wait_ge(A["max"], n + 1)
                            dve.tensor_scalar(nmx[:, n:n + 1], mx[:, n:n + 1], -1.0, None,
                                              ALU.mult).then_inc(A["nmax"], 1)

                        def take_pt(n):
                            qb, h = units[n]
                            dve.wait_ge(A["t_done"], n + 1)
                            if n >= 2:
                                dve.wait_ge(A["pv_done"], n - 1)
                            dve.tensor_copy(pt[:, n % 2, 0:(qb + 1) * P],
                                            ps[:, 2 + n % 2, 0:(qb + 1) * P]).then_inc(A["pt_ready"], 1)

                        def normalise(qb):
                            dve.wait_ge(A["pv_done"], H1 * (qb + 1))
                            cols = slice(H1 * qb, H1 * (qb + 1))
                            dve.reciprocal(rinv[:, cols], rsum[:, cols]).then_inc(A["rinv"], 1)
                            dve.wait_ge(A["rinv"], qb + 1)
                            if qb >= 2:
                                dve.wait_ge(A["ot_done"], qb - 1)
                            dve.tensor_tensor(o1[:, qb % 2, :].rearrange("p (h d) -> p h d", h=H1),
                                              ps[:, 6 + qb % 2, :].rearrange("p (h d) -> p h d", h=H1),
                                              rinv[:, cols].unsqueeze(2).to_broadcast([P, H1, HD]),
                                              ALU.mult).then_inc(A["o_ready"], 1)

                        def out_lo(qb):
                            dve.wait_ge(A["ohi"], qb + 1)
                            dve.tensor_tensor(hlo[:, 0:CT, qb * P:(qb + 1) * P],
                                              ps[:, 5, :].rearrange("p (t q) -> p t q", t=CT),
                                              hhi[:, 0:CT, qb * P:(qb + 1) * P].bitcast(F32),
                                              ALU.subtract).then_inc(A["olo"], 1)
                        taps = CK * CT - TAPS_EARLY
                        for n in range(NU + 4):
                            if n < NU:
                                neg_max(n)
                            if 1 <= n <= NU:
                                take_pt(n - 1)
                            if n >= H1 + 2 and (n - 2) % H1 == 0:
                                normalise((n - 2) // H1 - 1)
                            if n >= H1 + 4 and (n - 4) % H1 == 0:
                                out_lo((n - 4) // H1 - 1)
                            if n < NU:
                                conv_taps(dve, TAPS_EARLY + taps * n // NU, TAPS_EARLY + taps * (n + 1) // NU)
                        out_lo(TB - 1)
                        dve.wait_ge(A["mean"], 1)
                        for j in range(CT):
                            dve.scalar_tensor_tensor(out=cv[:, j, :], in0=ps[:, 4, :], scalar=-1.0 / AW,
                                                     in1=cv[:, j, :], op0=ALU.mult,
                                                     op1=ALU.add).then_inc(A["centred"], 1)
                        dve.wait_ge(A["std"], 1)
                        dve.reciprocal(lrs[:], lstd[:]).then_inc(A["rstd"], 1)
                        dve.wait_ge(A["rstd"], 1)
                        for j in range(CT):
                            dve.scalar_tensor_tensor(out=cv[:, j, :], in0=cv[:, j, :], scalar=v("ln_g", j),
                                                     in1=lrs[:], op0=ALU.mult,
                                                     op1=ALU.mult).then_inc(A["scaled"], 1)
                        for j in range(CT):
                            dve.wait_ge(A["silu"], j + 1)
                            dve.tensor_copy(hhi[:, CT + j, :], lsq[:, j, :]).then_inc(A["chi"], 1)
                            dve.wait_ge(A["chi"], j + 1)
                            dve.tensor_tensor(hlo[:, CT + j, :], lsq[:, j, :], hhi[:, CT + j, :].bitcast(F32),
                                              ALU.subtract).then_inc(A["clo"], 1)

            out_block("wo", [(hhi, hlo)])
        boundary("mix_post", "g1", [(v("ffn_pre"), "sc2", "sh2", hhi, hlo)])

        with ExitStack() as seg:
            fhi = sbuf(seg, "fhi", [P, FT, S], F32R)
            flo = sbuf(seg, "flo", [P, FT, S], F32R)
            fg = sbuf(seg, "fg", [P, 2, S])
            g_ready = sem("g_ready")
            prod_ready = sem("prod_ready")
            fhi_ready = sem("fhi_ready")
            flo_ready = sem("flo_ready")
            c0, q0, a0 = FIRST["ffn_in"], 10, 20
            parts = [(0, ADA_C2 - a0), (ADA_C2 - a0, FT)]
            with nc.Block() as block:
                @block.sync
                def _(sp):
                    pairs(sp, FT, lambda i, r: (load_panel(sp, c0 + r + 2, i), load_ada(sp, a0 + r + 2, i)))

                @block.gpsimd
                def _(pool):
                    for lo, hi in parts:
                        pairs(pool, hi - lo, lambda i, r, lo=lo: ada_multiply(pool, a0 + lo + r, i))

                @block.scalar
                def _(act):
                    def step(i, r):
                        split_hi(act, c0 + r + 1, i)
                        pair = (q0 + r) % 2
                        act.wait_ge(panels_used, at(c0 + r + 1, i))
                        act.activation(fg[:, pair, :], ps[:, 2 * pair, :], ACT.Silu).then_inc(g_ready, 1)
                    pairs(act, FT, step)

                @block.vector
                def _(dve):
                    def step(i, r):
                        split_lo(dve, c0 + r + 1, i)
                        pair = (q0 + r) % 2
                        t = r + i * 2
                        dve.wait_ge(g_ready, at(r + 1, i))
                        dve.tensor_tensor(fg[:, pair, :], ps[:, 2 * pair + 1, :], fg[:, pair, :],
                                          ALU.mult).then_inc(prod_ready, 1)
                        dve.wait_ge(prod_ready, at(r + 1, i))
                        dve.tensor_copy(fhi[:, bass.ds(t, 1), :], fg[:, pair, :]).then_inc(fhi_ready, 1)
                        dve.wait_ge(fhi_ready, at(r + 1, i))
                        dve.tensor_tensor(flo[:, bass.ds(t, 1), :], fg[:, pair, :],
                                          fhi[:, bass.ds(t, 1), :].bitcast(F32),
                                          ALU.subtract).then_inc(pair_free[pair], 1)
                        ada_sum(dve, a0 + r, i)
                    pairs(dve, FT, step)
                    read_mod(dve, 20, 42)

                @block.tensor
                def _(pe):
                    pairs(pe, FT, lambda i, r: (in_panel(pe, c0 + r, q0 + r, i, (hhi, hlo), False),
                                                ada_columns(pe, a0 + r, i)))
            out_block("ffn_out", [(fhi, flo)])
        boundary("ffn_post", "g2", [(v("norm2", 0, KT), "msc", "msh", hhi, hlo)])

        with ExitStack() as seg:
            xbc = sbuf(seg, "xbc", [P, XT, S])
            dtT = sbuf(seg, "dtT", [MH, S])
            acT = sbuf(seg, "acT", [MH, S])
            dt_seq = sem("dt_seq")
            c0, q0, a0 = FIRST["xbc"], 32, 42
            with ExitStack() as tmp:
                wd_raw = sbuf(tmp, "wd_raw", [P, KT, MH])
                wd_hi = sbuf(tmp, "wd_hi", [P, KT, P], F32R)
                wd_lo = sbuf(tmp, "wd_lo", [P, KT, P], F32R)
                dtt = sbuf(tmp, "dtt", [MH, 4, S])
                one_row = sbuf(tmp, "one_row2", [MH, S])
                aneg = sbuf(tmp, "aneg", [MH, 2])
                tap0 = sem("tap0")
                taps = sem("taps")
                xs_ready = sem("xs_ready")
                with nc.Block() as block:
                    @block.sync
                    def _(sp):
                        sp.dma_start(wd_raw[:].rearrange("p k n -> p (k n)"), w_dt).then_inc(small_landed, 16)
                        pairs(sp, XT // 2, lambda i, r: (load_panel(sp, c0 + r + 2, i),
                                                         load_ada(sp, a0 + r + 2, i)))

                    @block.gpsimd
                    def _(pool):
                        pairs(pool, XT // 2, lambda i, r: ada_multiply(pool, a0 + r, i))

                    @block.scalar
                    def _(act):
                        act.activation(aneg[:, 0:1], v("a_log")[0:MH, :], ACT.Exp).then_inc(dt_seq, 1)

                        def step(i, r):
                            split_hi(act, c0 + r + 1, i)
                            pair = (q0 + r) % 2
                            act.wait_ge(panels_used, at(c0 + r + 1, i))
                            for b in range(2):
                                t = 2 * r + b + i * 4
                                bc = VEC["mconv_b"][0] + t
                                wc = VEC["mconv_w"][0] + t * MK + MK - 1
                                act.activation(xbc[:, bass.ds(t, 1), :], ps[:, 2 * pair + b, :], ACT.Identity,
                                               bias=vec[:, bass.ds(bc, 1)],
                                               scale=vec[:, bass.ds(wc, 1)]).then_inc(tap0, 1)
                            act.wait_ge(taps, 6 * r + 6 + i * 12)
                            for half in (1, 0):
                                both = xbc[:, bass.ds(2 * r + i * 4, 2), half * 256:half * 256 + 256]
                                act.activation(both, both, ACT.Silu).then_inc(xs_ready, 1)
                        pairs(act, XT // 2, step)
                        small_exp(act, dtt, MH, 20, 2)

                    @block.vector
                    def _(dve):
                        dve.memset(one_row[:], 1.0).then_inc(pad_ready, 1)
                        dve.wait_ge(small_landed, 48)
                        split_small(dve, wd_hi, wd_lo, wd_raw, MH, 4)

                        def step(i, r):
                            split_lo(dve, c0 + r + 1, i)
                            pair = (q0 + r) % 2
                            for s in range(1, MK):
                                for b in range(2):
                                    t = 2 * r + b + i * 4
                                    wc = VEC["mconv_w"][0] + t * MK + MK - 1 - s
                                    if s == 1:
                                        dve.wait_ge(tap0, 2 * r + b + 1 + i * 4)
                                    else:
                                        dve.wait_ge(taps, 6 * r + (s - 1) * 2 + b - 1 + i * 12)
                                    ins = dve.scalar_tensor_tensor(
                                        out=xbc[:, bass.ds(t, 1), s:S], in0=ps[:, 2 * pair + b, 0:S - s],
                                        scalar=vec[:, bass.ds(wc, 1)], in1=xbc[:, bass.ds(t, 1), s:S],
                                        op0=ALU.mult, op1=ALU.add)
                                    ins.then_inc(taps, 1)
                            dve.wait_ge(taps, 6 * r + 6 + i * 12)
                            dve.sem_inc(pair_free[pair], 1)
                            ada_sum(dve, a0 + r, i)
                        pairs(dve, XT // 2, step)
                        read_mod(dve, 42, 54)
                        last, then = log1p_exp(dve, dtt, MH, v("dt_bias")[0:MH, :], 17, 2)
                        dve.tensor_scalar(dtt[:, 2, :], dtt[:, 0, :], 0.0, None, ALU.max).then_inc(dt_seq, 1)
                        dve.wait_ge(dt_seq, 2)
                        dve.tensor_tensor(dtT[:], dtt[:, 2, :], dtt[:, 1, :], ALU.add).then_inc(dt_seq, 1)
                        dve.tensor_scalar(aneg[:, 1:2], aneg[:, 0:1], -1.0, None, ALU.mult).then_inc(dt_seq, 1)
                        dve.wait_ge(dt_seq, 4)
                        dve.tensor_scalar(dtt[:, 3, :], dtT[:], aneg[:, 1:2], None, ALU.mult).then_inc(dt_seq, 1)
                        dve.wait_ge(dt_seq, 5)
                        for c in range(TB):
                            w = slice(c * P, (c + 1) * P)
                            dve.tensor_tensor_scan(acT[:, w], one_row[:, w], dtt[:, 3, w], 0.0, ALU.mult,
                                                   ALU.add).then_inc(dt_seq, 1)

                    @block.tensor
                    def _(pe):
                        small_projection(pe, wd_hi, wd_lo, 8)
                        pairs(pe, XT // 2, lambda i, r: (in_panel(pe, c0 + r, q0 + r, i, (hhi, hlo), False),
                                                         ada_columns(pe, a0 + r, i)))

            GH = MH // MG
            HB = 4
            with ExitStack() as tmp:
                xdt = sbuf(tmp, "xdt", [P, MH, HD])
                xw = sbuf(tmp, "xw", [P, MH, HD])
                btok = sbuf(tmp, "btok", [P, MG, MN])
                cb = sbuf(tmp, "cb", [P, MG, P])
                seg_t = sbuf(tmp, "seg_t", [P, 2, HB, P])
                dec = sbuf(tmp, "dec", [P, 2, HB, P])
                ea = sbuf(tmp, "ea", [P, 2, 4, P])
                state = sbuf(tmp, "state", [P, MG, GH * HD])
                dtc = sbuf(tmp, "dtc", [P, TB, MH])
                acc_c = sbuf(tmp, "acc_c", [P, TB, MH])
                dend = sbuf(tmp, "dend", [P, TB, MH])
                wend = sbuf(tmp, "wend", [P, TB, MH])
                M = {k: sem("m_" + k) for k in ("cols", "cols_c", "end", "wend0", "ends", "xdt", "xw", "bt",
                                                "btok", "cb", "cbm", "bc", "seg", "clip", "dec", "mat", "eab",
                                                "ea", "yo", "yd", "yscaled", "yskip", "ysum", "st", "decay",
                                                "state")}
                NB = MH // HB
                with nc.Block() as block:
                    @block.tensor
                    def _(pe):
                        for c in range(TB):
                            w = slice(c * P, (c + 1) * P)
                            pe.transpose(ps[:, 0, c * MH:(c + 1) * MH], dtT[:, w], ident[0:MH, 0:MH])
                            pe.transpose(ps[:, 0, P + c * MH:P + (c + 1) * MH], acT[:, w], ident[0:MH, 0:MH])
                            mm = pe.matmul(ps[:, 0, 2 * P + c * MH:2 * P + (c + 1) * MH],
                                           acT[:, c * P + P - 1:(c + 1) * P].to_broadcast([MH, P]),
                                           ident[0:MH, 0:MH], start=True, stop=True)
                        mm.then_inc(M["cols"], 1)

                        def along(n):
                            c, b = n // NB, n % NB
                            if n >= 2:
                                pe.wait_ge(M["seg"], n - 1)
                            for j in range(HB):
                                h = b * HB + j
                                mm = pe.matmul(ps[:, 2 + n % 2, j * P:(j + 1) * P],
                                               ident[0:MH, h:h + 1].to_broadcast([MH, P]),
                                               acT[:, c * P:(c + 1) * P], start=True, stop=True)
                            mm.then_inc(M["bc"], 1)

                        for c in range(TB):
                            w = slice(c * P, (c + 1) * P)
                            if c == 0:
                                pe.wait_ge(M["cols_c"], 3)
                            for r in range(4):
                                n = c * 6 + r
                                if r >= 2:
                                    pe.wait_ge(M["xdt"], 4 * c + r - 1)
                                elif c:
                                    pe.wait_ge(M["btok"] if r == 0 else M["cbm"], c)
                                for j in range(4):
                                    mm = pe.transpose(ps[:, n % 2, j * P:(j + 1) * P], xbc[:, 4 * r + j, w], ident)
                                mm.then_inc(M["bt"], 1)
                            if c < TB - 1:
                                pe.wait_ge(M["xdt"], 4 * c + 3)
                                for g in range(MG):
                                    mm = pe.transpose(ps[:, 0, g * P:(g + 1) * P], xbc[:, MT + g, w], ident)
                                mm.then_inc(M["bt"], 1)
                            pe.wait_ge(M["xdt"], 4 * c + 4)
                            for g in range(MG):
                                mm = pe.matmul(ps[:, 1, g * P:(g + 1) * P], xbc[:, MT + g, w],
                                               xbc[:, MT + MG + g, w], start=True, stop=True)
                            mm.then_inc(M["bt"], 1)
                            if c == 0:
                                along(0)
                            for g in range(MG):
                                gi = c * MG + g
                                if gi:
                                    pe.wait_ge(M["ea"], gi)
                                for j in range(GH):
                                    h, o = GH * g + j, HD * (j % 2)
                                    mm = pe.matmul(ps[o:o + HD, 4, j // 2 * P:(j // 2 + 1) * P],
                                                   ident[0:MH, h:h + 1].to_broadcast([MH, HD]),
                                                   acT[:, w], start=True, stop=True)
                                mm.then_inc(M["eab"], 1)
                                if c:
                                    pe.wait_ge(M["state"], 4 * (c - 1) + g + 1)
                                    if gi > MG:
                                        pe.wait_ge(M["yscaled"], gi - MG)
                                    for j in range(4):
                                        mm = pe.matmul(ps[:, 5, j * P:(j + 1) * P],
                                                       state[:, g, j * P:(j + 1) * P],
                                                       xbc[:, MT + MG + g, w], start=True, stop=True)
                                    mm.then_inc(M["yo"], 1)
                                for b in range(2):
                                    n = c * NB + g * 2 + b
                                    if n + 1 < TB * NB:
                                        along(n + 1)
                                    pe.wait_ge(M["mat"], n + 1)
                                    if b == 0 and gi >= 2:
                                        pe.wait_ge(M["yskip"], 4 * (gi - 1))
                                    for j in range(HB):
                                        h = g * GH + b * HB + j
                                        o = HD * (h % 2)
                                        t = (b * HB + j) // 2
                                        mm = pe.matmul(ps[o:o + HD, 6 + gi % 2, t * P:(t + 1) * P],
                                                       xdt[:, h, :], dec[:, n % 2, j, :], start=True, stop=True)
                                    mm.then_inc(M["yd"], 1)
                            if c < TB - 1:
                                pe.wait_ge(M["xw"], c + 1)
                                pe.wait_ge(M["btok"], c + 1)
                                for g in range(MG):
                                    n = c * MG + g
                                    pe.wait_ge(M["cbm"], c + 1)
                                    if g >= 2:
                                        pe.wait_ge(M["state"], n - 1)
                                    pe.matmul(ps[:, g % 2, :], btok[:, g, :],
                                              xw[:, g * GH:(g + 1) * GH, :], start=True,
                                              stop=True).then_inc(M["st"], 1)
                                pe.wait_ge(M["state"], 4 * (c + 1))

                    @block.scalar
                    def _(act):
                        act.wait_ge(M["cols_c"], 3)
                        act.wait_ge(M["wend0"], 1)
                        act.activation(dend[:], dend[:], ACT.Exp).then_inc(M["ends"], 1)
                        act.activation(wend[:], wend[:], ACT.Exp).then_inc(M["ends"], 1)
                        for c in range(TB):
                            if c < TB - 1:
                                act.wait_ge(M["bt"], 6 * c + 5)
                                if c:
                                    act.wait_ge(M["st"], 4 * c)
                                act.activation(btok[:], ps[:, 0, :].rearrange("p (g t) -> p g t", g=MG),
                                               ACT.Copy).then_inc(M["btok"], 1)
                            for g in range(MG):
                                gi = c * MG + g
                                act.wait_ge(M["eab"], gi + 1)
                                if c and gi >= MG + 2:
                                    act.wait_ge(M["yscaled"], gi - MG - 1)
                                act.activation(ea[:, gi % 2, :, :],
                                               ps[:, 4, :].rearrange("p (j t) -> p j t", j=4),
                                               ACT.Exp).then_inc(M["ea"], 1)
                                for b in range(2):
                                    n = c * NB + g * 2 + b
                                    act.wait_ge(M["clip"], n + 1)
                                    if n >= 2:
                                        act.wait_ge(M["yd"], n - 1)
                                    act.activation(dec[:, n % 2, :, :], seg_t[:, n % 2, :, :],
                                                   ACT.Exp).then_inc(M["dec"], 1)

                    @block.gpsimd
                    def _(pool):
                        for c in range(TB):
                            for b in range(NB):
                                n = c * NB + b
                                pool.wait_ge(M["dec"], n + 1)
                                pool.wait_ge(M["cbm"], c + 1)
                                pool.tensor_tensor(dec[:, n % 2, :, :], dec[:, n % 2, :, :],
                                                   cb[:, b // 2, :].unsqueeze(1).to_broadcast([P, HB, P]),
                                                   ALU.mult).then_inc(M["mat"], 1)

                    @block.vector
                    def _(dve):
                        dve.wait_ge(M["cols"], 1)
                        for k, t in enumerate((dtc, acc_c, dend)):
                            dve.tensor_copy(t[:], ps[:, 0, k * P:(k + 1) * P].rearrange("p (c h) -> p c h", c=TB)
                                            ).then_inc(M["cols_c"], 1)
                        dve.wait_ge(M["cols_c"], 3)
                        dve.tensor_tensor(wend[:], dend[:], acc_c[:], ALU.subtract).then_inc(M["wend0"], 1)

                        def difference(n):
                            c, b = n // NB, n % NB
                            dve.wait_ge(M["bc"], n + 1)
                            if n >= 2:
                                dve.wait_ge(M["dec"], n - 1)
                            dve.tensor_tensor(seg_t[:, n % 2, :, :],
                                              ps[:, 2 + n % 2, :].rearrange("p (j t) -> p j t", j=HB),
                                              acc_c[:, c, b * HB:(b + 1) * HB].unsqueeze(2).to_broadcast([P, HB, P]),
                                              ALU.subtract).then_inc(M["seg"], 1)
                            dve.wait_ge(M["seg"], n + 1)
                            dve.tensor_scalar(seg_t[:, n % 2, :, :], seg_t[:, n % 2, :, :], 0.0, None,
                                              ALU.min).then_inc(M["clip"], 1)

                        for c in range(TB):
                            w = slice(c * P, (c + 1) * P)
                            for r in range(4):
                                n = c * 6 + r
                                dve.wait_ge(M["bt"], n + 1)
                                if c:
                                    dve.wait_ge(M["yd"], NB * c)
                                    dve.wait_ge(M["xw"], c)
                                dve.tensor_tensor(xdt[:, 8 * r:8 * r + 8, :],
                                                  ps[:, n % 2, :].rearrange("p (h d) -> p h d", h=8),
                                                  dtc[:, c, 8 * r:8 * r + 8].unsqueeze(2).to_broadcast([P, 8, HD]),
                                                  ALU.mult).then_inc(M["xdt"], 1)
                            dve.wait_ge(M["bt"], 6 * c + (6 if c < TB - 1 else 5))
                            if c:
                                dve.wait_ge(M["mat"], NB * c)
                            dve.tensor_tensor(cb[:], ps[:, 1, :].rearrange("p (g t) -> p g t", g=MG),
                                              consts[:, CST["upper"], :].unsqueeze(1).to_broadcast([P, MG, P]),
                                              ALU.mult).then_inc(M["cbm"], 1)
                            if c < TB - 1:
                                dve.wait_ge(M["xdt"], 4 * c + 4)
                                dve.wait_ge(M["ends"], 2)
                                if c:
                                    dve.wait_ge(M["st"], 4 * c)
                                dve.tensor_tensor(xw[:], xdt[:],
                                                  wend[:, c, :].unsqueeze(2).to_broadcast([P, MH, HD]),
                                                  ALU.mult).then_inc(M["xw"], 1)
                            if c == 0:
                                difference(0)
                            for g in range(MG):
                                gi = c * MG + g
                                for b in range(2):
                                    n = c * NB + g * 2 + b
                                    if n + 1 < TB * NB:
                                        difference(n + 1)
                                if c:
                                    dve.wait_ge(M["yo"], gi - MG + 1)
                                    dve.wait_ge(M["ea"], gi + 1)
                                    dve.tensor_tensor(ea[:, gi % 2, :, :],
                                                      ps[:, 5, :].rearrange("p (j t) -> p j t", j=4),
                                                      ea[:, gi % 2, :, :], ALU.mult).then_inc(M["yscaled"], 1)
                                dve.wait_ge(M["yd"], 2 * gi + 2)
                                for j in range(4):
                                    t = 4 * g + j
                                    dve.scalar_tensor_tensor(out=xbc[:, t, w], in0=xbc[:, t, w],
                                                             scalar=v("m_d", t),
                                                             in1=ps[:, 6 + gi % 2, j * P:(j + 1) * P],
                                                             op0=ALU.mult, op1=ALU.add).then_inc(M["yskip"], 1)
                                if c:
                                    dve.wait_ge(M["yskip"], 4 * gi + 4)
                                    dve.wait_ge(M["yscaled"], gi - MG + 1)
                                    dve.tensor_tensor(xbc[:, 4 * g:4 * g + 4, w], xbc[:, 4 * g:4 * g + 4, w],
                                                      ea[:, gi % 2, :, :], ALU.add).then_inc(M["ysum"], 1)
                            if c < TB - 1:
                                for g in range(MG):
                                    n = c * MG + g
                                    dve.wait_ge(M["st"], n + 1)
                                    if c == 0:
                                        dve.tensor_copy(state[:, g, :], ps[:, g % 2, :]).then_inc(M["state"], 1)
                                    else:
                                        s3 = state[:, g, :].rearrange("p (h d) -> p h d", h=GH)
                                        dve.tensor_tensor(s3, s3, dend[:, c, g * GH:(g + 1) * GH].unsqueeze(2)
                                                          .to_broadcast([P, GH, HD]),
                                                          ALU.mult).then_inc(M["decay"], 1)
                                        dve.wait_ge(M["decay"], n - MG + 1)
                                        dve.tensor_tensor(state[:, g, :], state[:, g, :], ps[:, g % 2, :],
                                                          ALU.add).then_inc(M["state"], 1)

            c0, q0, a0 = FIRST["z"], 44, 54
            y2hi = sbuf(seg, "y2hi", [P, KT, S], F32R)
            y2lo = sbuf(seg, "y2lo", [P, KT, S], F32R)
            with ExitStack() as tmp:
                sz = sbuf(tmp, "sz", [P, 2, 2, S])
                gsq = sbuf(tmp, "gsq", [P, 2, S])
                gstd = sz[:, :, :, :].rearrange("p a b s -> p (a b) s")
                G = {k: sem("g_" + k) for k in ("sz", "gated", "sq", "ss", "std", "rs", "scaled", "hi", "lo")}
                with nc.Block() as block:
                    @block.sync
                    def _(sp):
                        pairs(sp, MT // 2, lambda i, r: load_panel(sp, c0 + r + 2, i))

                    @block.gpsimd
                    def _(pool):
                        for r in range(2):
                            ada_multiply(pool, a0 + r, 0)

                    @block.scalar
                    def _(act):
                        def step(i, r):
                            split_hi(act, c0 + r + 1, i)
                            pair = (q0 + r) % 2
                            act.wait_ge(panels_used, at(c0 + r + 1, i))
                            if not isinstance(i, int):
                                act.wait_ge(G["gated"], at(r, i))
                            act.activation(sz[:, pair, :, :], ps[:, 2 * pair:2 * pair + 2, :],
                                           ACT.Silu).then_inc(G["sz"], 1)
                        pairs(act, MT // 2, step)
                        for t in range(MT):
                            act.wait_ge(G["gated"], MT // 2)
                            if t >= 2:
                                act.wait_ge(G["ss"], t - 1)
                            act.activation(gsq[:, t % 2, :], xbc[:, t, :], ACT.Square).then_inc(G["sq"], 1)
                        for g in range(MG):
                            act.wait_ge(G["ss"], 4 * g + 4)
                            act.activation(gstd[:, g, :], ps[:, g, :], ACT.Sqrt, bias=eps[:, 0:1],
                                           scale=MG / MI).then_inc(G["std"], 1)
                        for t in range(MT):
                            act.wait_ge(G["scaled"], t + 1)
                            dst = hhi if t < KT else y2hi
                            act.activation(dst[:, t % KT, :], xbc[:, t, :], ACT.Copy).then_inc(G["hi"], 1)

                    @block.vector
                    def _(dve):
                        def step(i, r):
                            split_lo(dve, c0 + r + 1, i)
                            pair = (q0 + r) % 2
                            dve.wait_ge(G["sz"], at(r + 1, i))
                            dst = xbc[:, bass.ds(2 * r + i * 4, 2), :]
                            dve.tensor_tensor(dst, dst, sz[:, pair, :, :], ALU.mult).then_inc(G["gated"], 1)
                            dve.wait_ge(G["gated"], at(r + 1, i))
                            dve.sem_inc(pair_free[pair], 1)
                        pairs(dve, MT // 2, step)
                        for r in range(2):
                            ada_sum(dve, a0 + r, 0)
                        read_mod(dve, 54, 56)

                        def lo_part(t):
                            shi, slo = (hhi, hlo) if t < KT else (y2hi, y2lo)
                            dve.wait_ge(G["hi"], t + 1)
                            dve.tensor_tensor(slo[:, t % KT, :], xbc[:, t, :], shi[:, t % KT, :].bitcast(F32),
                                              ALU.subtract).then_inc(G["lo"], 1)
                        for g in range(MG):
                            dve.wait_ge(G["std"], g + 1)
                            dve.reciprocal(gstd[:, g, :], gstd[:, g, :]).then_inc(G["rs"], 1)
                            dve.wait_ge(G["rs"], g + 1)
                            for t in range(4 * g, 4 * g + 4):
                                dve.scalar_tensor_tensor(out=xbc[:, t, :], in0=xbc[:, t, :], scalar=v("m_norm", t),
                                                         in1=gstd[:, g, :], op0=ALU.mult,
                                                         op1=ALU.mult).then_inc(G["scaled"], 1)
                                if t:
                                    lo_part(t - 1)
                        lo_part(MT - 1)

                    @block.tensor
                    def _(pe):
                        pairs(pe, MT // 2, lambda i, r: in_panel(pe, c0 + r, q0 + r, i, (hhi, hlo), False))
                        for r in range(2):
                            ada_columns(pe, a0 + r, 0)
                        pe.wait_ge(pair_free[0], 27)
                        pe.wait_ge(pair_free[1], 27)
                        for t in range(MT):
                            pe.wait_ge(G["sq"], t + 1)
                            pe.matmul(ps[:, t // 4, :], ones, gsq[:, t % 2, :], start=t % 4 == 0,
                                      stop=t % 4 == 3).then_inc(G["ss"], 1)
            out_block("m_out", [(hhi, hlo), (y2hi, y2lo)])

        with ExitStack() as seg:
            k2 = sbuf(seg, "k2", [P, KT, S])
            v2 = sbuf(seg, "v2", [P, TB, D])
            q2 = sbuf(seg, "q2", [P, KT, S])
            z2 = sbuf(seg, "z2", [P, KT, S])
            with ExitStack() as tmp:
                h2hi = sbuf(tmp, "h2hi", [P, KT, S], F32R)
                h2lo = sbuf(tmp, "h2lo", [P, KT, S], F32R)
                boundary(None, "mg", [(v("kv_norm"), "kvsc", "kvsh", hhi, hlo),
                                      (v("norm2", KT, KT), "ssc", "ssh", h2hi, h2lo)], room=z2)
                c0, q0 = FIRST["k2"], 52
                segs = [("k2", False, (hhi, hlo)), ("v2", True, (hhi, hlo)), ("q2", False, (h2hi, h2lo)),
                        ("z2", False, (h2hi, h2lo))]
                with nc.Block() as block:
                    @block.sync
                    def _(sp):
                        pairs(sp, 16, lambda i, r: load_panel(sp, c0 + r + 2, i))

                    @block.scalar
                    def _(act):
                        for s, (name, by_token, _) in enumerate(segs):
                            def step(i, r, s=s, name=name):
                                split_hi(act, c0 + 4 * s + r + 1, i)
                                pair = (q0 + r) % 2
                                act.wait_ge(panels_used, at(c0 + 4 * s + r + 1, i))
                                bank = ps[:, 2 * pair:2 * pair + 2, :]
                                if name == "v2":
                                    act.activation(v2[:, :, bass.ds(r * 256 + i * 512, 256)],
                                                   bank.rearrange("p a (b c) -> p (a b) c", b=2),
                                                   ACT.Copy).then_inc(pair_free[pair], 1)
                                else:
                                    dst = {"k2": k2, "q2": q2, "z2": z2}[name]
                                    act.activation(dst[:, bass.ds(2 * r + i * 4, 2), :], bank,
                                                   ACT.Silu if name == "z2" else ACT.Copy,
                                                   scale=HD ** -0.5 if name == "q2" else 1.0
                                                   ).then_inc(pair_free[pair], 1)
                            pairs(act, 4, step)

                    @block.vector
                    def _(dve):
                        pairs(dve, 16, lambda i, r: split_lo(dve, c0 + r + 1, i))

                    @block.tensor
                    def _(pe):
                        for s, (_, by_token, src) in enumerate(segs):
                            pairs(pe, 4, lambda i, r: in_panel(pe, c0 + 4 * s + r, q0 + 4 * s + r, i, src, by_token))

            NU = TB * H2
            with ExitStack() as tmp:
                sig = sbuf(tmp, "sig", [P, 2, S])
                keep = sbuf(tmp, "keep", [P, 2, S])
                rest = sbuf(tmp, "rest", [P, 2, S + 1])
                zero = sbuf(tmp, "zero", [P, S])
                am = sbuf(tmp, "am", [P, 2, S])
                amt = sbuf(tmp, "amt", [P, 2, S])
                o2 = sbuf(tmp, "o2", [P, 2, D])
                og = sbuf(tmp, "og", [P, 2, 4, P])
                B = {k: sem("b_" + k) for k in ("zero", "z_done", "sig", "keep", "rest", "am", "t_done", "amt",
                                                "pv_done", "o_ready", "ot_done", "og", "ohi", "olo")}
                units = [(qb, h) for qb in range(TB) for h in range(H2)]
                with nc.Block() as block:
                    @block.tensor
                    def _(pe):
                        def logits(n):
                            qb, h = units[n]
                            nk = (qb + 1) * P
                            r0 = HD * (h % 2)
                            if n >= 2:
                                pe.wait_ge(B["keep"], n - 1)
                            pe.matmul(ps[:, n % 2, 0:nk], q2[r0:r0 + HD, h // 2, qb * P:nk],
                                      k2[r0:r0 + HD, h // 2, 0:nk], start=True, stop=False)
                            pe.matmul(ps[:, n % 2, qb * P:nk], ident, consts[:, CST["neg_from"], :],
                                      start=False, stop=True).then_inc(B["z_done"], 1)

                        def turn(n):
                            qb, h = units[n]
                            pe.wait_ge(B["am"], n + 1)
                            if n >= 2:
                                pe.wait_ge(B["amt"], n - 1)
                            for kb in range(qb + 1):
                                mm = pe.transpose(ps[:, 2 + n % 2, kb * P:(kb + 1) * P],
                                                  am[:, n % 2, kb * P:(kb + 1) * P], ident)
                            mm.then_inc(B["t_done"], 1)

                        def values(n):
                            qb, h = units[n]
                            half = n // 8
                            pe.wait_ge(B["amt"], n + 1)
                            if n % 8 == 0 and half >= 2:
                                pe.wait_ge(B["o_ready"], half - 1)
                            for kb in range(qb + 1):
                                mm = pe.matmul(ps[:, 4 + half % 2, (h % 8) * HD:(h % 8 + 1) * HD],
                                               amt[:, n % 2, kb * P:(kb + 1) * P],
                                               v2[:, kb, h * HD:(h + 1) * HD], start=kb == 0, stop=kb == qb)
                            mm.then_inc(B["pv_done"], 1)

                        def turn_out(half):
                            pe.wait_ge(B["o_ready"], half + 1)
                            if half >= 2:
                                pe.wait_ge(B["og"], half - 1)
                            for t in range(4):
                                mm = pe.transpose(ps[:, 6 + half % 2, t * P:(t + 1) * P],
                                                  o2[:, half % 2, t * P:(t + 1) * P], ident)
                            mm.then_inc(B["ot_done"], 1)

                        for n in range(NU + 5):
                            if n < NU:
                                logits(n)
                            if 2 <= n <= NU + 1:
                                turn(n - 2)
                            if 3 <= n <= NU + 2:
                                values(n - 3)
                            if n >= 12 and (n - 4) % 8 == 0:
                                turn_out((n - 4) // 8 - 1)

                    @block.scalar
                    def _(act):
                        def take(n):
                            qb, h = units[n]
                            nk = (qb + 1) * P
                            act.wait_ge(B["t_done"], n + 1)
                            if n >= 2:
                                act.wait_ge(B["pv_done"], n - 1)
                            act.activation(amt[:, n % 2, 0:nk], ps[:, 2 + n % 2, 0:nk], ACT.Copy).then_inc(B["amt"], 1)

                        def out_take(half):
                            act.wait_ge(B["pv_done"], 8 * half + 8)
                            if half >= 2:
                                act.wait_ge(B["ot_done"], half - 1)
                            act.activation(o2[:, half % 2, 0:512], ps[:, 4 + half % 2, :],
                                           ACT.Copy).then_inc(B["o_ready"], 1)

                        def out_hi(half):
                            qb, t0 = half // 2, 4 * (half % 2)
                            act.wait_ge(B["og"], half + 1)
                            act.activation(hhi[:, t0:t0 + 4, qb * P:(qb + 1) * P], og[:, half % 2, :, :],
                                           ACT.Copy).then_inc(B["ohi"], 1)

                        for n in range(NU + 6):
                            if n < NU:
                                qb, h = units[n]
                                nk = (qb + 1) * P
                                act.wait_ge(B["z_done"], n + 1)
                                if n >= 2:
                                    act.wait_ge(B["am"], n - 1)
                                act.activation(sig[:, n % 2, 0:nk], ps[:, n % 2, 0:nk],
                                               ACT.Sigmoid).then_inc(B["sig"], 1)
                                act.activation(keep[:, n % 2, 0:nk], ps[:, n % 2, 0:nk], ACT.Sigmoid,
                                               scale=-1.0).then_inc(B["keep"], 1)
                            if 2 <= n <= NU + 1:
                                take(n - 2)
                            if n >= 11 and (n - 3) % 8 == 0:
                                out_take((n - 3) // 8 - 1)
                            if n >= 13 and (n - 5) % 8 == 0:
                                out_hi((n - 5) // 8 - 1)

                    @block.gpsimd
                    def _(pool):
                        for n, (qb, h) in enumerate(units):
                            nk = (qb + 1) * P
                            pool.wait_ge(B["rest"], n + 1)
                            if n >= 2:
                                pool.wait_ge(B["t_done"], n - 1)
                            pool.tensor_tensor(am[:, n % 2, 0:nk], sig[:, n % 2, 0:nk], rest[:, n % 2, 1:nk + 1],
                                               ALU.mult).then_inc(B["am"], 1)

                    @block.vector
                    def _(dve):
                        dve.memset(zero[:], 0.0).then_inc(B["zero"], 1)
                        dve.wait_ge(B["zero"], 1)

                        def out_gate(half):
                            qb, t0 = half // 2, 4 * (half % 2)
                            dve.wait_ge(B["ot_done"], half + 1)
                            if half >= 2:
                                dve.wait_ge(B["olo"], half - 1)
                            dve.tensor_tensor(og[:, half % 2, :, :],
                                              ps[:, 6 + half % 2, :].rearrange("p (t q) -> p t q", t=4),
                                              z2[:, t0:t0 + 4, qb * P:(qb + 1) * P], ALU.mult).then_inc(B["og"], 1)

                        def out_lo(half):
                            qb, t0 = half // 2, 4 * (half % 2)
                            dve.wait_ge(B["ohi"], half + 1)
                            dve.tensor_tensor(hlo[:, t0:t0 + 4, qb * P:(qb + 1) * P], og[:, half % 2, :, :],
                                              hhi[:, t0:t0 + 4, qb * P:(qb + 1) * P].bitcast(F32),
                                              ALU.subtract).then_inc(B["olo"], 1)
                        for n in range(NU + 7):
                            if n < NU:
                                qb, h = units[n]
                                nk = (qb + 1) * P
                                if n >= 2:
                                    dve.wait_ge(B["am"], n - 1)
                                dve.memset(rest[:, n % 2, nk:nk + 1], 1.0).then_inc(B["zero"], 1)
                                dve.wait_ge(B["keep"], n + 1)
                                dve.tensor_tensor_scan(rest[:, n % 2, 0:nk][:, ::-1], keep[:, n % 2, 0:nk][:, ::-1],
                                                       zero[:, 0:nk], 1.0, ALU.mult,
                                                       ALU.add).then_inc(B["rest"], 1)
                            if n >= 12 and (n - 4) % 8 == 0:
                                out_gate((n - 4) // 8 - 1)
                            if n >= 14 and (n - 6) % 8 == 0:
                                out_lo((n - 6) // 8 - 1)
            out_block("sb_out", [(hhi, hlo)])
        boundary(None, "sg", [], final=True)


def _tiles(a):
    return a.reshape(-1, P).T


def _in_panel(w):
    return w.reshape(KT, P, 2, P).transpose(1, 0, 2, 3).reshape(P, 2048)


def _in_panels(w):
    return [_in_panel(w[:, i:i + 256]) for i in range(0, w.shape[1], 256)]


def _paired_panels(a, b):
    return [_in_panel(np.concatenate([a[:, i:i + P], b[:, i:i + P]], 1)) for i in range(0, a.shape[1], P)]


def _out_panels(w):
    w = w.reshape(-1, 2, P, KT, P).transpose(0, 2, 1, 3, 4)
    return [p.reshape(P, 2048) for p in w]


def _padded(a):
    return np.concatenate([a, np.zeros(P - a.shape[0], a.dtype)])[:, None]


def kernel(**inputs):
    import concourse.bacc as bacc
    from concourse.bass_utils import run_bass_kernel_spmd

    g = {k: np.asarray(a) for k, a in inputs.items()}
    w_in = g["w_in"][0]
    w_ffn = g["w_ffn_in"][0]
    m_in = g["m_in_w_2"][0]
    sb_in = g["sb_in_w_2"][0]
    a3 = 3 * AW
    weights = (_paired_panels(w_in[:, a3 + H1:a3 + H1 + AW], w_in[:, a3 + H1 + AW:])
               + _in_panels(w_in[:, 0:a3])
               + _out_panels(g["w_o"][0])
               + _paired_panels(w_ffn[:, 0:DFF], w_ffn[:, DFF:])
               + _out_panels(g["w_ffn_out"][0])
               + _in_panels(m_in[:, MI:MI + XT * P])
               + _in_panels(m_in[:, 0:MI])
               + _out_panels(g["m_out_w_2"][0])
               + _in_panels(g["kv_w_2"])
               + _in_panels(sb_in)
               + _out_panels(g["sb_out_w_2"][0]))
    ada_w = np.concatenate([g["ada_w"][0], g["ada_w_2"][0], g["kv_ada_w_2"], g["ada_w_2"][1]], 1)
    ada_b = np.concatenate([g["ada_b"][0], g["ada_b_2"][0], g["kv_ada_b_2"], g["ada_b_2"][1]])
    ada = [ada_w[:, i:i + 256].reshape(KT, P, 256).transpose(1, 0, 2).reshape(P, 2048)
           for i in range(0, ada_w.shape[1], 256)]
    vectors = dict(
        c=_tiles(g["c"]), c2=_tiles(g["c_2"]), ada_b=_tiles(ada_b), mix_pre=_tiles(g["mix_pre_g"]),
        mix_post=_tiles(g["mix_post_g"]), ffn_pre=_tiles(g["ffn_pre_g"]), ffn_post=_tiles(g["ffn_post_g"]),
        conv_w=g["conv_w"][0].reshape(CK, CT, P).transpose(2, 1, 0).reshape(P, CT * CK),
        conv_b=_tiles(g["conv_b"]), ln_g=_tiles(g["conv_ln_g"]), ln_b=_tiles(g["conv_ln_b"]),
        norm2=_tiles(g["norm_g_2"]),
        mconv_w=g["m_conv_w_2"][0].reshape(MK, XT, P).transpose(2, 1, 0).reshape(P, XT * MK),
        mconv_b=_tiles(g["m_conv_b_2"]), m_norm=_tiles(g["m_norm_g_2"]),
        m_d=_tiles(np.repeat(g["m_d_2"][0], HD)), kv_norm=_tiles(g["kv_norm_g_2"]),
        final=_tiles(g["final_g_2"]), b_f=_padded(g["b_f"][0]), dt_bias=_padded(g["m_dt_bias_2"][0]),
        a_log=_padded(g["m_a_log_2"][0]))
    i = np.arange(P)
    shapes = np.stack([np.eye(P), i[:, None] <= i[None, :], (i[None, :] > i[:, None]) * NEG,
                       (i[None, :] >= i[:, None]) * NEG, np.ones((P, P))], 1).astype(np.float32)
    arrays = {
        "x_in": g["x"][0].T.reshape(KT, P, S).transpose(1, 0, 2),
        "panels": np.stack(weights),
        "ada": np.stack(ada),
        "vecs": np.concatenate([vectors[k] for k in VEC], 1),
        "cst": shapes.reshape(P, 5 * P),
        "w_f": w_in[:, a3:a3 + H1].reshape(KT, P, H1).transpose(1, 0, 2).reshape(P, KT * H1),
        "w_dt": m_in[:, MI + XT * P:].reshape(KT, P, MH).transpose(1, 0, 2).reshape(P, KT * MH),
    }
    arrays = {k: np.ascontiguousarray(a) for k, a in arrays.items()}
    nc = bacc.Bacc("TRN2", target_bir_lowering=False, num_devices=1, dynamic_dma_scratch_size=1024)
    args = [nc.dram_tensor(k, a.shape, mybir.dt.from_np(a.dtype), kind="ExternalInput").ap()
            for k, a in arrays.items()]
    out = nc.dram_tensor("out", (KT, P, S), F32, kind="ExternalOutput").ap()
    build(nc, *args, out)
    r = run_bass_kernel_spmd(nc, [arrays], core_ids=[0])
    return r.results[0]["out"].reshape(D, S).T.reshape(1, S, D)
```

```python
from contextlib import ExitStack

import numpy as np

import concourse.bass as bass
from concourse import mybir

F32 = mybir.dt.float32
F32R = mybir.dt.float32r
ALU = mybir.AluOpType
ACT = mybir.ActivationFunctionType
AX = mybir.AxisListType

P = 128
S = 512
TB = S // P
D = 1024
KT = D // P
EPS = 1e-6
NEG = -1.0e30

AW = D // 2
HD = 64
H1 = AW // HD
CT = AW // P
CK = 31
DFF = 2816
FT = DFF // P

MI = 2 * D
MT = MI // P
MH = MI // HD
MG = 4
MN = 128
XT = (MI + 2 * MG * MN) // P
MK = 4

H2 = D // HD

SEGS = [("conv", CT), ("q1", AW // 256), ("k1", AW // 256), ("v1", AW // 256), ("wo", KT // 2),
        ("ffn_in", FT), ("ffn_out", FT // 2), ("xbc", XT // 2), ("z", MT // 2), ("m_out", MT // 2),
        ("k2", KT // 2), ("v2", KT // 2), ("q2", KT // 2), ("z2", KT // 2), ("sb_out", KT // 2)]
FIRST = {}
NPAN = 0
for _name, _n in SEGS:
    FIRST[_name] = NPAN
    NPAN += _n
COUNT = dict(SEGS)

MOD = dict(sh1=0, sc1=8, g1=16, sh2=24, sc2=32, g2=40, msh=48, msc=56, mg=64, kvsh=72, kvsc=80, ssh=88,
           ssc=96, sg=104)
NMOD = 112
NADA = NMOD // 2
ADA_C2 = 24
ADA_FIRST = 10

VEC = {}
NVEC = 0
for _name, _n in [("c", KT), ("c2", KT), ("ada_b", NMOD), ("mix_pre", KT), ("mix_post", KT), ("ffn_pre", KT),
                  ("ffn_post", KT), ("conv_w", CT * CK), ("conv_b", CT), ("ln_g", CT), ("ln_b", CT),
                  ("norm2", 2 * KT), ("mconv_w", XT * MK), ("mconv_b", XT), ("m_norm", MT), ("m_d", MT),
                  ("kv_norm", KT), ("final", KT), ("b_f", 1), ("dt_bias", 1), ("a_log", 1)]:
    VEC[_name] = (NVEC, _n)
    NVEC += _n
CST = dict(ident=0, upper=1, neg_after=2, neg_from=3, ones=4)


def at(c, i):
    return c + 2 * i


def pairs(e, n, body):
    if n // 2 >= 2:
        with e.Fori(0, n // 2) as i:
            for u in range(2):
                body(i, u)
    else:
        for i in range(n // 2):
            for u in range(2):
                body(i, u)
    if n % 2:
        body(n // 2, 0)


def build(nc, x_in, panels, ada, vecs, cst, w_f, w_dt, x_kept, ac_rows, out):
    ctx = ExitStack()
    with ctx:
        def sem(name):
            return ctx.enter_context(nc.semaphore(name))

        def sbuf(scope, name, shape, dt=F32):
            return scope.enter_context(nc.sbuf_tensor(name, shape, dt))

        x = sbuf(ctx, "x", [P, KT, S])
        hhi = sbuf(ctx, "hhi", [P, KT, S], F32R)
        hlo = sbuf(ctx, "hlo", [P, KT, S], F32R)
        raw = sbuf(ctx, "raw", [P, 2, 16, P])
        whi = sbuf(ctx, "whi", [P, 2, 16, P], F32R)
        wlo = sbuf(ctx, "wlo", [P, 2, 16, P], F32R)
        ada_raw = sbuf(ctx, "ada_raw", [P, 2, KT, 256])
        ada_acc = sbuf(ctx, "ada_acc", [P, 2, 256])
        vec = sbuf(ctx, "vec", [P, NVEC])
        consts = sbuf(ctx, "consts", [P, 5, P])
        mod = sbuf(ctx, "mod", [P, NMOD])
        cs = sbuf(ctx, "cs", [P, 2, KT])
        coef = sbuf(ctx, "coef", [P, 3, KT])
        eps = sbuf(ctx, "eps", [P, 1])
        ps = ctx.enter_context(nc.psum_tensor("ps", [P, 8, S], F32))
        MODB = 4
        ident = consts[:, CST["ident"], :]
        ones = consts[:, CST["ones"], :]

        def v(name, i=None, n=None):
            a, w = VEC[name]
            if i is None:
                return vec[:, a:a + w]
            return vec[:, a + i:a + i + (n or 1)]

        def m(name, n=KT):
            return mod[:, MOD[name]:MOD[name] + n]

        w_landed = [sem("w_landed0"), sem("w_landed1")]
        hi_split = sem("hi_split")
        lo_split = sem("lo_split")
        panels_used = sem("panels_used")
        pair_free = [sem("pair_free0"), sem("pair_free1")]
        ada_landed = [sem("ada_landed0"), sem("ada_landed1")]
        ada_mul = sem("ada_mul")
        acc_ready = sem("acc_ready")
        mod_done = sem("mod_done")
        ada_chain = sem("ada_chain")
        sg_ready = sem("sg_ready")
        small_landed = sem("small_landed")
        setup = sem("setup")
        ws_ready = sem("ws_ready")
        small_done = sem("small_done")
        mod_read = sem("mod_read")

        def load_panel(e, c, i):
            if c + (0 if isinstance(i, int) else 0) >= 2 or not isinstance(i, int):
                e.wait_ge(lo_split, at(c - 1, i))
            e.dma_start(raw[:, c % 2, :, :].rearrange("p t n -> p (t n)"),
                        panels[at(c, i)]).then_inc(w_landed[c % 2], 16)

        def load_ada(e, c, i):
            if c >= 2:
                e.wait_ge(acc_ready, at(c - 1, i))
            e.dma_start(ada_raw[:, c % 2, :, :].rearrange("p k n -> p (k n)"),
                        ada[at(c, i)]).then_inc(ada_landed[c % 2], 16)

        def split_hi(e, c, i):
            e.wait_ge(w_landed[c % 2], (c // 2 + i + 1) * 16)
            if c >= 2 or not isinstance(i, int):
                e.wait_ge(panels_used, at(c - 1, i))
            e.activation(whi[:, c % 2, :, :], raw[:, c % 2, :, :], ACT.Copy).then_inc(hi_split, 1)

        def split_lo(e, c, i):
            e.wait_ge(hi_split, at(c + 1, i))
            e.tensor_tensor(wlo[:, c % 2, :, :], raw[:, c % 2, :, :], whi[:, c % 2, :, :].bitcast(F32),
                            ALU.subtract).then_inc(lo_split, 1)

        def ada_multiply(e, c, i):
            e.wait_ge(ada_landed[c % 2], (c // 2 + i + 1) * 16)
            which = 0 if c < ADA_C2 else 1
            e.tensor_tensor(ada_raw[:, c % 2, :, :], ada_raw[:, c % 2, :, :],
                            cs[:, which, :].unsqueeze(2).to_broadcast([P, KT, 256]),
                            ALU.mult).then_inc(ada_mul, 1)

        def ada_sum(e, c, i):
            e.wait_ge(ada_mul, at(c + 1 - ADA_FIRST, i))
            e.wait_ge(mod_done, at(c - 1, i))
            e.tensor_reduce(ada_acc[:, c % 2, :], ada_raw[:, c % 2, :, :].rearrange("p k n -> p n k"),
                            AX.X, ALU.add).then_inc(acc_ready, 1)

        def ada_columns(e, c, i):
            e.wait_ge(acc_ready, at(c + 1, i))
            for b in range(2):
                col = c * 2 + i * 4 + b
                mm = e.matmul(ps[:, MODB, col:col + 1] if isinstance(i, int) else ps[:, MODB, bass.ds(col, 1)],
                              ada_acc[:, c % 2, b * P:(b + 1) * P], ones[:, 0:1], start=True, stop=True)
            mm.then_inc(mod_done, 1)

        def read_mod(e, a0, a1):
            e.wait_ge(mod_done, a1)
            lo, hi = 2 * a0, 2 * a1
            e.tensor_tensor(mod[:, lo:hi], ps[:, MODB, lo:hi], v("ada_b")[:, lo:hi], ALU.add).then_inc(mod_read, 1)

        PASSES = ((whi, 0), (whi, 1), (wlo, 0))

        def in_panel(e, c, qc, i, src, by_token):
            e.wait_ge(lo_split, at(c + 1, i))
            e.wait_ge(pair_free[qc % 2], qc // 2 + 1 + i)
            for b in range(TB if by_token else 2):
                for k in range(KT):
                    for n, (w, part) in enumerate(PASSES):
                        flags = dict(start=(k == 0 and n == 0), stop=(k == KT - 1 and n == 2))
                        if by_token:
                            o = ps[:, 2 * (qc % 2) + b // 2, (b % 2) * 256:(b % 2) * 256 + 256]
                            mm = e.matmul(o, src[part][:, k, b * P:(b + 1) * P],
                                          w[:, c % 2, 2 * k:2 * k + 2, :], **flags)
                        else:
                            mm = e.matmul(ps[:, 2 * (qc % 2) + b, :], w[:, c % 2, 2 * k + b, :],
                                          src[part][:, k, :], **flags)
            mm.then_inc(panels_used, 1)

        def out_projection(e, name, parts, ready=None):
            c0, n = FIRST[name], COUNT[name]
            per = n // len(parts)

            def panel(c, i, src, k0, first, last):
                e.wait_ge(lo_split, at(c + 1, i))
                for k2 in range(2):
                    for b in range(8):
                        for j, (w, part) in enumerate(PASSES):
                            rhs = (src[part][:, k0 + k2, :] if isinstance(i, int) else
                                   src[part][:, bass.ds(k0 + k2 + i * 4, 1), :])
                            mm = e.matmul(ps[:, b, :], w[:, c % 2, k2 * 8 + b, :], rhs,
                                          start=(first and k2 == 0 and j == 0),
                                          stop=(last and k2 == 1 and j == 2), skip_group_check=True)
                mm.then_inc(panels_used, 1)

            for s, src in enumerate(parts):
                lo = 1 if s == 0 else 0
                hi = per - 1 if s == len(parts) - 1 else per
                base = c0 + s * per
                if s and ready:
                    e.wait_ge(*ready)
                if s == 0:
                    panel(base, 0, src, 0, True, False)
                mid = hi - lo
                if mid >= 4:
                    with e.Fori(0, mid // 2) as i:
                        for u in range(2):
                            panel(base + lo + u, i, src, 2 * (lo + u), False, False)
                    rest = range(lo + mid // 2 * 2, hi)
                else:
                    rest = range(lo, hi)
                for k in rest:
                    panel(base + k, 0, src, 2 * k, False, False)
                if s == len(parts) - 1:
                    panel(base + per - 1, 0, src, 2 * (per - 1), False, True)

        def stream(e, name, *, load=False, hi=False, lo=False, keep_last=0):
            c0, n = FIRST[name], COUNT[name]

            def step(i, u):
                if load:
                    load_panel(e, c0 + u + 4, i)
                if hi:
                    split_hi(e, c0 + u + 2, i)
                if lo:
                    split_lo(e, c0 + u + 2, i)
            ahead = 4 if load else 2
            whole = min(n, NPAN - ahead - c0)
            if whole == n:
                pairs(e, n - keep_last, step)
            else:
                for k in range(whole):
                    step(k // 2, k % 2)

        def out_block(name, parts):
            with nc.Block() as block:
                @block.sync
                def _(sp):
                    stream(sp, name, load=True, keep_last=1)

                @block.scalar
                def _(act):
                    act.activation(warm[:], ones[:, 0:1], ACT.Sqrt)
                    stream(act, name, hi=True, keep_last=1)

                @block.vector
                def _(dve):
                    stream(dve, name, lo=True, keep_last=1)

                @block.tensor
                def _(pe):
                    out_projection(pe, name, parts)

        nsem = {k: sem(k) for k in ("y_kept", "sq_ready", "ss_used", "std_ready", "rs_ready", "scaled", "x_new0", "x_new1", "h0_ready", "hi_ready", "lo_ready",
                                    "coef_ready", "out_ready", "out_stored")}
        done = {k: 0 for k in nsem}
        warm = sbuf(ctx, "warm", [P, 1])
        ORDER = [7, 6, 0, 1, 2, 3, 4, 5]

        def boundary(post, gate, targets, final=False, mods=None, room=None, panel=None, count=1, split=True):
            N = nsem
            normed = post not in (None, "none")
            fresh = post != "none"
            nt = len(targets)

            def n_(name, count):
                return N[name], base[name] + count
            base = dict(done)
            with ExitStack() as tmp:
                tag = base["coef_ready"] + base["sq_ready"]
                y = sbuf(tmp, f"y{tag}", [P, KT, S]) if normed or final else None
                if room is None:
                    room = sbuf(tmp, f"room{tag}", [P, 6, S])
                sq, h0, rs = room[:, 0:3, :], room[:, 3:5, :], room[:, 5, :]
                norms = ([0] if normed else []) + [1]
                bank_of = {0: 7, 1: 6}
                with nc.Block() as block:
                    if split and panel:
                        @block.sync
                        def _(sp):
                            load_panel(sp, panel[0] + 3, 0)

                    @block.scalar
                    def _(act):
                        for s in norms:
                            ssb = base["ss_used"] + (KT if s and normed else 0)
                            for j, k in enumerate(ORDER):
                                if s and fresh:
                                    act.wait_ge(*n_(f"x_new{j % 2}", j // 2 + 1))
                                if j >= 3 or ssb > base["ss_used"]:
                                    act.wait_ge(N["ss_used"], ssb + j - 2)
                                act.activation(sq[:, j % 3, :], x[:, k, :] if s else ps[:, k, :],
                                               ACT.Square).then_inc(N["sq_ready"], 1)
                            act.wait_ge(N["ss_used"], ssb + KT)
                            act.activation(rs, ps[:, bank_of[s], :], ACT.Sqrt, bias=eps[:, 0:1],
                                           scale=1.0 / D).then_inc(N["std_ready"], 1)
                            if s == norms[0] and panel and split:
                                split_hi(act, panel[0] + 1, 0)
                        for t, (gain, sc, sh, thi, tlo) in enumerate(targets):
                            for k in range(KT):
                                act.wait_ge(*n_("h0_ready", t * KT + k + 1))
                                act.activation(thi[:, k, :], h0[:, k % 2, :], ACT.Identity,
                                               bias=m(sh)[:, k:k + 1]).then_inc(N["hi_ready"], 1)

                    @block.tensor
                    def _(pe):
                        for s in norms:
                            bank = bank_of[s]
                            if normed and not s:
                                pe.wait_ge(*n_("y_kept", 1))
                            if normed and s:
                                pe.wait_ge(*n_("scaled", 2))
                            elif fresh and s:
                                pe.wait_ge(*n_("x_new1", 1))
                            for j in range(KT):
                                pe.wait_ge(*n_("sq_ready", (KT if s and normed else 0) + j + 1))
                                pe.matmul(ps[:, bank, :], ones, sq[:, j % 3, :], start=j == 0,
                                          stop=j == KT - 1).then_inc(N["ss_used"], 1)
                        if panel:
                            c, qc = panel
                            pe.wait_ge(pair_free[qc % 2], qc // 2 + 1)
                            pe.wait_ge(lo_split, c + 1)
                            if fresh:
                                for r in range(2):
                                    pe.wait_ge(*n_(f"x_new{r}", KT // 2))
                            thi, tlo = targets[0][3:]
                            for k in range(KT):
                                pe.wait_ge(*n_("lo_ready", k + 1))
                                for b in range(2):
                                    for n, (w, part) in enumerate(PASSES):
                                        mm = pe.matmul(ps[:, 2 * (qc % 2) + b, :], w[:, c % 2, 2 * k + b, :],
                                                       (thi, tlo)[part][:, k, :], start=(k == 0 and n == 0),
                                                       stop=(k == KT - 1 and n == 2), skip_group_check=True)
                            mm.then_inc(panels_used, 1)
                            for r in range(1, count):
                                in_panel(pe, c + r, qc + r, 0, (thi, tlo), False)

                    @block.vector
                    def _(dve):
                        if mods:
                            read_mod(dve, *mods)
                            dve.wait_ge(mod_read, read_counts[mods])
                        if normed:
                            dve.tensor_tensor(coef[:, 0, :], v(post), m(gate), ALU.mult).then_inc(N["coef_ready"], 1)
                        for t, (gain, sc, sh, thi, tlo) in enumerate(targets):
                            dve.scalar_tensor_tensor(out=coef[:, 1 + t, :], in0=m(sc), scalar=1.0, in1=gain,
                                                     op0=ALU.add, op1=ALU.mult).then_inc(N["coef_ready"], 1)
                        if normed:
                            dve.wait_ge(*n_("sq_ready", 1))
                            dve.tensor_copy(y[:, ORDER[0], :], ps[:, ORDER[0], :]).then_inc(N["y_kept"], 1)
                            dve.wait_ge(*n_("std_ready", 1))
                            dve.reciprocal(rs, rs).then_inc(N["rs_ready"], 1)
                            dve.wait_ge(*n_("rs_ready", 1))
                            dve.wait_ge(*n_("y_kept", 1))
                            dve.wait_ge(*n_("coef_ready", 1))
                            for j, k in enumerate(ORDER):
                                dve.scalar_tensor_tensor(out=y[:, k, :], in0=ps[:, k, :] if j else y[:, k, :],
                                                         scalar=coef[:, 0, k:k + 1], in1=rs, op0=ALU.mult,
                                                         op1=ALU.mult).then_inc(N["scaled"], 1)
                                if j % 2:
                                    dve.wait_ge(*n_("scaled", j + 1))
                                    dve.tensor_tensor(x[:, k, :], x[:, k, :], y[:, k, :],
                                                      ALU.add).then_inc(N["x_new1"], 1)
                        elif fresh:
                            for j, k in enumerate(ORDER):
                                dve.scalar_tensor_tensor(out=x[:, k, :], in0=ps[:, k, :], scalar=m(gate)[:, k:k + 1],
                                                         in1=x[:, k, :], op0=ALU.mult,
                                                         op1=ALU.add).then_inc(N[f"x_new{j % 2}"], 1)
                        if panel and split:
                            split_lo(dve, panel[0] + 1, 0)
                        if fresh:
                            for r in range(2):
                                dve.wait_ge(*n_(f"x_new{r}", KT // 2))
                        if normed:
                            dve.wait_ge(*n_("scaled", KT))
                        dve.wait_ge(*n_("std_ready", len(norms)))
                        dve.reciprocal(rs, rs).then_inc(N["rs_ready"], 1)
                        dve.wait_ge(*n_("rs_ready", len(norms)))
                        if final:
                            for k in range(KT):
                                dve.scalar_tensor_tensor(out=y[:, k, :], in0=x[:, k, :], scalar=v("final", k),
                                                         in1=rs, op0=ALU.mult,
                                                         op1=ALU.mult).then_inc(N["out_ready"], 1)
                        for t, (gain, sc, sh, thi, tlo) in enumerate(targets):
                            if not t:
                                dve.wait_ge(*n_("coef_ready", normed + nt))

                            def lo(k):
                                n = t * KT + k
                                dve.wait_ge(*n_("hi_ready", n + 1))
                                dve.scalar_tensor_tensor(out=tlo[:, k, :], in0=h0[:, k % 2, :],
                                                         scalar=m(sh)[:, k:k + 1], in1=thi[:, k, :].bitcast(F32),
                                                         op0=ALU.add, op1=ALU.subtract).then_inc(N["lo_ready"], 1)
                            for k in range(KT):
                                n = t * KT + k
                                if n >= 2:
                                    dve.wait_ge(*n_("lo_ready", n - 1))
                                dve.scalar_tensor_tensor(out=h0[:, k % 2, :], in0=x[:, k, :],
                                                         scalar=coef[:, 1 + t, k:k + 1], in1=rs,
                                                         op0=ALU.mult, op1=ALU.mult).then_inc(N["h0_ready"], 1)
                                if k:
                                    lo(k - 1)
                            lo(KT - 1)

                    if normed:
                        @block.gpsimd
                        def _(pool):
                            for j in range(0, KT, 2):
                                k = ORDER[j]
                                pool.wait_ge(*n_("scaled", j + 1))
                                pool.tensor_tensor(x[:, k, :], x[:, k, :], y[:, k, :],
                                                   ALU.add).then_inc(N["x_new0"], 1)

                    if final:
                        @block.sync
                        def _(sp):
                            for k in range(KT):
                                sp.wait_ge(*n_("out_ready", k + 1))
                                sp.dma_start(out[k], y[:, k, :]).then_inc(N["out_stored"], 16)
                            sp.wait_ge(N["out_stored"], 16 * KT)

            for name, n in (("y_kept", normed), ("sq_ready", KT * len(norms)), ("ss_used", KT * len(norms)),
                            ("std_ready", len(norms)), ("rs_ready", len(norms)), ("scaled", KT * normed), ("x_new0", KT // 2 * fresh),
                            ("x_new1", KT // 2 * fresh), ("h0_ready", KT * nt), ("hi_ready", KT * nt),
                            ("lo_ready", KT * nt), ("coef_ready", nt + normed)):
                done[name] += n

        read_counts = {(0, ADA_FIRST): 1, (10, 20): 2, (20, 42): 3, (42, 54): 4, (54, 56): 5}

        def split_small(dve, whi_s, wlo_s, raw_s, n, base):
            for w in (whi_s, wlo_s):
                dve.memset(w[:].bitcast(F32), 0.0).then_inc(ws_ready, 1)
            dve.wait_ge(ws_ready, base + 2)
            dve.tensor_copy(whi_s[:, :, 0:n], raw_s[:, :, 0:n]).then_inc(ws_ready, 1)
            dve.wait_ge(ws_ready, base + 3)
            dve.tensor_tensor(wlo_s[:, :, 0:n], raw_s[:, :, 0:n], whi_s[:, :, 0:n].bitcast(F32),
                              ALU.subtract).then_inc(ws_ready, 1)

        def small_projection(pe, whi_s, wlo_s, ready):
            pe.wait_ge(ws_ready, ready)
            for k in range(KT):
                for n, (w, part) in enumerate(((whi_s, hhi), (whi_s, hlo), (wlo_s, hhi))):
                    mm = pe.matmul(ps[:, 5, :], w[:, k, :], part[:, k, :], start=(k == 0 and n == 0),
                                   stop=(k == KT - 1 and n == 2))
            mm.then_inc(small_done, 1)

        sp_step = sem("sp_step")
        sp_exp = sem("sp_exp")

        def log1p_exp(dve, t, rows, bias, base, ready):
            r = slice(0, rows)
            n = [base]

            def then(ins):
                n[0] += 1
                ins.then_inc(sp_step, 1)
                dve.wait_ge(sp_step, n[0])
            dve.wait_ge(small_done, ready)
            then(dve.tensor_scalar(t[r, 0, :], ps[r, 5, :], bias, None, ALU.add))
            then(dve.tensor_scalar(t[r, 1, :], t[r, 0, :], -1.0, None, ALU.mult))
            then(dve.tensor_tensor(t[r, 2, :], t[r, 0, :], t[r, 1, :], ALU.min))
            dve.wait_ge(sp_exp, ready)
            then(dve.tensor_scalar(t[r, 2, :], t[r, 1, :], 2.0, None, ALU.add))
            then(dve.reciprocal(t[r, 3, :], t[r, 2, :]))
            then(dve.tensor_tensor(t[r, 1, :], t[r, 1, :], t[r, 3, :], ALU.mult))
            then(dve.tensor_tensor(t[r, 2, :], t[r, 1, :], t[r, 1, :], ALU.mult))
            then(dve.tensor_scalar(t[r, 3, :], t[r, 2, :], 1.0 / 17, None, ALU.mult))
            for k in range(7, 0, -1):
                then(dve.scalar_tensor_tensor(out=t[r, 3, :], in0=t[r, 3, :], scalar=1.0 / (2 * k + 1),
                                              in1=t[r, 2, :], op0=ALU.add, op1=ALU.mult))
            then(dve.scalar_tensor_tensor(out=t[r, 3, :], in0=t[r, 3, :], scalar=1.0, in1=t[r, 1, :],
                                          op0=ALU.add, op1=ALU.mult))
            then(dve.tensor_scalar(t[r, 1, :], t[r, 3, :], 2.0, None, ALU.mult))
            return n[0], then

        def small_exp(act, t, rows, step, use):
            act.wait_ge(sp_step, step)
            act.activation(t[0:rows, 1, :], t[0:rows, 2, :], ACT.Exp).then_inc(sp_exp, 1)

        with nc.Block() as block:
            @block.sync
            def _(sp):
                sp.dma_start(vec[:], vecs).then_inc(setup, 16)
                sp.dma_start(consts[:].rearrange("p a b -> p (a b)"), cst).then_inc(setup, 16)
                for c in range(2):
                    load_ada(sp, c, 0)
                sp.dma_start(x[:], x_in).then_inc(small_landed, 16)
                for c in range(2):
                    load_panel(sp, c, 0)
                for c in range(2, ADA_FIRST + 2):
                    load_ada(sp, c, 0)
                for c in range(2, 4):
                    load_panel(sp, c, 0)

            @block.scalar
            def _(act):
                act.wait_ge(setup, 32)
                act.activation(cs[:].rearrange("p a b -> p (a b)"), vec[:, 0:2 * KT], ACT.Silu).then_inc(ada_chain, 1)
                act.activation(warm[:], ones[:, 0:1], ACT.Sqrt)
                split_hi(act, 0, 0)
                split_hi(act, 1, 0)

            @block.vector
            def _(dve):
                dve.memset(eps[:], EPS).then_inc(pair_free[0], 1)
                dve.memset(coef[:], 0.0).then_inc(pair_free[1], 1)
                dve.wait_ge(ada_chain, 1)
                n = 1
                for c in range(ADA_FIRST):
                    dve.wait_ge(ada_landed[c % 2], 16 * (c // 2 + 1))
                    if c >= 2:
                        dve.wait_ge(mod_done, c - 1)
                    for k in range(KT):
                        if k == 0:
                            ins = dve.tensor_scalar(ada_acc[:, c % 2, :], ada_raw[:, c % 2, k, :], cs[:, 0, k:k + 1],
                                                    None, ALU.mult)
                        else:
                            dve.wait_ge(ada_chain, n)
                            ins = dve.scalar_tensor_tensor(out=ada_acc[:, c % 2, :], in0=ada_raw[:, c % 2, k, :],
                                                           scalar=cs[:, 0, k:k + 1], in1=ada_acc[:, c % 2, :],
                                                           op0=ALU.mult, op1=ALU.add)
                        if k < KT - 1:
                            ins.then_inc(ada_chain, 1)
                            n += 1
                        else:
                            ins.then_inc(acc_ready, 1)
                split_lo(dve, 0, 0)
                split_lo(dve, 1, 0)
                dve.wait_ge(small_landed, 16)

            @block.tensor
            def _(pe):
                pe.wait_ge(setup, 32)
                for c in range(ADA_FIRST):
                    ada_columns(pe, c, 0)

        boundary("none", None, [(v("mix_pre"), "sc1", "sh1", hhi, hlo)], mods=(0, ADA_FIRST),
                 panel=(0, 0), split=False)

        with ExitStack() as seg:
            qk = sbuf(seg, "qk", [P, 2 * CT, S])
            vt = sbuf(seg, "vt", [P, TB, AW])
            u = sbuf(seg, "u", [P, CT, CK - 1 + S])
            cv = sbuf(seg, "cv", [P, CT, S])
            ncum = sbuf(seg, "ncum", [H1, S])
            sg = sbuf(seg, "sg", [P, 2, S])
            conv_step = sem("conv_step")
            lf_ready = sem("lf_ready")
            pad_ready = sem("pad_ready")

            def conv_taps(dve, n0, n1):
                for n in range(n0, n1):
                    j, tap = n % CT, n // CT
                    w = v("conv_w", j * CK + tap)
                    src = u[:, j, tap:tap + S]
                    if tap == 0:
                        dve.tensor_scalar(cv[:, j, :], src, w, v("conv_b", j), ALU.mult,
                                          ALU.add).then_inc(conv_step, 1)
                    else:
                        dve.wait_ge(conv_step, n - CT + 1)
                        dve.scalar_tensor_tensor(out=cv[:, j, :], in0=src, scalar=w, in1=cv[:, j, :],
                                                 op0=ALU.mult, op1=ALU.add).then_inc(conv_step, 1)
            TAPS_EARLY = 54

            with ExitStack() as tmp:
                wf_raw = sbuf(tmp, "wf_raw", [P, KT, H1])
                wf_hi = sbuf(tmp, "wf_hi", [P, KT, P], F32R)
                wf_lo = sbuf(tmp, "wf_lo", [P, KT, P], F32R)
                ft = sbuf(tmp, "ft", [H1, 4, S])
                one_row = sbuf(tmp, "one_row", [H1, S])
                c0, q0, a0 = 0, 0, ADA_FIRST
                segs = [("conv", 4), ("q1", 2), ("k1", 2), ("v1", 2)]
                with nc.Block() as block:
                    @block.sync
                    def _(sp):
                        sp.dma_start(wf_raw[:].rearrange("p k n -> p (k n)"), w_f).then_inc(small_landed, 16)

                        def step(i, r):
                            load_panel(sp, c0 + r + 4, i)
                            load_ada(sp, a0 + r + 2, i)
                        pairs(sp, 10, step)

                    @block.gpsimd
                    def _(pool):
                        pairs(pool, 10, lambda i, r: ada_multiply(pool, a0 + r, i))

                    @block.scalar
                    def _(act):
                        at0 = 0
                        for name, n in segs:
                            def step(i, r, name=name, at0=at0):
                                c = at0 + r
                                pair = c % 2
                                act.wait_ge(panels_used, at(c + 1, i))
                                bank = ps[:, 2 * pair:2 * pair + 2, :]
                                if name == "conv":
                                    act.activation(sg[:, pair, :], ps[:, 2 * pair + 1, :],
                                                   ACT.Sigmoid).then_inc(sg_ready, 1)
                                elif name == "v1":
                                    act.activation(vt[:, :, r * 256:(r + 1) * 256],
                                                   bank.rearrange("p a (b c) -> p (a b) c", b=2),
                                                   ACT.Copy).then_inc(pair_free[pair], 1)
                                else:
                                    t = 2 * r + (CT if name == "k1" else 0)
                                    act.activation(qk[:, t:t + 2, :], bank, ACT.Copy,
                                                   scale=HD ** -0.5 if name == "q1" else 1.0
                                                   ).then_inc(pair_free[pair], 1)
                                split_hi(act, c + 2, i)
                            pairs(act, n, step)
                            at0 += n
                            if name == "conv":
                                small_exp(act, ft, H1, 3, 1)

                    @block.vector
                    def _(dve):
                        dve.memset(u[:, :, 0:CK - 1], 0.0).then_inc(pad_ready, 1)
                        dve.memset(one_row[:], 1.0).then_inc(pad_ready, 1)
                        dve.wait_ge(small_landed, 32)
                        split_small(dve, wf_hi, wf_lo, wf_raw, H1, 0)

                        def conv(i, r):
                            c = r
                            ada_sum(dve, a0 + c, i)
                            dve.wait_ge(sg_ready, at(c + 1, i))
                            j = r + i * 2
                            dst = u[:, j, CK - 1:] if isinstance(i, int) else u[:, bass.ds(j, 1), CK - 1:]
                            dve.tensor_tensor(dst, ps[:, 2 * r, :], sg[:, r, :], ALU.mult).then_inc(pair_free[r], 1)
                            split_lo(dve, c + 2, i)
                        pairs(dve, 4, conv)
                        last, then = log1p_exp(dve, ft, H1, v("b_f")[0:H1, :], 0, 1)
                        dve.tensor_scalar(ft[:, 2, :], ft[:, 0, :], 0.0, -1.0, ALU.min,
                                          ALU.mult).then_inc(lf_ready, 1)
                        dve.wait_ge(lf_ready, 1)
                        dve.tensor_tensor(ft[:, 3, :], ft[:, 2, :], ft[:, 1, :], ALU.add).then_inc(lf_ready, 1)
                        dve.wait_ge(lf_ready, 2)
                        dve.tensor_tensor_scan(ncum[:], one_row[:], ft[:, 3, :], 0.0, ALU.mult,
                                               ALU.add).then_inc(lf_ready, 1)
                        dve.wait_ge(pair_free[0], 3)
                        dve.wait_ge(pair_free[1], 3)
                        for k in range(4, 10):
                            ada_sum(dve, a0 + k, 0)
                            split_lo(dve, k + 2, 0)
                            conv_taps(dve, (k - 4) * TAPS_EARLY // 6, (k - 3) * TAPS_EARLY // 6)

                    @block.tensor
                    def _(pe):
                        def step(i, r, by_token=False):
                            in_panel(pe, 1 + r, 1 + r, i, (hhi, hlo), by_token)
                            ada_columns(pe, a0 + r, i)
                        pairs(pe, 3, step)
                        small_projection(pe, wf_hi, wf_lo, 4)
                        pairs(pe, 4, lambda i, r: step(i, 3 + r))
                        step(0, 7, True)
                        step(0, 8, True)
                        ada_columns(pe, a0 + 9, 0)

            NU = TB * H1
            with ExitStack() as tmp:
                pm = sbuf(tmp, "pm", [P, 2, S])
                pt = sbuf(tmp, "pt", [P, 2, S])
                mx = sbuf(tmp, "mx", [P, NU])
                nmx = sbuf(tmp, "nmx", [P, NU])
                rsum = sbuf(tmp, "rsum", [P, NU])
                rinv = sbuf(tmp, "rinv", [P, NU])
                o1 = sbuf(tmp, "o1", [P, 2, AW])
                lsq = sbuf(tmp, "lsq", [P, CT, S])
                lstd = sbuf(tmp, "lstd", [P, S])
                lrs = sbuf(tmp, "lrs", [P, S])
                A = {k: sem("a1_" + k) for k in ("s_done", "max", "nmax", "exp", "t_done", "pt_ready", "pv_done",
                                                 "rinv", "o_ready", "ot_done", "ohi", "olo", "mean", "centred",
                                                 "sq", "var", "std", "rstd", "scaled", "silu", "chi", "clo")}
                units = [(qb, h) for qb in range(TB) for h in range(H1)]
                with nc.Block() as block:
                    @block.tensor
                    def _(pe):
                        def logits(n):
                            qb, h = units[n]
                            nk = (qb + 1) * P
                            r0 = HD * (h % 2)
                            if n >= 2:
                                pe.wait_ge(A["exp"], n - 1)
                            o = ps[:, n % 2, 0:nk]
                            pe.matmul(o, qk[r0:r0 + HD, h // 2, qb * P:(qb + 1) * P],
                                      qk[r0:r0 + HD, CT + h // 2, 0:nk], start=True, stop=False)
                            pe.matmul(o, ident[0:H1, h:h + 1].to_broadcast([H1, P]), ncum[:, 0:nk],
                                      start=False, stop=False)
                            pe.matmul(ps[:, n % 2, qb * P:nk], ident, consts[:, CST["neg_after"], :],
                                      start=False, stop=True).then_inc(A["s_done"], 1)

                        def turn(n):
                            qb, h = units[n]
                            pe.wait_ge(A["exp"], n + 1)
                            if n >= 2:
                                pe.wait_ge(A["pt_ready"], n - 1)
                            for kb in range(qb + 1):
                                mm = pe.transpose(ps[:, 2 + n % 2, kb * P:(kb + 1) * P],
                                                  pm[:, n % 2, kb * P:(kb + 1) * P], ident)
                            mm.then_inc(A["t_done"], 1)

                        def values(n):
                            qb, h = units[n]
                            pe.wait_ge(A["pt_ready"], n + 1)
                            if h == 0 and qb >= 2:
                                pe.wait_ge(A["o_ready"], qb - 1)
                            for kb in range(qb + 1):
                                mm = pe.matmul(ps[:, 6 + qb % 2, h * HD:(h + 1) * HD],
                                               pt[:, n % 2, kb * P:(kb + 1) * P],
                                               vt[:, kb, h * HD:(h + 1) * HD], start=kb == 0, stop=kb == qb)
                            mm.then_inc(A["pv_done"], 1)

                        def turn_out(qb):
                            pe.wait_ge(A["o_ready"], qb + 1)
                            if qb:
                                pe.wait_ge(A["olo"], qb)
                            for t in range(CT):
                                mm = pe.transpose(ps[:, 5, t * P:(t + 1) * P], o1[:, qb % 2, t * P:(t + 1) * P],
                                                  ident)
                            mm.then_inc(A["ot_done"], 1)

                        for n in range(NU + 4):
                            if n < NU:
                                logits(n)
                            if 1 <= n <= NU:
                                turn(n - 1)
                            if 2 <= n <= NU + 1:
                                values(n - 2)
                            if n >= H1 + 3 and (n - 3) % H1 == 0:
                                turn_out((n - 3) // H1 - 1)
                        for j in range(CT):
                            pe.wait_ge(conv_step, CK * CT - CT + j + 1)
                            mm = pe.matmul(ps[:, 4, :], ones, cv[:, j, :], start=j == 0, stop=j == CT - 1)
                        mm.then_inc(A["mean"], 1)
                        for j in range(CT):
                            pe.wait_ge(A["sq"], j + 1)
                            mm = pe.matmul(ps[:, 0, :], ones, lsq[:, j, :], start=j == 0, stop=j == CT - 1)
                        mm.then_inc(A["var"], 1)

                    @block.scalar
                    def _(act):
                        def out_hi(qb):
                            act.wait_ge(A["ot_done"], qb + 1)
                            act.activation(hhi[:, 0:CT, qb * P:(qb + 1) * P],
                                           ps[:, 5, :].rearrange("p (t q) -> p t q", t=CT),
                                           ACT.Copy).then_inc(A["ohi"], 1)
                        for n, (qb, h) in enumerate(units):
                            nk = (qb + 1) * P
                            act.wait_ge(A["nmax"], n + 1)
                            if n >= 2:
                                act.wait_ge(A["t_done"], n - 1)
                            act.activation(pm[:, n % 2, 0:nk], ps[:, n % 2, 0:nk], ACT.Exp, bias=nmx[:, n:n + 1],
                                           accum_out=rsum[:, n:n + 1]).then_inc(A["exp"], 1)
                            if n >= H1 + 3 and (n - 3) % H1 == 0:
                                out_hi((n - 3) // H1 - 1)
                        out_hi(TB - 1)
                        for j in range(CT):
                            act.wait_ge(A["centred"], j + 1)
                            act.activation(lsq[:, j, :], cv[:, j, :], ACT.Square).then_inc(A["sq"], 1)
                        act.wait_ge(A["var"], 1)
                        act.activation(lstd[:], ps[:, 0, :], ACT.Sqrt, bias=eps[:, 0:1],
                                       scale=1.0 / AW).then_inc(A["std"], 1)
                        for j in range(CT):
                            act.wait_ge(A["scaled"], j + 1)
                            act.activation(lsq[:, j, :], cv[:, j, :], ACT.Silu,
                                           bias=v("ln_b", j)).then_inc(A["silu"], 1)

                    @block.vector
                    def _(dve):
                        read_mod(dve, 10, 20)

                        def neg_max(n):
                            qb, h = units[n]
                            dve.wait_ge(A["s_done"], n + 1)
                            dve.tensor_reduce(mx[:, n:n + 1], ps[:, n % 2, 0:(qb + 1) * P], AX.X,
                                              ALU.max).then_inc(A["max"], 1)
                            dve.wait_ge(A["max"], n + 1)
                            dve.tensor_scalar(nmx[:, n:n + 1], mx[:, n:n + 1], -1.0, None,
                                              ALU.mult).then_inc(A["nmax"], 1)

                        def take_pt(n):
                            qb, h = units[n]
                            dve.wait_ge(A["t_done"], n + 1)
                            if n >= 2:
                                dve.wait_ge(A["pv_done"], n - 1)
                            dve.tensor_copy(pt[:, n % 2, 0:(qb + 1) * P],
                                            ps[:, 2 + n % 2, 0:(qb + 1) * P]).then_inc(A["pt_ready"], 1)

                        def normalise(qb):
                            dve.wait_ge(A["pv_done"], H1 * (qb + 1))
                            cols = slice(H1 * qb, H1 * (qb + 1))
                            dve.reciprocal(rinv[:, cols], rsum[:, cols]).then_inc(A["rinv"], 1)
                            dve.wait_ge(A["rinv"], qb + 1)
                            if qb >= 2:
                                dve.wait_ge(A["ot_done"], qb - 1)
                            dve.tensor_tensor(o1[:, qb % 2, :].rearrange("p (h d) -> p h d", h=H1),
                                              ps[:, 6 + qb % 2, :].rearrange("p (h d) -> p h d", h=H1),
                                              rinv[:, cols].unsqueeze(2).to_broadcast([P, H1, HD]),
                                              ALU.mult).then_inc(A["o_ready"], 1)

                        def out_lo(qb):
                            dve.wait_ge(A["ohi"], qb + 1)
                            dve.tensor_tensor(hlo[:, 0:CT, qb * P:(qb + 1) * P],
                                              ps[:, 5, :].rearrange("p (t q) -> p t q", t=CT),
                                              hhi[:, 0:CT, qb * P:(qb + 1) * P].bitcast(F32),
                                              ALU.subtract).then_inc(A["olo"], 1)
                        taps = CK * CT - TAPS_EARLY
                        for n in range(NU + 4):
                            if n < NU:
                                neg_max(n)
                            if 1 <= n <= NU:
                                take_pt(n - 1)
                            if n >= H1 + 2 and (n - 2) % H1 == 0:
                                normalise((n - 2) // H1 - 1)
                            if n >= H1 + 4 and (n - 4) % H1 == 0:
                                out_lo((n - 4) // H1 - 1)
                            if n < NU:
                                conv_taps(dve, TAPS_EARLY + taps * n // NU, TAPS_EARLY + taps * (n + 1) // NU)
                        out_lo(TB - 1)
                        dve.wait_ge(A["mean"], 1)
                        for j in range(CT):
                            dve.scalar_tensor_tensor(out=cv[:, j, :], in0=ps[:, 4, :], scalar=-1.0 / AW,
                                                     in1=cv[:, j, :], op0=ALU.mult,
                                                     op1=ALU.add).then_inc(A["centred"], 1)
                        dve.wait_ge(A["std"], 1)
                        dve.reciprocal(lrs[:], lstd[:]).then_inc(A["rstd"], 1)
                        dve.wait_ge(A["rstd"], 1)
                        for j in range(CT):
                            dve.scalar_tensor_tensor(out=cv[:, j, :], in0=cv[:, j, :], scalar=v("ln_g", j),
                                                     in1=lrs[:], op0=ALU.mult,
                                                     op1=ALU.mult).then_inc(A["scaled"], 1)
                        for j in range(CT):
                            dve.wait_ge(A["silu"], j + 1)
                            dve.tensor_copy(hhi[:, CT + j, :], lsq[:, j, :]).then_inc(A["chi"], 1)
                            dve.wait_ge(A["chi"], j + 1)
                            dve.tensor_tensor(hlo[:, CT + j, :], lsq[:, j, :], hhi[:, CT + j, :].bitcast(F32),
                                              ALU.subtract).then_inc(A["clo"], 1)

            out_block("wo", [(hhi, hlo)])
        boundary("mix_post", "g1", [(v("ffn_pre"), "sc2", "sh2", hhi, hlo)], panel=(FIRST["ffn_in"], 10))

        with ExitStack() as seg:
            fhi = sbuf(seg, "fhi", [P, FT, S], F32R)
            flo = sbuf(seg, "flo", [P, FT, S], F32R)
            fg = sbuf(seg, "fg", [P, 2, S])
            g_ready = sem("g_ready")
            prod_ready = sem("prod_ready")
            fhi_ready = sem("fhi_ready")
            flo_ready = sem("flo_ready")
            c0, q0, a0 = FIRST["ffn_in"], 10, 20
            parts = [(0, ADA_C2 - a0), (ADA_C2 - a0, FT)]
            with nc.Block() as block:
                @block.sync
                def _(sp):
                    pairs(sp, FT, lambda i, r: (load_panel(sp, c0 + r + 4, i), load_ada(sp, a0 + r + 2, i)))

                @block.gpsimd
                def _(pool):
                    for lo, hi in parts:
                        pairs(pool, hi - lo, lambda i, r, lo=lo: ada_multiply(pool, a0 + lo + r, i))

                @block.scalar
                def _(act):
                    def step(i, r):
                        pair = (q0 + r) % 2
                        act.wait_ge(panels_used, at(c0 + r + 1, i))
                        act.activation(fg[:, pair, :], ps[:, 2 * pair, :], ACT.Silu).then_inc(g_ready, 1)
                        split_hi(act, c0 + r + 2, i)
                    pairs(act, FT, step)

                @block.vector
                def _(dve):
                    def step(i, r):
                        ada_sum(dve, a0 + r, i)
                        pair = (q0 + r) % 2
                        t = r + i * 2
                        dve.wait_ge(g_ready, at(r + 1, i))
                        dve.tensor_tensor(fg[:, pair, :], ps[:, 2 * pair + 1, :], fg[:, pair, :],
                                          ALU.mult).then_inc(prod_ready, 1)
                        dve.wait_ge(prod_ready, at(r + 1, i))
                        dve.tensor_copy(fhi[:, bass.ds(t, 1), :], fg[:, pair, :]).then_inc(fhi_ready, 1)
                        dve.wait_ge(fhi_ready, at(r + 1, i))
                        dve.tensor_tensor(flo[:, bass.ds(t, 1), :], fg[:, pair, :],
                                          fhi[:, bass.ds(t, 1), :].bitcast(F32),
                                          ALU.subtract).then_inc(pair_free[pair], 1)
                        split_lo(dve, c0 + r + 2, i)
                    pairs(dve, FT, step)
                    read_mod(dve, 20, 42)

                @block.tensor
                def _(pe):
                    pairs(pe, FT - 1, lambda i, r: (in_panel(pe, c0 + 1 + r, q0 + 1 + r, i, (hhi, hlo), False),
                                                    ada_columns(pe, a0 + r, i)))
                    ada_columns(pe, a0 + FT - 1, 0)
            out_block("ffn_out", [(fhi, flo)])
        boundary("ffn_post", "g2", [(v("norm2", 0, KT), "msc", "msh", hhi, hlo)], panel=(FIRST["xbc"], 32))

        with ExitStack() as seg:
            xbc = sbuf(seg, "xbc", [P, XT, S])
            dtT = sbuf(seg, "dtT", [MH, S])
            acT = sbuf(seg, "acT", [MH, S])
            state = sbuf(seg, "state", [P, MG, MI // MG])
            dt_seq = sem("dt_seq")
            x_stored = sem("x_stored")
            x_back = sem("x_back")
            G = {k: sem("g_" + k) for k in ("z", "gated", "sq", "ss", "std", "rs", "scaled", "hi", "lo")}
            c0, q0, a0 = FIRST["xbc"], 32, 42
            with ExitStack() as tmp:
                wd_raw = sbuf(tmp, "wd_raw", [P, KT, MH])
                wd_hi = sbuf(tmp, "wd_hi", [P, KT, P], F32R)
                wd_lo = sbuf(tmp, "wd_lo", [P, KT, P], F32R)
                dtt = sbuf(tmp, "dtt", [MH, 4, S])
                one_row = sbuf(tmp, "one_row2", [MH, S])
                aneg = sbuf(tmp, "aneg", [MH, 2])
                tap0 = sem("tap0")
                taps = sem("taps")
                xs_ready = sem("xs_ready")
                with nc.Block() as block:
                    @block.sync
                    def _(sp):
                        sp.dma_start(wd_raw[:].rearrange("p k n -> p (k n)"), w_dt).then_inc(small_landed, 16)
                        sp.dma_start(x_kept, x[:]).then_inc(x_stored, 16)
                        pairs(sp, XT // 2 - 2, lambda i, r: (load_panel(sp, c0 + r + 4, i),
                                                             load_ada(sp, a0 + r + 2, i)))
                        for r in range(2):
                            load_panel(sp, c0 + r + 4, XT // 4 - 1)

                    @block.gpsimd
                    def _(pool):
                        pairs(pool, XT // 2, lambda i, r: ada_multiply(pool, a0 + r, i))

                    @block.scalar
                    def _(act):
                        act.activation(aneg[:, 0:1], v("a_log")[0:MH, :], ACT.Exp).then_inc(dt_seq, 1)

                        def step(i, r):
                            pair = (q0 + r) % 2
                            act.wait_ge(panels_used, at(c0 + r + 1, i))
                            for b in range(2):
                                t = 2 * r + b + i * 4
                                bc = VEC["mconv_b"][0] + t
                                wc = VEC["mconv_w"][0] + t * MK + MK - 1
                                act.activation(xbc[:, bass.ds(t, 1), :], ps[:, 2 * pair + b, :], ACT.Identity,
                                               bias=vec[:, bass.ds(bc, 1)],
                                               scale=vec[:, bass.ds(wc, 1)]).then_inc(tap0, 1)
                            split_hi(act, c0 + r + 2, i)
                            act.wait_ge(taps, 6 * r + 6 + i * 12)
                            for half in (1, 0):
                                both = xbc[:, bass.ds(2 * r + i * 4, 2), half * 256:half * 256 + 256]
                                act.activation(both, both, ACT.Silu).then_inc(xs_ready, 1)
                        pairs(act, XT // 2, step)
                        small_exp(act, dtt, MH, 20, 2)

                    @block.vector
                    def _(dve):
                        dve.memset(one_row[:], 1.0).then_inc(pad_ready, 1)
                        dve.wait_ge(small_landed, 48)
                        split_small(dve, wd_hi, wd_lo, wd_raw, MH, 4)

                        def step(i, r):
                            ada_sum(dve, a0 + r, i)
                            pair = (q0 + r) % 2
                            for s in range(1, MK):
                                for b in range(2):
                                    t = 2 * r + b + i * 4
                                    wc = VEC["mconv_w"][0] + t * MK + MK - 1 - s
                                    if s == 1:
                                        dve.wait_ge(tap0, 2 * r + b + 1 + i * 4)
                                    else:
                                        dve.wait_ge(taps, 6 * r + (s - 1) * 2 + b - 1 + i * 12)
                                    ins = dve.scalar_tensor_tensor(
                                        out=xbc[:, bass.ds(t, 1), s:S], in0=ps[:, 2 * pair + b, 0:S - s],
                                        scalar=vec[:, bass.ds(wc, 1)], in1=xbc[:, bass.ds(t, 1), s:S],
                                        op0=ALU.mult, op1=ALU.add)
                                    ins.then_inc(taps, 1)
                            dve.wait_ge(taps, 6 * r + 6 + i * 12)
                            dve.sem_inc(pair_free[pair], 1)
                            split_lo(dve, c0 + r + 2, i)
                        pairs(dve, XT // 2, step)
                        read_mod(dve, 42, 54)
                        last, then = log1p_exp(dve, dtt, MH, v("dt_bias")[0:MH, :], 17, 2)
                        dve.tensor_scalar(dtt[:, 2, :], dtt[:, 0, :], 0.0, None, ALU.max).then_inc(dt_seq, 1)
                        dve.wait_ge(dt_seq, 2)
                        dve.tensor_tensor(dtT[:], dtt[:, 2, :], dtt[:, 1, :], ALU.add).then_inc(dt_seq, 1)
                        dve.tensor_scalar(aneg[:, 1:2], aneg[:, 0:1], -1.0, None, ALU.mult).then_inc(dt_seq, 1)
                        dve.wait_ge(dt_seq, 4)
                        dve.tensor_scalar(dtt[:, 3, :], dtT[:], aneg[:, 1:2], None, ALU.mult).then_inc(dt_seq, 1)
                        dve.wait_ge(dt_seq, 5)
                        for c in range(TB):
                            w = slice(c * P, (c + 1) * P)
                            dve.tensor_tensor_scan(acT[:, w], one_row[:, w], dtt[:, 3, w], 0.0, ALU.mult,
                                                   ALU.add).then_inc(dt_seq, 1)

                    @block.tensor
                    def _(pe):
                        small_projection(pe, wd_hi, wd_lo, 8)
                        pairs(pe, XT // 2 - 1,
                              lambda i, r: (in_panel(pe, c0 + 1 + r, q0 + 1 + r, i, (hhi, hlo), False),
                                            ada_columns(pe, a0 + r, i)))
                        ada_columns(pe, a0 + XT // 2 - 1, 0)

            GH = MH // MG
            HB = 4
            NB = MH // HB
            NN = TB * NB
            c0, q0 = FIRST["z"], 44
            QUARTERS = [range(2 * n, 2 * n + 2) if n < NB else range(n + NB, n + NB + 1) if n < 3 * NB else range(0)
                        for n in range(NN)]

            def taken_at(n):
                return [k // 4 for k in (QUARTERS[n - 1] if n > 0 else ()) if k % 4 == 3]

            def gate_part(e, g):
                z = x[:, 4 * g:4 * g + 4, :] if g < 2 else zb[:, 4 * g - 8:4 * g - 4, :]
                y = xbc[:, 4 * g:4 * g + 4, :]
                e.tensor_tensor(y, y, z, ALU.mult).then_inc(G["gated"], 1)

            def norm_part(dve, g):
                dve.wait_ge(G["std"], g + 1)
                dve.reciprocal(state[:, g, :], state[:, g, :]).then_inc(G["rs"], 1)
                dve.wait_ge(G["rs"], g + 1)
                for t in range(4 * g, 4 * g + 4):
                    dve.scalar_tensor_tensor(out=xbc[:, t, :], in0=xbc[:, t, :], scalar=v("m_norm", t),
                                             in1=state[:, g, :], op0=ALU.mult,
                                             op1=ALU.mult).then_inc(G["scaled"], 1)

            def lo_part(dve, g, y2=None):
                for t in range(4 * g, 4 * g + 4):
                    shi, slo = (hhi, hlo) if t < KT else y2
                    dve.wait_ge(G["hi"], t + 1)
                    dve.tensor_tensor(slo[:, t % KT, :], xbc[:, t, :], shi[:, t % KT, :].bitcast(F32),
                                      ALU.subtract).then_inc(G["lo"], 1)

            def hi_part(act, g, y2=None):
                for t in range(4 * g, 4 * g + 4):
                    act.wait_ge(G["scaled"], t + 1)
                    dst = hhi if t < KT else y2[0]
                    act.activation(dst[:, t % KT, :], xbc[:, t, :], ACT.Copy).then_inc(G["hi"], 1)

            with ExitStack() as tmp:
                zb = sbuf(tmp, "zb", [P, KT, S])
                xdt = ada_raw[:, 0, :, :].rearrange("p k n -> p (k n)").rearrange("p (h d) -> p h d", h=MH)
                xw = ada_raw[:, 1, :, :].rearrange("p k n -> p (k n)").rearrange("p (h d) -> p h d", h=MH)
                gsq = ada_raw[:, 1, :, :].rearrange("p k n -> p (k n)").rearrange("p (a s) -> p a s", a=4)
                btok = sbuf(tmp, "btok", [P, MG, MN])
                cb = sbuf(tmp, "cb", [P, MG, P])
                bc = sbuf(tmp, "bc", [P, 2, HB, P])
                seg_t = sbuf(tmp, "seg_t", [P, 2, HB, P])
                dec = sbuf(tmp, "dec", [P, 2, HB, P])
                ce = sbuf(tmp, "ce", [P, 2, HB, P])
                dtc = sbuf(tmp, "dtc", [P, TB, MH])
                acc_c = sbuf(tmp, "acc_c", [P, TB, MH])
                dend = sbuf(tmp, "dend", [P, TB, MH])
                wend = sbuf(tmp, "wend", [P, TB, MH])
                M = {k: sem("m_" + k) for k in ("cols", "cols_c", "wend0", "ends", "xdt", "xw", "bt", "btok",
                                                "cbm", "rows", "bc0", "bc1", "seg", "clip", "grow", "ce", "dec",
                                                "mat", "yd", "yskip", "st", "decay", "state")}

                with nc.Block() as block:
                    @block.sync
                    def _(sp):
                        sp.dma_start(ac_rows, acT[:]).then_inc(M["rows"], 16)
                        sp.wait_ge(M["rows"], 16)
                        sp.wait_ge(x_stored, 16)
                        for n in range(NN):
                            c, b = n // NB, n % NB
                            if n >= 2:
                                sp.wait_ge(M["clip"], n - 1)
                                if n - 2 >= NB:
                                    sp.wait_ge(M["grow"], n - 1 - NB)
                            sp.dma_start(bc[:, n % 2, :, :],
                                         ac_rows[b * HB:(b + 1) * HB, c * P:(c + 1) * P].unsqueeze(0)
                                         .to_broadcast([P, HB, P])).then_inc(M[f"bc{n % 2}"], 16)
                            for p in taken_at(n - 2):
                                load_panel(sp, c0 + p + 4, 0)

                    @block.tensor
                    def _(pe):
                        for c in range(TB):
                            w = slice(c * P, (c + 1) * P)
                            pe.transpose(ps[:, 4, c * MH:(c + 1) * MH], dtT[:, w], ident[0:MH, 0:MH])
                            pe.transpose(ps[:, 4, P + c * MH:P + (c + 1) * MH], acT[:, w], ident[0:MH, 0:MH])
                            mm = pe.matmul(ps[:, 4, 2 * P + c * MH:2 * P + (c + 1) * MH],
                                           acT[:, c * P + P - 1:(c + 1) * P].to_broadcast([MH, P]),
                                           ident[0:MH, 0:MH], start=True, stop=True)
                        mm.then_inc(M["cols"], 1)

                        def z_quarter(k):
                            p, b, k0 = k // 4, k // 2 % 2, 4 * (k % 2)
                            cp, qp = c0 + p, q0 + p
                            if k % 4 == 0:
                                pe.wait_ge(lo_split, cp + 1)
                                pe.wait_ge(pair_free[qp % 2], qp // 2 + 1)
                            for kt in range(k0, k0 + 4):
                                for j, (wt, part) in enumerate(PASSES):
                                    mm = pe.matmul(ps[:, 2 * (qp % 2) + b, :], wt[:, cp % 2, 2 * kt + b, :],
                                                   (hhi, hlo)[part][:, kt, :], start=(kt == 0 and j == 0),
                                                   stop=(kt == KT - 1 and j == 2))
                            if k % 4 == 3:
                                mm.then_inc(panels_used, 1)

                        def squares(g):
                            for t in range(4 * g, 4 * g + 4):
                                pe.wait_ge(G["sq"], t + 1)
                                pe.matmul(ps[:, 4 + g % 2, :], ones, gsq[:, t % 4, :], start=t % 4 == 0,
                                          stop=t % 4 == 3).then_inc(G["ss"], 1)

                        for c in range(TB):
                            w = slice(c * P, (c + 1) * P)
                            if c == 0:
                                pe.wait_ge(M["cols_c"], 3)
                            else:
                                pe.wait_ge(M["state"], MG * c)
                            for r in range(4):
                                if r >= 2:
                                    pe.wait_ge(M["xdt"], 4 * c + r - 1)
                                for j in range(4):
                                    mm = pe.transpose(ps[:, 4 + r % 2, j * P:(j + 1) * P], xbc[:, 4 * r + j, w],
                                                      ident)
                                mm.then_inc(M["bt"], 1)
                            if c < TB - 1:
                                pe.wait_ge(M["xdt"], 4 * c + 3)
                                for g in range(MG):
                                    mm = pe.transpose(ps[:, 4, g * P:(g + 1) * P], xbc[:, MT + g, w], ident)
                                mm.then_inc(M["bt"], 1)
                            pe.wait_ge(M["xdt"], 4 * c + 4)
                            for g in range(MG):
                                mm = pe.matmul(ps[:, 5, g * P:(g + 1) * P], xbc[:, MT + g, w],
                                               xbc[:, MT + MG + g, w], start=True, stop=True)
                            mm.then_inc(M["bt"], 1)
                            for g in range(MG):
                                gi = c * MG + g
                                for b in range(2):
                                    n = c * NB + g * 2 + b
                                    for k in QUARTERS[n]:
                                        z_quarter(k)
                                    pe.wait_ge(M["mat"], n + 1)
                                    if c:
                                        pe.wait_ge(M["ce"], n + 1 - NB)
                                    if b == 0 and gi >= 2:
                                        pe.wait_ge(M["yskip"], 4 * (gi - 1))
                                    for j in range(HB):
                                        hg = b * HB + j
                                        h = g * GH + hg
                                        o = HD * (h % 2)
                                        dst = ps[o:o + HD, 6 + gi % 2, hg // 2 * P:(hg // 2 + 1) * P]
                                        mm = pe.matmul(dst, xdt[:, h, :], dec[:, n % 2, j, :], start=True,
                                                       stop=c == 0)
                                        if c:
                                            mm = pe.matmul(dst, state[:, g, hg * HD:(hg + 1) * HD],
                                                           ce[:, n % 2, j, :], start=False, stop=True)
                                    mm.then_inc(M["yd"], 1)
                                if c == TB - 1 and g:
                                    squares(g - 1)
                            if c < TB - 1:
                                pe.wait_ge(M["xw"], c + 1)
                                pe.wait_ge(M["btok"], c + 1)
                                pe.wait_ge(M["cbm"], c + 1)
                                for g in range(MG):
                                    n = c * MG + g
                                    if g >= 2:
                                        pe.wait_ge(M["state"], n - 1)
                                    pe.matmul(ps[:, 4 + g % 2, :], btok[:, g, :],
                                              xw[:, g * GH:(g + 1) * GH, :], start=True,
                                              stop=True).then_inc(M["st"], 1)
                        squares(MG - 1)

                    @block.scalar
                    def _(act):
                        act.wait_ge(M["cols_c"], 3)
                        act.wait_ge(M["wend0"], 1)
                        act.activation(dend[:], dend[:], ACT.Exp).then_inc(M["ends"], 1)
                        act.activation(wend[:], wend[:], ACT.Exp).then_inc(M["ends"], 1)

                        def take_z(p):
                            pair = (q0 + p) % 2
                            act.wait_ge(panels_used, c0 + p + 1)
                            if p == 0:
                                act.wait_ge(M["bc0"], 16)
                            dst = x[:, 2 * p:2 * p + 2, :] if p < 4 else zb[:, 2 * p - 8:2 * p - 6, :]
                            act.activation(dst, ps[:, 2 * pair:2 * pair + 2, :],
                                           ACT.Silu).then_inc(pair_free[pair], 1)
                            split_hi(act, c0 + p + 2, 0)

                        def group_stats(g):
                            for t in range(4 * g, 4 * g + 4):
                                act.wait_ge(G["gated"], g + 1)
                                if t >= 4:
                                    act.wait_ge(G["ss"], t - 3)
                                act.activation(gsq[:, t % 4, :], xbc[:, t, :], ACT.Square).then_inc(G["sq"], 1)
                            act.wait_ge(G["ss"], 4 * g + 4)
                            act.activation(state[:, g, :], ps[:, 4 + g % 2, :], ACT.Sqrt, bias=eps[:, 0:1],
                                           scale=MG / MI).then_inc(G["std"], 1)

                        for c in range(TB):
                            if c < TB - 1:
                                act.wait_ge(M["bt"], 6 * c + 5)
                                if c:
                                    act.wait_ge(M["st"], MG * c)
                                act.activation(btok[:], ps[:, 4, :].rearrange("p (g t) -> p g t", g=MG),
                                               ACT.Copy).then_inc(M["btok"], 1)
                            for g in range(MG):
                                for b in range(2):
                                    n = c * NB + g * 2 + b
                                    if n >= 2:
                                        act.wait_ge(M["yd"], n - 1)
                                    if c:
                                        act.wait_ge(M[f"bc{n % 2}"], 16 * (n // 2 + 1))
                                        act.activation(ce[:, n % 2, :, :], bc[:, n % 2, :, :],
                                                       ACT.Exp).then_inc(M["grow"], 1)
                                    act.wait_ge(M["clip"], n + 1)
                                    act.activation(dec[:, n % 2, :, :], seg_t[:, n % 2, :, :],
                                                   ACT.Exp).then_inc(M["dec"], 1)
                                    for p in taken_at(n):
                                        take_z(p)
                                if c == TB - 1 and g:
                                    group_stats(g - 1)
                                if c == TB - 1 and g >= 2:
                                    hi_part(act, g - 2)
                        group_stats(MG - 1)

                    @block.gpsimd
                    def _(pool):
                        for n in range(NN):
                            c, b = n // NB, n % NB
                            pool.wait_ge(M["dec"], n + 1)
                            pool.wait_ge(M["cbm"], c + 1)
                            pool.tensor_tensor(dec[:, n % 2, :, :], dec[:, n % 2, :, :],
                                               cb[:, b // 2, :].unsqueeze(1).to_broadcast([P, HB, P]),
                                               ALU.mult).then_inc(M["mat"], 1)

                    @block.vector
                    def _(dve):
                        dve.wait_ge(M["cols"], 1)
                        for k, t in enumerate((dtc, acc_c, dend)):
                            dve.tensor_copy(t[:], ps[:, 4, k * P:(k + 1) * P].rearrange("p (c h) -> p c h", c=TB)
                                            ).then_inc(M["cols_c"], 1)
                        dve.wait_ge(M["cols_c"], 3)
                        dve.tensor_tensor(wend[:], dend[:], acc_c[:], ALU.subtract).then_inc(M["wend0"], 1)

                        def difference(n):
                            c, b = n // NB, n % NB
                            dve.wait_ge(M[f"bc{n % 2}"], 16 * (n // 2 + 1))
                            if n >= 2:
                                dve.wait_ge(M["dec"], n - 1)
                            dve.tensor_tensor(seg_t[:, n % 2, :, :], bc[:, n % 2, :, :],
                                              acc_c[:, c, b * HB:(b + 1) * HB].unsqueeze(2).to_broadcast([P, HB, P]),
                                              ALU.subtract).then_inc(M["seg"], 1)
                            dve.wait_ge(M["seg"], n + 1)
                            dve.tensor_scalar(seg_t[:, n % 2, :, :], seg_t[:, n % 2, :, :], 0.0, None,
                                              ALU.min).then_inc(M["clip"], 1)
                            if c:
                                dve.wait_ge(M["grow"], n + 1 - NB)
                                dve.tensor_tensor(ce[:, n % 2, :, :], ce[:, n % 2, :, :],
                                                  xbc[:, MT + MG + b // 2, c * P:(c + 1) * P].unsqueeze(1)
                                                  .to_broadcast([P, HB, P]), ALU.mult).then_inc(M["ce"], 1)

                        for c in range(TB):
                            w = slice(c * P, (c + 1) * P)
                            for r in range(4):
                                dve.wait_ge(M["bt"], 6 * c + r + 1)
                                if c:
                                    dve.wait_ge(M["yd"], NB * c)
                                    dve.wait_ge(M["xw"], c)
                                dve.tensor_tensor(xdt[:, 8 * r:8 * r + 8, :],
                                                  ps[:, 4 + r % 2, :].rearrange("p (h d) -> p h d", h=8),
                                                  dtc[:, c, 8 * r:8 * r + 8].unsqueeze(2).to_broadcast([P, 8, HD]),
                                                  ALU.mult).then_inc(M["xdt"], 1)
                            dve.wait_ge(M["bt"], 6 * c + (6 if c < TB - 1 else 5))
                            if c:
                                dve.wait_ge(M["mat"], NB * c)
                            dve.tensor_tensor(cb[:], ps[:, 5, :].rearrange("p (g t) -> p g t", g=MG),
                                              consts[:, CST["upper"], :].unsqueeze(1).to_broadcast([P, MG, P]),
                                              ALU.mult).then_inc(M["cbm"], 1)
                            difference(c * NB)
                            if c < TB - 1:
                                dve.wait_ge(M["xdt"], 4 * c + 4)
                                dve.wait_ge(M["ends"], 2)
                                if c:
                                    dve.wait_ge(M["st"], MG * c)
                                dve.tensor_tensor(xw[:], xdt[:],
                                                  wend[:, c, :].unsqueeze(2).to_broadcast([P, MH, HD]),
                                                  ALU.mult).then_inc(M["xw"], 1)
                            for g in range(MG):
                                gi = c * MG + g
                                for b in range(2):
                                    n = c * NB + g * 2 + b
                                    if n % NB < NB - 1:
                                        difference(n + 1)
                                    for p in taken_at(n):
                                        split_lo(dve, c0 + p + 2, 0)
                                dve.wait_ge(M["yd"], 2 * gi + 2)
                                for j in range(4):
                                    t = 4 * g + j
                                    dve.scalar_tensor_tensor(out=xbc[:, t, w], in0=xbc[:, t, w],
                                                             scalar=v("m_d", t),
                                                             in1=ps[:, 6 + gi % 2, j * P:(j + 1) * P],
                                                             op0=ALU.mult, op1=ALU.add).then_inc(M["yskip"], 1)
                                if c == TB - 1:
                                    dve.wait_ge(M["yskip"], 4 * gi + 4)
                                    for pair in range(2):
                                        dve.wait_ge(pair_free[pair], q0 // 2 + 2 + g)
                                    gate_part(dve, g)
                                    if g:
                                        norm_part(dve, g - 1)
                                    if g >= 2:
                                        lo_part(dve, g - 2)
                            if c < TB - 1:
                                for g in range(MG):
                                    n = c * MG + g
                                    dve.wait_ge(M["st"], n + 1)
                                    if c == 0:
                                        dve.tensor_copy(state[:, g, :], ps[:, 4 + g % 2, :]).then_inc(M["state"], 1)
                                    else:
                                        s3 = state[:, g, :].rearrange("p (h d) -> p h d", h=GH)
                                        dve.tensor_tensor(s3, s3, dend[:, c, g * GH:(g + 1) * GH].unsqueeze(2)
                                                          .to_broadcast([P, GH, HD]),
                                                          ALU.mult).then_inc(M["decay"], 1)
                                        dve.wait_ge(M["decay"], n - MG + 1)
                                        dve.tensor_tensor(state[:, g, :], state[:, g, :], ps[:, 4 + g % 2, :],
                                                          ALU.add).then_inc(M["state"], 1)

            y2 = (sbuf(seg, "y2hi", [P, KT, S], F32R), sbuf(seg, "y2lo", [P, KT, S], F32R))
            c0 = FIRST["m_out"]
            with nc.Block() as block:
                @block.sync
                def _(sp):
                    sp.dma_start(x[:], x_kept).then_inc(x_back, 16)
                    stream(sp, "m_out", load=True, keep_last=1)

                @block.scalar
                def _(act):
                    hi_part(act, 2, y2)
                    split_hi(act, c0 + 2, 0)
                    hi_part(act, 3, y2)
                    for k in range(1, MT // 2 - 1):
                        split_hi(act, c0 + k + 2, 0)

                @block.vector
                def _(dve):
                    norm_part(dve, 3)
                    lo_part(dve, 2, y2)
                    split_lo(dve, c0 + 2, 0)
                    lo_part(dve, 3, y2)
                    for k in range(1, MT // 2 - 1):
                        split_lo(dve, c0 + k + 2, 0)
                    dve.wait_ge(x_back, 16)

                @block.tensor
                def _(pe):
                    out_projection(pe, "m_out", [(hhi, hlo), y2], ready=(G["lo"], MT))

        with ExitStack() as seg:
            k2 = sbuf(seg, "k2", [P, KT, S])
            v2 = sbuf(seg, "v2", [P, TB, D])
            q2 = sbuf(seg, "q2", [P, KT, S])
            z2 = sbuf(seg, "z2", [P, KT, S])
            with ExitStack() as tmp:
                h2hi = sbuf(tmp, "h2hi", [P, KT, S], F32R)
                h2lo = sbuf(tmp, "h2lo", [P, KT, S], F32R)
                boundary(None, "mg", [(v("kv_norm"), "kvsc", "kvsh", hhi, hlo),
                                      (v("norm2", KT, KT), "ssc", "ssh", h2hi, h2lo)], room=z2,
                         panel=(FIRST["k2"], 52), count=2)
                c0, q0 = FIRST["k2"], 52
                segs = [("k2", False, (hhi, hlo)), ("v2", True, (hhi, hlo)), ("q2", False, (h2hi, h2lo)),
                        ("z2", False, (h2hi, h2lo))]
                with nc.Block() as block:
                    @block.sync
                    def _(sp):
                        for r in range(2):
                            load_ada(sp, NADA - 2 + r, 0)
                        stream(sp, "k2", load=True)
                        stream(sp, "v2", load=True)
                        stream(sp, "q2", load=True)
                        stream(sp, "z2", load=True)

                    @block.gpsimd
                    def _(pool):
                        for r in range(2):
                            ada_multiply(pool, NADA - 2 + r, 0)

                    @block.scalar
                    def _(act):
                        for s, (name, by_token, _) in enumerate(segs):
                            def step(i, r, s=s, name=name):
                                pair = (q0 + r) % 2
                                act.wait_ge(panels_used, at(c0 + 4 * s + r + 1, i))
                                bank = ps[:, 2 * pair:2 * pair + 2, :]
                                if name == "v2":
                                    act.activation(v2[:, :, bass.ds(r * 256 + i * 512, 256)],
                                                   bank.rearrange("p a (b c) -> p (a b) c", b=2),
                                                   ACT.Copy).then_inc(pair_free[pair], 1)
                                else:
                                    dst = {"k2": k2, "q2": q2, "z2": z2}[name]
                                    act.activation(dst[:, bass.ds(2 * r + i * 4, 2), :], bank,
                                                   ACT.Silu if name == "z2" else ACT.Copy,
                                                   scale=HD ** -0.5 if name == "q2" else 1.0
                                                   ).then_inc(pair_free[pair], 1)
                                if c0 + 4 * s + 4 + 2 <= NPAN:
                                    split_hi(act, c0 + 4 * s + r + 2, i)
                            pairs(act, 4, step)

                    @block.vector
                    def _(dve):
                        for r in range(2):
                            split_lo(dve, c0 + r + 2, 0)
                        for r in range(2):
                            ada_sum(dve, NADA - 2 + r, 0)
                        pairs(dve, 14, lambda i, r: split_lo(dve, c0 + r + 4, i))
                        read_mod(dve, NADA - 2, NADA)

                    @block.tensor
                    def _(pe):
                        for s, (_, by_token, src) in enumerate(segs):
                            if s == 1:
                                for r in range(2):
                                    ada_columns(pe, NADA - 2 + r, 0)
                            skip = 0 if s else 2
                            pairs(pe, 4 - skip, lambda i, r: in_panel(pe, c0 + 4 * s + skip + r,
                                                                      q0 + 4 * s + skip + r, i, src, by_token))

            NU = TB * H2
            with ExitStack() as tmp:
                sig = sbuf(tmp, "sig", [P, 2, S])
                keep = sbuf(tmp, "keep", [P, 2, S])
                rest = sbuf(tmp, "rest", [P, 2, S + 1])
                zero = sbuf(tmp, "zero", [P, S])
                am = sbuf(tmp, "am", [P, 2, S])
                amt = sbuf(tmp, "amt", [P, 2, S])
                o2 = sbuf(tmp, "o2", [P, 2, D])
                og = sbuf(tmp, "og", [P, 2, 4, P])
                B = {k: sem("b_" + k) for k in ("zero", "z_done", "sig", "keep", "rest", "am", "t_done", "amt",
                                                "pv_done", "o_ready", "ot_done", "og", "ohi", "olo")}
                units = [(qb, h) for qb in range(TB) for h in range(H2)]
                with nc.Block() as block:
                    @block.tensor
                    def _(pe):
                        def logits(n):
                            qb, h = units[n]
                            nk = (qb + 1) * P
                            r0 = HD * (h % 2)
                            if n >= 2:
                                pe.wait_ge(B["keep"], n - 1)
                            pe.matmul(ps[:, n % 2, 0:nk], q2[r0:r0 + HD, h // 2, qb * P:nk],
                                      k2[r0:r0 + HD, h // 2, 0:nk], start=True, stop=False)
                            pe.matmul(ps[:, n % 2, qb * P:nk], ident, consts[:, CST["neg_from"], :],
                                      start=False, stop=True).then_inc(B["z_done"], 1)

                        def turn(n):
                            qb, h = units[n]
                            pe.wait_ge(B["am"], n + 1)
                            if n >= 2:
                                pe.wait_ge(B["amt"], n - 1)
                            for kb in range(qb + 1):
                                mm = pe.transpose(ps[:, 2 + n % 2, kb * P:(kb + 1) * P],
                                                  am[:, n % 2, kb * P:(kb + 1) * P], ident)
                            mm.then_inc(B["t_done"], 1)

                        def values(n):
                            qb, h = units[n]
                            half = n // 8
                            pe.wait_ge(B["amt"], n + 1)
                            if n % 8 == 0 and half >= 2:
                                pe.wait_ge(B["o_ready"], half - 1)
                            for kb in range(qb + 1):
                                mm = pe.matmul(ps[:, 4 + half % 2, (h % 8) * HD:(h % 8 + 1) * HD],
                                               amt[:, n % 2, kb * P:(kb + 1) * P],
                                               v2[:, kb, h * HD:(h + 1) * HD], start=kb == 0, stop=kb == qb)
                            mm.then_inc(B["pv_done"], 1)

                        def turn_out(half):
                            pe.wait_ge(B["o_ready"], half + 1)
                            if half >= 2:
                                pe.wait_ge(B["og"], half - 1)
                            for t in range(4):
                                mm = pe.transpose(ps[:, 6 + half % 2, t * P:(t + 1) * P],
                                                  o2[:, half % 2, t * P:(t + 1) * P], ident)
                            mm.then_inc(B["ot_done"], 1)

                        for n in range(NU + 5):
                            if n < NU:
                                logits(n)
                            if 2 <= n <= NU + 1:
                                turn(n - 2)
                            if 3 <= n <= NU + 2:
                                values(n - 3)
                            if n >= 12 and (n - 4) % 8 == 0:
                                turn_out((n - 4) // 8 - 1)

                    @block.scalar
                    def _(act):
                        def take(n):
                            qb, h = units[n]
                            nk = (qb + 1) * P
                            act.wait_ge(B["t_done"], n + 1)
                            if n >= 2:
                                act.wait_ge(B["pv_done"], n - 1)
                            act.activation(amt[:, n % 2, 0:nk], ps[:, 2 + n % 2, 0:nk], ACT.Copy).then_inc(B["amt"], 1)

                        def out_take(half):
                            act.wait_ge(B["pv_done"], 8 * half + 8)
                            if half >= 2:
                                act.wait_ge(B["ot_done"], half - 1)
                            act.activation(o2[:, half % 2, 0:512], ps[:, 4 + half % 2, :],
                                           ACT.Copy).then_inc(B["o_ready"], 1)

                        def out_hi(half):
                            qb, t0 = half // 2, 4 * (half % 2)
                            act.wait_ge(B["og"], half + 1)
                            act.activation(hhi[:, t0:t0 + 4, qb * P:(qb + 1) * P], og[:, half % 2, :, :],
                                           ACT.Copy).then_inc(B["ohi"], 1)

                        for n in range(NU + 6):
                            if n < NU:
                                qb, h = units[n]
                                nk = (qb + 1) * P
                                act.wait_ge(B["z_done"], n + 1)
                                if n >= 2:
                                    act.wait_ge(B["am"], n - 1)
                                act.activation(sig[:, n % 2, 0:nk], ps[:, n % 2, 0:nk],
                                               ACT.Sigmoid).then_inc(B["sig"], 1)
                                act.activation(keep[:, n % 2, 0:nk], ps[:, n % 2, 0:nk], ACT.Sigmoid,
                                               scale=-1.0).then_inc(B["keep"], 1)
                            if 2 <= n <= NU + 1:
                                take(n - 2)
                            if n >= 11 and (n - 3) % 8 == 0:
                                out_take((n - 3) // 8 - 1)
                            if n >= 13 and (n - 5) % 8 == 0:
                                out_hi((n - 5) // 8 - 1)

                    @block.gpsimd
                    def _(pool):
                        for n, (qb, h) in enumerate(units):
                            nk = (qb + 1) * P
                            pool.wait_ge(B["rest"], n + 1)
                            if n >= 2:
                                pool.wait_ge(B["t_done"], n - 1)
                            pool.tensor_tensor(am[:, n % 2, 0:nk], sig[:, n % 2, 0:nk], rest[:, n % 2, 1:nk + 1],
                                               ALU.mult).then_inc(B["am"], 1)

                    @block.vector
                    def _(dve):
                        dve.memset(zero[:], 0.0).then_inc(B["zero"], 1)
                        dve.wait_ge(B["zero"], 1)

                        def out_gate(half):
                            qb, t0 = half // 2, 4 * (half % 2)
                            dve.wait_ge(B["ot_done"], half + 1)
                            if half >= 2:
                                dve.wait_ge(B["olo"], half - 1)
                            dve.tensor_tensor(og[:, half % 2, :, :],
                                              ps[:, 6 + half % 2, :].rearrange("p (t q) -> p t q", t=4),
                                              z2[:, t0:t0 + 4, qb * P:(qb + 1) * P], ALU.mult).then_inc(B["og"], 1)

                        def out_lo(half):
                            qb, t0 = half // 2, 4 * (half % 2)
                            dve.wait_ge(B["ohi"], half + 1)
                            dve.tensor_tensor(hlo[:, t0:t0 + 4, qb * P:(qb + 1) * P], og[:, half % 2, :, :],
                                              hhi[:, t0:t0 + 4, qb * P:(qb + 1) * P].bitcast(F32),
                                              ALU.subtract).then_inc(B["olo"], 1)
                        for n in range(NU + 7):
                            if n < NU:
                                qb, h = units[n]
                                nk = (qb + 1) * P
                                if n >= 2:
                                    dve.wait_ge(B["am"], n - 1)
                                dve.memset(rest[:, n % 2, nk:nk + 1], 1.0).then_inc(B["zero"], 1)
                                dve.wait_ge(B["keep"], n + 1)
                                dve.tensor_tensor_scan(rest[:, n % 2, 0:nk][:, ::-1], keep[:, n % 2, 0:nk][:, ::-1],
                                                       zero[:, 0:nk], 1.0, ALU.mult,
                                                       ALU.add).then_inc(B["rest"], 1)
                            if n >= 12 and (n - 4) % 8 == 0:
                                out_gate((n - 4) // 8 - 1)
                            if n >= 14 and (n - 6) % 8 == 0:
                                out_lo((n - 6) // 8 - 1)
            out_block("sb_out", [(hhi, hlo)])
        boundary(None, "sg", [], final=True)


def _tiles(a):
    return a.reshape(-1, P).T


def _in_panel(w):
    return w.reshape(KT, P, 2, P).transpose(1, 0, 2, 3).reshape(P, 2048)


def _in_panels(w):
    return [_in_panel(w[:, i:i + 256]) for i in range(0, w.shape[1], 256)]


def _paired_panels(a, b):
    return [_in_panel(np.concatenate([a[:, i:i + P], b[:, i:i + P]], 1)) for i in range(0, a.shape[1], P)]


def _out_panels(w):
    w = w.reshape(-1, 2, P, KT, P).transpose(0, 2, 1, 3, 4)
    return [p.reshape(P, 2048) for p in w]


def _padded(a):
    return np.concatenate([a, np.zeros(P - a.shape[0], a.dtype)])[:, None]


def kernel(**inputs):
    import concourse.bacc as bacc
    from concourse.bass_utils import run_bass_kernel_spmd

    g = {k: np.asarray(a) for k, a in inputs.items()}
    w_in = g["w_in"][0]
    w_ffn = g["w_ffn_in"][0]
    m_in = g["m_in_w_2"][0]
    sb_in = g["sb_in_w_2"][0]
    a3 = 3 * AW
    weights = (_paired_panels(w_in[:, a3 + H1:a3 + H1 + AW], w_in[:, a3 + H1 + AW:])
               + _in_panels(w_in[:, 0:a3])
               + _out_panels(g["w_o"][0])
               + _paired_panels(w_ffn[:, 0:DFF], w_ffn[:, DFF:])
               + _out_panels(g["w_ffn_out"][0])
               + _in_panels(m_in[:, MI:MI + XT * P])
               + _in_panels(m_in[:, 0:MI])
               + _out_panels(g["m_out_w_2"][0])
               + _in_panels(g["kv_w_2"])
               + _in_panels(sb_in)
               + _out_panels(g["sb_out_w_2"][0]))
    ada_w = np.concatenate([g["ada_w"][0], g["ada_w_2"][0], g["kv_ada_w_2"], g["ada_w_2"][1]], 1)
    ada_b = np.concatenate([g["ada_b"][0], g["ada_b_2"][0], g["kv_ada_b_2"], g["ada_b_2"][1]])
    ada = [ada_w[:, i:i + 256].reshape(KT, P, 256).transpose(1, 0, 2).reshape(P, 2048)
           for i in range(0, ada_w.shape[1], 256)]
    vectors = dict(
        c=_tiles(g["c"]), c2=_tiles(g["c_2"]), ada_b=_tiles(ada_b), mix_pre=_tiles(g["mix_pre_g"]),
        mix_post=_tiles(g["mix_post_g"]), ffn_pre=_tiles(g["ffn_pre_g"]), ffn_post=_tiles(g["ffn_post_g"]),
        conv_w=g["conv_w"][0].reshape(CK, CT, P).transpose(2, 1, 0).reshape(P, CT * CK),
        conv_b=_tiles(g["conv_b"]), ln_g=_tiles(g["conv_ln_g"]), ln_b=_tiles(g["conv_ln_b"]),
        norm2=_tiles(g["norm_g_2"]),
        mconv_w=g["m_conv_w_2"][0].reshape(MK, XT, P).transpose(2, 1, 0).reshape(P, XT * MK),
        mconv_b=_tiles(g["m_conv_b_2"]), m_norm=_tiles(g["m_norm_g_2"]),
        m_d=_tiles(np.repeat(g["m_d_2"][0], HD)), kv_norm=_tiles(g["kv_norm_g_2"]),
        final=_tiles(g["final_g_2"]), b_f=_padded(g["b_f"][0]), dt_bias=_padded(g["m_dt_bias_2"][0]),
        a_log=_padded(g["m_a_log_2"][0]))
    i = np.arange(P)
    shapes = np.stack([np.eye(P), i[:, None] <= i[None, :], (i[None, :] > i[:, None]) * NEG,
                       (i[None, :] >= i[:, None]) * NEG, np.ones((P, P))], 1).astype(np.float32)
    arrays = {
        "x_in": g["x"][0].T.reshape(KT, P, S).transpose(1, 0, 2),
        "panels": np.stack(weights),
        "ada": np.stack(ada),
        "vecs": np.concatenate([vectors[k] for k in VEC], 1),
        "cst": shapes.reshape(P, 5 * P),
        "w_f": w_in[:, a3:a3 + H1].reshape(KT, P, H1).transpose(1, 0, 2).reshape(P, KT * H1),
        "w_dt": m_in[:, MI + XT * P:].reshape(KT, P, MH).transpose(1, 0, 2).reshape(P, KT * MH),
    }
    arrays = {k: np.ascontiguousarray(a) for k, a in arrays.items()}
    nc = bacc.Bacc("TRN2", target_bir_lowering=False, num_devices=1, dynamic_dma_scratch_size=1024)
    args = [nc.dram_tensor(k, a.shape, mybir.dt.from_np(a.dtype), kind="ExternalInput").ap()
            for k, a in arrays.items()]
    out = nc.dram_tensor("out", (KT, P, S), F32, kind="ExternalOutput").ap()
    scratch = [nc.dram_tensor("x_kept", (P, KT, S), F32, kind="Internal").ap(),
               nc.dram_tensor("ac_rows", (MH, S), F32, kind="Internal").ap()]
    build(nc, *args, *scratch, out)
    r = run_bass_kernel_spmd(nc, [arrays], core_ids=[0])
    return r.results[0]["out"].reshape(D, S).T.reshape(1, S, D)
```

```python
from contextlib import ExitStack

import numpy as np

import concourse.bass as bass
from concourse import mybir

F32 = mybir.dt.float32
F32R = mybir.dt.float32r
ALU = mybir.AluOpType
ACT = mybir.ActivationFunctionType
AX = mybir.AxisListType

P = 128
S = 512
TB = S // P
D = 1024
KT = D // P
EPS = 1e-6
NEG = -1.0e30

AW = D // 2
HD = 64
H1 = AW // HD
CT = AW // P
CK = 31
DFF = 2816
FT = DFF // P

MI = 2 * D
MT = MI // P
MH = MI // HD
MG = 4
MN = 128
XT = (MI + 2 * MG * MN) // P
MK = 4

H2 = D // HD

SEGS = [("conv", CT), ("q1", AW // 256), ("k1", AW // 256), ("v1", AW // 256), ("wo", KT // 2),
        ("ffn_in", FT), ("ffn_out", FT // 2), ("xbc", XT // 2), ("z", MT // 2), ("m_out", MT // 2),
        ("k2", KT // 2), ("v2", KT // 2), ("q2", KT // 2), ("z2", KT // 2), ("sb_out", KT // 2)]
FIRST = {}
NPAN = 0
for _name, _n in SEGS:
    FIRST[_name] = NPAN
    NPAN += _n
COUNT = dict(SEGS)

MOD = dict(sh1=0, sc1=8, g1=16, sh2=24, sc2=32, g2=40, msh=48, msc=56, mg=64, kvsh=72, kvsc=80, ssh=88,
           ssc=96, sg=104)
NMOD = 112
NADA = NMOD // 2
ADA_C2 = 24
ADA_FIRST = 10
ADA_OWN = 8

VEC = {}
NVEC = 0
for _name, _n in [("c", KT), ("c2", KT), ("ada_b", NMOD), ("mix_pre", KT), ("mix_post", KT), ("ffn_pre", KT),
                  ("ffn_post", KT), ("conv_w", CT * CK), ("conv_b", CT), ("ln_g", CT), ("ln_b", CT),
                  ("norm2", 2 * KT), ("mconv_w", XT * MK), ("mconv_b", XT), ("m_norm", MT), ("m_d", MT),
                  ("kv_norm", KT), ("final", KT), ("b_f", 1), ("dt_bias", 1), ("a_log", 1)]:
    VEC[_name] = (NVEC, _n)
    NVEC += _n
CST = dict(ident=0, upper=1, neg_after=2, neg_from=3, ones=4)


def at(c, i):
    return c + 2 * i


def pairs(e, n, body):
    if n // 2 >= 2:
        with e.Fori(0, n // 2) as i:
            for u in range(2):
                body(i, u)
    else:
        for i in range(n // 2):
            for u in range(2):
                body(i, u)
    if n % 2:
        body(n // 2, 0)


def build(nc, x_in, panels, ada, vecs, cst, w_f, w_dt, x_kept, ac_rows, out):
    ctx = ExitStack()
    with ctx:
        def sem(name):
            return ctx.enter_context(nc.semaphore(name))

        def sbuf(scope, name, shape, dt=F32):
            return scope.enter_context(nc.sbuf_tensor(name, shape, dt))

        def shared_sbuf(scope, first, then):
            with nc.sbuf_tensor(*first) as tensor:
                pass
            return [tensor] + [sbuf(scope, *one) for one in then]

        x = sbuf(ctx, "x", [P, KT, S])
        hhi = sbuf(ctx, "hhi", [P, KT, S], F32R)
        hlo = sbuf(ctx, "hlo", [P, KT, S], F32R)
        raw = sbuf(ctx, "raw", [P, 2, 16, P])
        whi = sbuf(ctx, "whi", [P, 2, 16, P], F32R)
        wlo = sbuf(ctx, "wlo", [P, 2, 16, P], F32R)
        ada_raw = sbuf(ctx, "ada_raw", [P, 2, KT, 256])
        ada_acc = sbuf(ctx, "ada_acc", [P, 2, 256])
        vec = sbuf(ctx, "vec", [P, NVEC])
        consts = sbuf(ctx, "consts", [P, 5, P])
        mod = sbuf(ctx, "mod", [P, NMOD])
        cs = sbuf(ctx, "cs", [P, 2, KT])
        coef = sbuf(ctx, "coef", [P, 3, KT])
        eps = sbuf(ctx, "eps", [P, 1])
        exact = sbuf(ctx, "exact", [P, 4, P], F32R)
        ps = ctx.enter_context(nc.psum_tensor("ps", [P, 8, S], F32))
        MODB = 4
        ident = consts[:, CST["ident"], :]
        ones = consts[:, CST["ones"], :]
        ident_r = exact[:, CST["ident"], :]

        def v(name, i=None, n=None):
            a, w = VEC[name]
            if i is None:
                return vec[:, a:a + w]
            return vec[:, a + i:a + i + (n or 1)]

        def m(name, n=KT):
            return mod[:, MOD[name]:MOD[name] + n]

        w_landed = [sem("w_landed0"), sem("w_landed1")]
        hi_split = sem("hi_split")
        lo_split = sem("lo_split")
        panels_used = sem("panels_used")
        pair_free = [sem("pair_free0"), sem("pair_free1")]
        ada_landed = [sem("ada_landed0"), sem("ada_landed1")]
        ada_mul = sem("ada_mul")
        acc_ready = sem("acc_ready")
        mod_done = sem("mod_done")
        ada_chain = sem("ada_chain")
        sg_ready = sem("sg_ready")
        small_landed = sem("small_landed")
        setup = sem("setup")
        ws_ready = sem("ws_ready")
        small_done = sem("small_done")
        mod_read = sem("mod_read")

        def load_panel(e, c, i):
            if c + (0 if isinstance(i, int) else 0) >= 2 or not isinstance(i, int):
                e.wait_ge(lo_split, at(c - 1, i))
            e.dma_start(raw[:, c % 2, :, :].rearrange("p t n -> p (t n)"),
                        panels[at(c, i)]).then_inc(w_landed[c % 2], 16)

        def load_ada(e, c, i):
            if c >= ADA_OWN + 2:
                e.wait_ge(acc_ready, at(c - 1, i))
            e.dma_start(ada_raw[:, c % 2, :, :].rearrange("p k n -> p (k n)"),
                        ada[at(c, i)]).then_inc(ada_landed[c % 2], 16)

        def split_hi(e, c, i):
            e.wait_ge(w_landed[c % 2], (c // 2 + i + 1) * 16)
            if c >= 2 or not isinstance(i, int):
                e.wait_ge(panels_used, at(c - 1, i))
            e.activation(whi[:, c % 2, :, :], raw[:, c % 2, :, :], ACT.Copy).then_inc(hi_split, 1)

        def split_lo(e, c, i):
            e.wait_ge(hi_split, at(c + 1, i))
            e.tensor_tensor(wlo[:, c % 2, :, :], raw[:, c % 2, :, :], whi[:, c % 2, :, :].bitcast(F32),
                            ALU.subtract).then_inc(lo_split, 1)

        def ada_multiply(e, c, i):
            e.wait_ge(ada_landed[c % 2], (c // 2 + i + 1 - ADA_OWN // 2) * 16)
            which = 0 if c < ADA_C2 else 1
            e.tensor_tensor(ada_raw[:, c % 2, :, :], ada_raw[:, c % 2, :, :],
                            cs[:, which, :].unsqueeze(2).to_broadcast([P, KT, 256]),
                            ALU.mult).then_inc(ada_mul, 1)

        def ada_sum(e, c, i):
            e.wait_ge(ada_mul, at(c + 1 - ADA_FIRST, i))
            e.wait_ge(mod_done, at(c - 1, i))
            e.tensor_reduce(ada_acc[:, c % 2, :], ada_raw[:, c % 2, :, :].rearrange("p k n -> p n k"),
                            AX.X, ALU.add).then_inc(acc_ready, 1)

        def ada_columns(e, c, i):
            e.wait_ge(acc_ready, at(c + 1, i))
            for b in range(2):
                col = c * 2 + i * 4 + b
                mm = e.matmul(ps[:, MODB, col:col + 1] if isinstance(i, int) else ps[:, MODB, bass.ds(col, 1)],
                              ada_acc[:, c % 2, b * P:(b + 1) * P], ones[:, 0:1], start=True, stop=True)
            mm.then_inc(mod_done, 1)

        def read_mod(e, a0, a1):
            e.wait_ge(mod_done, a1)
            lo, hi = 2 * a0, 2 * a1
            e.tensor_tensor(mod[:, lo:hi], ps[:, MODB, lo:hi], v("ada_b")[:, lo:hi], ALU.add).then_inc(mod_read, 1)

        PASSES = ((whi, 0), (whi, 1), (wlo, 0))

        def in_panel(e, c, qc, i, src, by_token):
            e.wait_ge(lo_split, at(c + 1, i))
            e.wait_ge(pair_free[qc % 2], qc // 2 + 1 + i)
            for b in range(TB if by_token else 2):
                for k in range(KT):
                    for n, (w, part) in enumerate(PASSES):
                        flags = dict(start=(k == 0 and n == 0), stop=(k == KT - 1 and n == 2))
                        if by_token:
                            o = ps[:, 2 * (qc % 2) + b // 2, (b % 2) * 256:(b % 2) * 256 + 256]
                            mm = e.matmul(o, src[part][:, k, b * P:(b + 1) * P],
                                          w[:, c % 2, 2 * k:2 * k + 2, :], **flags)
                        else:
                            mm = e.matmul(ps[:, 2 * (qc % 2) + b, :], w[:, c % 2, 2 * k + b, :],
                                          src[part][:, k, :], **flags)
            mm.then_inc(panels_used, 1)

        def out_projection(e, name, parts, ready=None):
            c0, n = FIRST[name], COUNT[name]
            per = n // len(parts)

            def panel(c, i, src, k0, first, last):
                e.wait_ge(lo_split, at(c + 1, i))
                for k2 in range(2):
                    for b in range(8):
                        for j, (w, part) in enumerate(PASSES):
                            rhs = (src[part][:, k0 + k2, :] if isinstance(i, int) else
                                   src[part][:, bass.ds(k0 + k2 + i * 4, 1), :])
                            mm = e.matmul(ps[:, b, :], w[:, c % 2, k2 * 8 + b, :], rhs,
                                          start=(first and k2 == 0 and j == 0),
                                          stop=(last and k2 == 1 and j == 2), skip_group_check=True)
                mm.then_inc(panels_used, 1)

            for s, src in enumerate(parts):
                lo = 1 if s == 0 else 0
                hi = per - 1 if s == len(parts) - 1 else per
                base = c0 + s * per
                if s and ready:
                    e.wait_ge(*ready)
                if s == 0:
                    panel(base, 0, src, 0, True, False)
                mid = hi - lo
                if mid >= 4:
                    with e.Fori(0, mid // 2) as i:
                        for u in range(2):
                            panel(base + lo + u, i, src, 2 * (lo + u), False, False)
                    rest = range(lo + mid // 2 * 2, hi)
                else:
                    rest = range(lo, hi)
                for k in rest:
                    panel(base + k, 0, src, 2 * k, False, False)
                if s == len(parts) - 1:
                    panel(base + per - 1, 0, src, 2 * (per - 1), False, True)

        def stream(e, name, *, load=False, hi=False, lo=False, keep_last=0):
            c0, n = FIRST[name], COUNT[name]

            def step(i, u):
                if load:
                    load_panel(e, c0 + u + 4, i)
                if hi:
                    split_hi(e, c0 + u + 2, i)
                if lo:
                    split_lo(e, c0 + u + 2, i)
            ahead = 4 if load else 2
            whole = min(n, NPAN - ahead - c0)
            if whole == n:
                pairs(e, n - keep_last, step)
            else:
                for k in range(whole):
                    step(k // 2, k % 2)

        def out_block(name, parts):
            with nc.Block() as block:
                @block.sync
                def _(sp):
                    stream(sp, name, load=True, keep_last=1)

                @block.scalar
                def _(act):
                    act.activation(warm[:], ones[:, 0:1], ACT.Sqrt)
                    stream(act, name, hi=True, keep_last=1)

                @block.vector
                def _(dve):
                    stream(dve, name, lo=True, keep_last=1)

                @block.tensor
                def _(pe):
                    out_projection(pe, name, parts)

        nsem = {k: sem(k) for k in ("y_kept", "sq_ready", "ss_used", "std_ready", "rs_ready", "scaled", "x_new0", "x_new1", "h0_ready", "hi_ready", "lo_ready",
                                    "coef_ready", "out_ready", "out_stored")}
        done = {k: 0 for k in nsem}
        warm = sbuf(ctx, "warm", [P, 1])
        ORDER = [7, 6, 0, 1, 2, 3, 4, 5]

        def boundary(post, gate, targets, final=False, mods=None, room=None, panel=None, count=1, split=True,
                     given=None):
            N = nsem
            normed = post not in (None, "none")
            fresh = post != "none"
            nt = len(targets)

            def n_(name, count):
                return N[name], base[name] + count
            base = dict(done)
            with ExitStack() as tmp:
                tag = base["coef_ready"] + base["sq_ready"]
                y = sbuf(tmp, f"y{tag}", [P, KT, S]) if normed or final else None
                if given is not None:
                    room = sbuf(tmp, f"room{tag}", [P, 5, S])
                elif room is None:
                    room = sbuf(tmp, f"room{tag}", [P, 6, S])
                sq, h0 = room[:, 0:3, :], room[:, 3:5, :]
                rs = room[:, 5, :] if given is None else given
                norms = [] if given is not None else ([0] if normed else []) + [1]
                bank_of = {0: 7, 1: 6}
                with nc.Block() as block:
                    if split and panel:
                        @block.sync
                        def _(sp):
                            load_panel(sp, panel[0] + 3, 0)

                    @block.scalar
                    def _(act):
                        for s in norms:
                            ssb = base["ss_used"] + (KT if s and normed else 0)
                            for j, k in enumerate(ORDER):
                                if s and fresh:
                                    act.wait_ge(*n_(f"x_new{j % 2}", j // 2 + 1))
                                if j >= 3 or ssb > base["ss_used"]:
                                    act.wait_ge(N["ss_used"], ssb + j - 2)
                                act.activation(sq[:, j % 3, :], x[:, k, :] if s else ps[:, k, :],
                                               ACT.Square).then_inc(N["sq_ready"], 1)
                            act.wait_ge(N["ss_used"], ssb + KT)
                            act.activation(rs, ps[:, bank_of[s], :], ACT.Sqrt, bias=eps[:, 0:1],
                                           scale=1.0 / D).then_inc(N["std_ready"], 1)
                            if s == norms[0] and panel and split:
                                split_hi(act, panel[0] + 1, 0)
                        for t, (gain, sc, sh, thi, tlo) in enumerate(targets):
                            for k in range(KT):
                                act.wait_ge(*n_("h0_ready", t * KT + k + 1))
                                act.activation(thi[:, k, :], h0[:, k % 2, :], ACT.Identity,
                                               bias=m(sh)[:, k:k + 1]).then_inc(N["hi_ready"], 1)

                    @block.tensor
                    def _(pe):
                        for s in norms:
                            bank = bank_of[s]
                            if normed and not s:
                                pe.wait_ge(*n_("y_kept", 1))
                            if normed and s:
                                pe.wait_ge(*n_("scaled", 2))
                            elif fresh and s:
                                pe.wait_ge(*n_("x_new1", 1))
                            for j in range(KT):
                                pe.wait_ge(*n_("sq_ready", (KT if s and normed else 0) + j + 1))
                                pe.matmul(ps[:, bank, :], ones, sq[:, j % 3, :], start=j == 0,
                                          stop=j == KT - 1).then_inc(N["ss_used"], 1)
                        if panel:
                            c, qc = panel
                            pe.wait_ge(pair_free[qc % 2], qc // 2 + 1)
                            pe.wait_ge(lo_split, c + 1)
                            if fresh:
                                for r in range(2):
                                    pe.wait_ge(*n_(f"x_new{r}", KT // 2))
                            thi, tlo = targets[0][3:]
                            for k in range(KT):
                                pe.wait_ge(*n_("lo_ready", k + 1))
                                for b in range(2):
                                    for n, (w, part) in enumerate(PASSES):
                                        mm = pe.matmul(ps[:, 2 * (qc % 2) + b, :], w[:, c % 2, 2 * k + b, :],
                                                       (thi, tlo)[part][:, k, :], start=(k == 0 and n == 0),
                                                       stop=(k == KT - 1 and n == 2), skip_group_check=True)
                            mm.then_inc(panels_used, 1)
                            for r in range(1, count):
                                in_panel(pe, c + r, qc + r, 0, (thi, tlo), False)

                    @block.vector
                    def _(dve):
                        if mods:
                            read_mod(dve, *mods)
                            dve.wait_ge(mod_read, read_counts[mods])
                        if normed:
                            dve.tensor_tensor(coef[:, 0, :], v(post), m(gate), ALU.mult).then_inc(N["coef_ready"], 1)
                        for t, (gain, sc, sh, thi, tlo) in enumerate(targets):
                            dve.scalar_tensor_tensor(out=coef[:, 1 + t, :], in0=m(sc), scalar=1.0, in1=gain,
                                                     op0=ALU.add, op1=ALU.mult).then_inc(N["coef_ready"], 1)
                        if normed:
                            dve.wait_ge(*n_("sq_ready", 1))
                            dve.tensor_copy(y[:, ORDER[0], :], ps[:, ORDER[0], :]).then_inc(N["y_kept"], 1)
                            dve.wait_ge(*n_("std_ready", 1))
                            dve.reciprocal(rs, rs).then_inc(N["rs_ready"], 1)
                            dve.wait_ge(*n_("rs_ready", 1))
                            dve.wait_ge(*n_("y_kept", 1))
                            dve.wait_ge(*n_("coef_ready", 1))
                            for j, k in enumerate(ORDER):
                                dve.scalar_tensor_tensor(out=y[:, k, :], in0=ps[:, k, :] if j else y[:, k, :],
                                                         scalar=coef[:, 0, k:k + 1], in1=rs, op0=ALU.mult,
                                                         op1=ALU.mult).then_inc(N["scaled"], 1)
                                if j % 2:
                                    dve.wait_ge(*n_("scaled", j + 1))
                                    dve.tensor_tensor(x[:, k, :], x[:, k, :], y[:, k, :],
                                                      ALU.add).then_inc(N["x_new1"], 1)
                        elif fresh:
                            for j, k in enumerate(ORDER):
                                dve.scalar_tensor_tensor(out=x[:, k, :], in0=ps[:, k, :], scalar=m(gate)[:, k:k + 1],
                                                         in1=x[:, k, :], op0=ALU.mult,
                                                         op1=ALU.add).then_inc(N[f"x_new{j % 2}"], 1)
                        if panel and split:
                            split_lo(dve, panel[0] + 1, 0)
                        if fresh:
                            for r in range(2):
                                dve.wait_ge(*n_(f"x_new{r}", KT // 2))
                        if normed:
                            dve.wait_ge(*n_("scaled", KT))
                        if norms:
                            dve.wait_ge(*n_("std_ready", len(norms)))
                            dve.reciprocal(rs, rs).then_inc(N["rs_ready"], 1)
                            dve.wait_ge(*n_("rs_ready", len(norms)))
                        if final:
                            for k in range(KT):
                                dve.scalar_tensor_tensor(out=y[:, k, :], in0=x[:, k, :], scalar=v("final", k),
                                                         in1=rs, op0=ALU.mult,
                                                         op1=ALU.mult).then_inc(N["out_ready"], 1)
                        for t, (gain, sc, sh, thi, tlo) in enumerate(targets):
                            if not t:
                                dve.wait_ge(*n_("coef_ready", normed + nt))

                            def lo(k):
                                n = t * KT + k
                                dve.wait_ge(*n_("hi_ready", n + 1))
                                dve.scalar_tensor_tensor(out=tlo[:, k, :], in0=h0[:, k % 2, :],
                                                         scalar=m(sh)[:, k:k + 1], in1=thi[:, k, :].bitcast(F32),
                                                         op0=ALU.add, op1=ALU.subtract).then_inc(N["lo_ready"], 1)
                            for k in range(KT):
                                n = t * KT + k
                                if n >= 2:
                                    dve.wait_ge(*n_("lo_ready", n - 1))
                                dve.scalar_tensor_tensor(out=h0[:, k % 2, :], in0=x[:, k, :],
                                                         scalar=coef[:, 1 + t, k:k + 1], in1=rs,
                                                         op0=ALU.mult, op1=ALU.mult).then_inc(N["h0_ready"], 1)
                                if k:
                                    lo(k - 1)
                            lo(KT - 1)

                    if normed:
                        @block.gpsimd
                        def _(pool):
                            for j in range(0, KT, 2):
                                k = ORDER[j]
                                pool.wait_ge(*n_("scaled", j + 1))
                                pool.tensor_tensor(x[:, k, :], x[:, k, :], y[:, k, :],
                                                   ALU.add).then_inc(N["x_new0"], 1)

                    if final:
                        @block.sync
                        def _(sp):
                            for k in range(KT):
                                sp.wait_ge(*n_("out_ready", k + 1))
                                sp.dma_start(out[k], y[:, k, :]).then_inc(N["out_stored"], 16)
                            sp.wait_ge(N["out_stored"], 16 * KT)

            for name, n in (("y_kept", normed), ("sq_ready", KT * len(norms)), ("ss_used", KT * len(norms)),
                            ("std_ready", len(norms)), ("rs_ready", len(norms)), ("scaled", KT * normed), ("x_new0", KT // 2 * fresh),
                            ("x_new1", KT // 2 * fresh), ("h0_ready", KT * nt), ("hi_ready", KT * nt),
                            ("lo_ready", KT * nt), ("coef_ready", nt + normed)):
                done[name] += n

        read_counts = {(0, ADA_FIRST): 1, (10, 20): 2, (20, 42): 3, (42, 54): 4, (54, 56): 5}

        def split_small(dve, whi_s, wlo_s, raw_s, n, base):
            for w in (whi_s, wlo_s):
                dve.memset(w[:].bitcast(F32), 0.0).then_inc(ws_ready, 1)
            dve.wait_ge(ws_ready, base + 2)
            dve.tensor_copy(whi_s[:, :, 0:n], raw_s[:, :, 0:n]).then_inc(ws_ready, 1)
            dve.wait_ge(ws_ready, base + 3)
            dve.tensor_tensor(wlo_s[:, :, 0:n], raw_s[:, :, 0:n], whi_s[:, :, 0:n].bitcast(F32),
                              ALU.subtract).then_inc(ws_ready, 1)

        def small_projection(pe, whi_s, wlo_s, ready):
            pe.wait_ge(ws_ready, ready)
            for k in range(KT):
                for n, (w, part) in enumerate(((whi_s, hhi), (whi_s, hlo), (wlo_s, hhi))):
                    mm = pe.matmul(ps[:, 5, :], w[:, k, :], part[:, k, :], start=(k == 0 and n == 0),
                                   stop=(k == KT - 1 and n == 2))
            mm.then_inc(small_done, 1)

        sp_step = sem("sp_step")
        sp_exp = sem("sp_exp")

        def log1p_exp(dve, t, rows, bias, base, ready, by_chunk=False):
            r = slice(0, rows)
            n = [base]

            def then(ins):
                n[0] += 1
                ins.then_inc(sp_step, 1)
                dve.wait_ge(sp_step, n[0])
            dve.wait_ge(small_done, ready)
            if by_chunk:
                for c in range(TB):
                    w = P // TB
                    then(dve.tensor_copy(t[c * w:(c + 1) * w, 3, :], ps[0:w, 5, c * P:(c + 1) * P]))
            then(dve.tensor_scalar(t[r, 0, :], t[r, 3, :] if by_chunk else ps[r, 5, :], bias, None, ALU.add))
            then(dve.tensor_scalar(t[r, 1, :], t[r, 0, :], -1.0, None, ALU.mult))
            then(dve.tensor_tensor(t[r, 2, :], t[r, 0, :], t[r, 1, :], ALU.min))
            dve.wait_ge(sp_exp, ready)
            then(dve.tensor_scalar(t[r, 2, :], t[r, 1, :], 2.0, None, ALU.add))
            then(dve.reciprocal(t[r, 3, :], t[r, 2, :]))
            then(dve.tensor_tensor(t[r, 1, :], t[r, 1, :], t[r, 3, :], ALU.mult))
            then(dve.tensor_tensor(t[r, 2, :], t[r, 1, :], t[r, 1, :], ALU.mult))
            then(dve.tensor_scalar(t[r, 3, :], t[r, 2, :], 1.0 / 17, None, ALU.mult))
            for k in range(7, 0, -1):
                then(dve.scalar_tensor_tensor(out=t[r, 3, :], in0=t[r, 3, :], scalar=1.0 / (2 * k + 1),
                                              in1=t[r, 2, :], op0=ALU.add, op1=ALU.mult))
            then(dve.scalar_tensor_tensor(out=t[r, 3, :], in0=t[r, 3, :], scalar=1.0, in1=t[r, 1, :],
                                          op0=ALU.add, op1=ALU.mult))
            then(dve.tensor_scalar(t[r, 1, :], t[r, 3, :], 2.0, None, ALU.mult))
            return n[0], then

        def small_exp(act, t, rows, step, use):
            act.wait_ge(sp_step, step)
            act.activation(t[0:rows, 1, :], t[0:rows, 2, :], ACT.Exp).then_inc(sp_exp, 1)

        with ExitStack() as seg:
            first = sbuf(seg, "first", [P, ADA_OWN, KT, 256])
            xsq = sbuf(seg, "xsq", [P, 3, S])
            rs0 = sbuf(seg, "rs0", [P, S])
            BY = "PDPDPDPDPD"
            first_mul = sem("first_mul")
            first_acc = sem("first_acc")
            first_landed = [sem(f"first_landed{c}") for c in range(ADA_OWN)]
            x_landed = sem("x_landed")

            def landing(c):
                return first[:, c, :, :] if c < ADA_OWN else ada_raw[:, c % 2, :, :]

            def landed(c):
                return (first_landed[c], 16) if c < ADA_OWN else (ada_landed[c % 2], 16)

            xsq_ready = sem("xsq_ready")
            xss = sem("xss")
            x_std = sem("x_std")
            x_rs = sem("x_rs")
            with nc.Block() as block:
                @block.sync
                def _(sp):
                    sp.dma_start(vec[:], vecs).then_inc(setup, 16)
                    sp.dma_start(consts[:].rearrange("p a b -> p (a b)"), cst).then_inc(setup, 16)
                    for c in range(ADA_OWN):
                        sp.dma_start(first[:, c, :, :].rearrange("p k n -> p (k n)"),
                                     ada[c]).then_inc(first_landed[c], 16)
                        if c == 0:
                            sp.dma_start(x[:], x_in).then_inc(x_landed, 16)
                        if c >= ADA_OWN - 2:
                            load_panel(sp, c - ADA_OWN + 2, 0)
                    for c in range(2):
                        load_ada(sp, ADA_OWN + c, 0)
                    for c in range(2):
                        load_ada(sp, ADA_FIRST + c, 0)
                    for c in range(2, 4):
                        load_panel(sp, c, 0)

                @block.scalar
                def _(act):
                    act.wait_ge(setup, 32)
                    act.activation(cs[:].rearrange("p a b -> p (a b)"), vec[:, 0:2 * KT],
                                   ACT.Silu).then_inc(ada_chain, 1)
                    act.activation(exact[:], consts[:, 0:4, :], ACT.Copy)
                    act.wait_ge(x_landed, 16)
                    for k in range(KT):
                        if k >= 3:
                            act.wait_ge(xss, k - 2)
                        act.activation(xsq[:, k % 3, :], x[:, k, :], ACT.Square).then_inc(xsq_ready, 1)
                    act.wait_ge(xss, KT)
                    act.wait_ge(pair_free[0], 1)
                    act.activation(rs0[:], ps[:, 0, :], ACT.Sqrt, bias=eps[:, 0:1], scale=1.0 / D).then_inc(x_std, 1)
                    split_hi(act, 0, 0)
                    split_hi(act, 1, 0)

                @block.gpsimd
                def _(pool):
                    pool.wait_ge(ada_chain, 1)
                    for c in range(ADA_FIRST):
                        if BY[c] == "P":
                            pool.wait_ge(*landed(c))
                            pool.tensor_tensor(landing(c), landing(c),
                                               cs[:, 0, :].unsqueeze(2).to_broadcast([P, KT, 256]),
                                               ALU.mult).then_inc(first_mul, 1)

                @block.vector
                def _(dve):
                    dve.memset(eps[:], EPS).then_inc(pair_free[0], 1)
                    dve.memset(coef[:], 0.0).then_inc(pair_free[1], 1)
                    dve.sem_inc(acc_ready, ADA_OWN)
                    dve.wait_ge(ada_chain, 1)
                    n = 1
                    slot_user = {}
                    for c in range(ADA_FIRST):
                        if c == 3:
                            dve.wait_ge(x_std, 1)
                            dve.reciprocal(rs0[:], rs0[:]).then_inc(x_rs, 1)
                        src = landing(c)
                        counted = first_acc if c < ADA_OWN else acc_ready
                        if c % 2 in slot_user:
                            dve.wait_ge(mod_done, slot_user[c % 2] + 1)
                        slot_user[c % 2] = c
                        if BY[c] == "P":
                            dve.wait_ge(first_mul, BY[:c + 1].count("P"))
                            dve.tensor_reduce(ada_acc[:, c % 2, :], src.rearrange("p k n -> p n k"),
                                              AX.X, ALU.add).then_inc(counted, 1)
                            continue
                        dve.wait_ge(*landed(c))
                        for k in range(KT):
                            if k == 0:
                                ins = dve.tensor_scalar(ada_acc[:, c % 2, :], src[:, k, :], cs[:, 0, k:k + 1],
                                                        None, ALU.mult)
                            else:
                                dve.wait_ge(ada_chain, n)
                                ins = dve.scalar_tensor_tensor(out=ada_acc[:, c % 2, :], in0=src[:, k, :],
                                                               scalar=cs[:, 0, k:k + 1], in1=ada_acc[:, c % 2, :],
                                                               op0=ALU.mult, op1=ALU.add)
                            if k < KT - 1:
                                ins.then_inc(ada_chain, 1)
                                n += 1
                            else:
                                ins.then_inc(counted, 1)
                    split_lo(dve, 0, 0)
                    split_lo(dve, 1, 0)

                @block.tensor
                def _(pe):
                    pe.wait_ge(ada_chain, 1)
                    pe.wait_ge(setup, 32)
                    for c in range(ADA_OWN):
                        if c == 0:
                            for k in range(KT):
                                pe.wait_ge(xsq_ready, k + 1)
                                pe.matmul(ps[:, 0, :], ones, xsq[:, k % 3, :], start=k == 0,
                                          stop=k == KT - 1).then_inc(xss, 1)
                        pe.wait_ge(first_acc, c + 1)
                        for b in range(2):
                            mm = pe.matmul(ps[:, MODB, 2 * c + b:2 * c + b + 1],
                                           ada_acc[:, c % 2, b * P:(b + 1) * P], ones[:, 0:1], start=True, stop=True)
                        mm.then_inc(mod_done, 1)
                    for c in range(ADA_OWN, ADA_FIRST):
                        ada_columns(pe, c, 0)

            boundary("none", None, [(v("mix_pre"), "sc1", "sh1", hhi, hlo)], mods=(0, ADA_FIRST),
                     panel=(0, 0), split=False, given=rs0[:])

        with ExitStack() as seg:
            qk = sbuf(seg, "qk", [P, 2 * CT, S])
            vt = sbuf(seg, "vt", [P, TB, AW])
            u = sbuf(seg, "u", [P, CT, CK - 1 + S])
            cv = sbuf(seg, "cv", [P, CT, S])
            ncum = sbuf(seg, "ncum", [H1, S])
            ncum_p = sbuf(seg, "ncum_p", [H1, 2, S], F32R)
            sg = sbuf(seg, "sg", [P, 2, S])
            conv_step = sem("conv_step")
            lf_ready = sem("lf_ready")
            pad_ready = sem("pad_ready")

            def conv_taps(dve, n0, n1):
                for n in range(n0, n1):
                    j, tap = n % CT, n // CT
                    w = v("conv_w", j * CK + tap)
                    src = u[:, j, tap:tap + S]
                    if tap == 0:
                        dve.tensor_scalar(cv[:, j, :], src, w, v("conv_b", j), ALU.mult,
                                          ALU.add).then_inc(conv_step, 1)
                    else:
                        dve.wait_ge(conv_step, n - CT + 1)
                        dve.scalar_tensor_tensor(out=cv[:, j, :], in0=src, scalar=w, in1=cv[:, j, :],
                                                 op0=ALU.mult, op1=ALU.add).then_inc(conv_step, 1)
            TAPS_EARLY = 46

            with ExitStack() as tmp:
                wf_raw = sbuf(tmp, "wf_raw", [P, KT, H1])
                wf_hi = sbuf(tmp, "wf_hi", [P, KT, P], F32R)
                wf_lo = sbuf(tmp, "wf_lo", [P, KT, P], F32R)
                ft = sbuf(tmp, "ft", [H1, 4, S])
                one_row = sbuf(tmp, "one_row", [H1, S])
                c0, q0, a0 = 0, 0, ADA_FIRST
                segs = [("conv", 4), ("q1", 2), ("k1", 2), ("v1", 2)]
                with nc.Block() as block:
                    @block.sync
                    def _(sp):
                        sp.dma_start(wf_raw[:].rearrange("p k n -> p (k n)"), w_f).then_inc(small_landed, 16)

                        def step(i, r):
                            load_panel(sp, c0 + r + 4, i)
                            load_ada(sp, a0 + r + 2, i)
                        pairs(sp, 10, step)

                    @block.gpsimd
                    def _(pool):
                        pairs(pool, 10, lambda i, r: ada_multiply(pool, a0 + r, i))

                    @block.scalar
                    def _(act):
                        at0 = 0
                        for name, n in segs:
                            def step(i, r, name=name, at0=at0):
                                c = at0 + r
                                pair = c % 2
                                act.wait_ge(panels_used, at(c + 1, i))
                                bank = ps[:, 2 * pair:2 * pair + 2, :]
                                if name == "conv":
                                    act.activation(sg[:, pair, :], ps[:, 2 * pair + 1, :],
                                                   ACT.Sigmoid).then_inc(sg_ready, 1)
                                elif name == "v1":
                                    act.activation(vt[:, :, r * 256:(r + 1) * 256],
                                                   bank.rearrange("p a (b c) -> p (a b) c", b=2),
                                                   ACT.Copy).then_inc(pair_free[pair], 1)
                                else:
                                    t = 2 * r + (CT if name == "k1" else 0)
                                    act.activation(qk[:, t:t + 2, :], bank, ACT.Copy,
                                                   scale=HD ** -0.5 if name == "q1" else 1.0
                                                   ).then_inc(pair_free[pair], 1)
                                split_hi(act, c + 2, i)
                            pairs(act, n, step)
                            at0 += n
                            if name == "conv":
                                small_exp(act, ft, H1, 3, 1)

                    @block.vector
                    def _(dve):
                        dve.memset(u[:, :, 0:CK - 1], 0.0).then_inc(pad_ready, 1)
                        dve.memset(one_row[:], 1.0).then_inc(pad_ready, 1)
                        dve.wait_ge(small_landed, 16)
                        split_small(dve, wf_hi, wf_lo, wf_raw, H1, 0)

                        def conv(i, r):
                            c = r
                            ada_sum(dve, a0 + c, i)
                            dve.wait_ge(sg_ready, at(c + 1, i))
                            j = r + i * 2
                            dst = u[:, j, CK - 1:] if isinstance(i, int) else u[:, bass.ds(j, 1), CK - 1:]
                            dve.tensor_tensor(dst, ps[:, 2 * r, :], sg[:, r, :], ALU.mult).then_inc(pair_free[r], 1)
                            split_lo(dve, c + 2, i)
                        pairs(dve, 4, conv)
                        last, then = log1p_exp(dve, ft, H1, v("b_f")[0:H1, :], 0, 1)
                        dve.tensor_scalar(ft[:, 2, :], ft[:, 0, :], 0.0, -1.0, ALU.min,
                                          ALU.mult).then_inc(lf_ready, 1)
                        dve.wait_ge(lf_ready, 1)
                        dve.tensor_tensor(ft[:, 3, :], ft[:, 2, :], ft[:, 1, :], ALU.add).then_inc(lf_ready, 1)
                        dve.wait_ge(lf_ready, 2)
                        dve.tensor_tensor_scan(ncum[:], one_row[:], ft[:, 3, :], 0.0, ALU.mult,
                                               ALU.add).then_inc(lf_ready, 1)
                        dve.wait_ge(lf_ready, 3)
                        dve.tensor_copy(ncum_p[:, 0, :], ncum[:]).then_inc(lf_ready, 1)
                        dve.wait_ge(lf_ready, 4)
                        dve.tensor_tensor(ncum_p[:, 1, :], ncum[:], ncum_p[:, 0, :].bitcast(F32),
                                          ALU.subtract).then_inc(lf_ready, 1)
                        dve.wait_ge(pair_free[0], 3)
                        dve.wait_ge(pair_free[1], 3)
                        for k in range(4, 10):
                            ada_sum(dve, a0 + k, 0)
                            split_lo(dve, k + 2, 0)
                            if k < 9:
                                conv_taps(dve, (k - 4) * TAPS_EARLY // 5, (k - 3) * TAPS_EARLY // 5)

                    @block.tensor
                    def _(pe):
                        def step(i, r, by_token=False):
                            in_panel(pe, 1 + r, 1 + r, i, (hhi, hlo), by_token)
                            ada_columns(pe, a0 + r, i)
                        pairs(pe, 3, step)
                        small_projection(pe, wf_hi, wf_lo, 4)
                        pairs(pe, 4, lambda i, r: step(i, 3 + r))
                        step(0, 7, True)
                        step(0, 8, True)
                        ada_columns(pe, a0 + 9, 0)

            NU = TB * H1
            lsq = sbuf(seg, "lsq", [P, CT, S])
            lrs = sbuf(seg, "lrs", [P, S])
            TAPS_BY = NU - 5
            with ExitStack() as tmp:
                pm = sbuf(tmp, "pm", [P, 2, S])
                pt = sbuf(tmp, "pt", [P, 2, S])
                mx = sbuf(tmp, "mx", [P, NU])
                nmx = sbuf(tmp, "nmx", [P, NU])
                rsum = sbuf(tmp, "rsum", [P, NU])
                rinv = sbuf(tmp, "rinv", [P, NU])
                o1 = sbuf(tmp, "o1", [P, 2, AW])
                A = {k: sem("a1_" + k) for k in ("s_done", "max", "nmax", "exp", "t_done", "pt_ready", "pv_done",
                                                 "rinv", "o_ready", "ot_done", "ohi", "olo", "mean", "centred",
                                                 "sq", "var", "std", "rstd", "scaled", "silu", "chi", "clo")}
                units = [(qb, h) for qb in range(TB) for h in range(H1)]
                with nc.Block() as block:
                    @block.tensor
                    def _(pe):
                        def logits(n):
                            qb, h = units[n]
                            nk = (qb + 1) * P
                            r0 = HD * (h % 2)
                            if n >= 2:
                                pe.wait_ge(A["exp"], n - 1)
                            o = ps[:, n % 2, 0:nk]
                            pe.matmul(o, qk[r0:r0 + HD, h // 2, qb * P:(qb + 1) * P],
                                      qk[r0:r0 + HD, CT + h // 2, 0:nk], start=True, stop=False)
                            for part in range(2):
                                pe.matmul(o, ident_r[0:H1, h:h + 1].to_broadcast([H1, P]), ncum_p[:, part, 0:nk],
                                          start=False, stop=False)
                            pe.matmul(ps[:, n % 2, qb * P:nk], ident_r, exact[:, CST["neg_after"], :],
                                      start=False, stop=True).then_inc(A["s_done"], 1)

                        def turn(n):
                            qb, h = units[n]
                            pe.wait_ge(A["exp"], n + 1)
                            if n >= 2:
                                pe.wait_ge(A["pt_ready"], n - 1)
                            for kb in range(qb + 1):
                                mm = pe.transpose(ps[:, 2 + n % 2, kb * P:(kb + 1) * P],
                                                  pm[:, n % 2, kb * P:(kb + 1) * P], ident)
                            mm.then_inc(A["t_done"], 1)

                        def values(n):
                            qb, h = units[n]
                            pe.wait_ge(A["pt_ready"], n + 1)
                            if h == 0 and qb >= 2:
                                pe.wait_ge(A["o_ready"], qb - 1)
                            for kb in range(qb + 1):
                                mm = pe.matmul(ps[:, 6 + qb % 2, h * HD:(h + 1) * HD],
                                               pt[:, n % 2, kb * P:(kb + 1) * P],
                                               vt[:, kb, h * HD:(h + 1) * HD], start=kb == 0, stop=kb == qb)
                            mm.then_inc(A["pv_done"], 1)

                        def turn_out(qb):
                            pe.wait_ge(A["o_ready"], qb + 1)
                            if qb:
                                pe.wait_ge(A["olo"], qb)
                            for t in range(CT):
                                mm = pe.transpose(ps[:, 5, t * P:(t + 1) * P], o1[:, qb % 2, t * P:(t + 1) * P],
                                                  ident)
                            mm.then_inc(A["ot_done"], 1)

                        for n in range(NU + 4):
                            if n < NU:
                                logits(n)
                            if 1 <= n <= NU:
                                turn(n - 1)
                            if 2 <= n <= NU + 1:
                                values(n - 2)
                            if n >= H1 + 3 and (n - 3) % H1 == 0:
                                turn_out((n - 3) // H1 - 1)
                            if n == TAPS_BY + 1:
                                for j in range(CT):
                                    pe.wait_ge(conv_step, CK * CT - CT + j + 1)
                                    if j == 0:
                                        pe.wait_ge(mod_read, read_counts[(10, 20)])
                                    mm = pe.matmul(ps[:, 4, :], ones, cv[:, j, :], start=j == 0, stop=j == CT - 1)
                                mm.then_inc(A["mean"], 1)
                            if n == TAPS_BY + 6:
                                pe.wait_ge(A["centred"], CT)
                                for j in range(CT):
                                    pe.wait_ge(A["sq"], j + 1)
                                    mm = pe.matmul(ps[:, 4, :], ones, lsq[:, j, :], start=j == 0, stop=j == CT - 1)
                                mm.then_inc(A["var"], 1)

                    @block.scalar
                    def _(act):
                        def out_hi(qb):
                            act.wait_ge(A["ot_done"], qb + 1)
                            act.activation(hhi[:, 0:CT, qb * P:(qb + 1) * P],
                                           ps[:, 5, :].rearrange("p (t q) -> p t q", t=CT),
                                           ACT.Copy).then_inc(A["ohi"], 1)
                        for n, (qb, h) in enumerate(units):
                            nk = (qb + 1) * P
                            act.wait_ge(A["nmax"], n + 1)
                            if n >= 2:
                                act.wait_ge(A["t_done"], n - 1)
                            act.activation(pm[:, n % 2, 0:nk], ps[:, n % 2, 0:nk], ACT.Exp, bias=nmx[:, n:n + 1],
                                           accum_out=rsum[:, n:n + 1]).then_inc(A["exp"], 1)
                            if n >= H1 + 3 and (n - 3) % H1 == 0:
                                out_hi((n - 3) // H1 - 1)
                            if n >= TAPS_BY + 3:
                                for j in range(CT):
                                    if TAPS_BY + 3 + j // 2 == n:
                                        act.wait_ge(A["centred"], j + 1)
                                        act.activation(lsq[:, j, :], cv[:, j, :], ACT.Square).then_inc(A["sq"], 1)
                        act.wait_ge(A["var"], 1)
                        act.activation(lrs[:], ps[:, 4, :], ACT.Sqrt, bias=eps[:, 0:1],
                                       scale=1.0 / AW).then_inc(A["std"], 1)
                        out_hi(TB - 1)

                    @block.vector
                    def _(dve):
                        read_mod(dve, 10, 20)

                        def neg_max(n):
                            qb, h = units[n]
                            dve.wait_ge(A["s_done"], n + 1)
                            dve.tensor_reduce(mx[:, n:n + 1], ps[:, n % 2, 0:(qb + 1) * P], AX.X,
                                              ALU.max).then_inc(A["max"], 1)
                            dve.wait_ge(A["max"], n + 1)
                            dve.tensor_scalar(nmx[:, n:n + 1], mx[:, n:n + 1], -1.0, None,
                                              ALU.mult).then_inc(A["nmax"], 1)

                        def take_pt(n):
                            qb, h = units[n]
                            dve.wait_ge(A["t_done"], n + 1)
                            if n >= 2:
                                dve.wait_ge(A["pv_done"], n - 1)
                            dve.tensor_copy(pt[:, n % 2, 0:(qb + 1) * P],
                                            ps[:, 2 + n % 2, 0:(qb + 1) * P]).then_inc(A["pt_ready"], 1)

                        def normalise(qb):
                            dve.wait_ge(A["pv_done"], H1 * (qb + 1))
                            cols = slice(H1 * qb, H1 * (qb + 1))
                            dve.reciprocal(rinv[:, cols], rsum[:, cols]).then_inc(A["rinv"], 1)
                            dve.wait_ge(A["rinv"], qb + 1)
                            if qb >= 2:
                                dve.wait_ge(A["ot_done"], qb - 1)
                            dve.tensor_tensor(o1[:, qb % 2, :].rearrange("p (h d) -> p h d", h=H1),
                                              ps[:, 6 + qb % 2, :].rearrange("p (h d) -> p h d", h=H1),
                                              rinv[:, cols].unsqueeze(2).to_broadcast([P, H1, HD]),
                                              ALU.mult).then_inc(A["o_ready"], 1)

                        def out_lo(qb):
                            dve.wait_ge(A["ohi"], qb + 1)
                            dve.tensor_tensor(hlo[:, 0:CT, qb * P:(qb + 1) * P],
                                              ps[:, 5, :].rearrange("p (t q) -> p t q", t=CT),
                                              hhi[:, 0:CT, qb * P:(qb + 1) * P].bitcast(F32),
                                              ALU.subtract).then_inc(A["olo"], 1)
                        taps = CK * CT - TAPS_EARLY
                        for n in range(NU + 4):
                            if n < NU:
                                neg_max(n)
                            if 1 <= n <= NU:
                                take_pt(n - 1)
                            if n >= H1 + 2 and (n - 2) % H1 == 0:
                                normalise((n - 2) // H1 - 1)
                            if n >= H1 + 4 and (n - 4) % H1 == 0:
                                out_lo((n - 4) // H1 - 1)
                            if n < TAPS_BY:
                                conv_taps(dve, TAPS_EARLY + taps * n // TAPS_BY, TAPS_EARLY + taps * (n + 1) // TAPS_BY)
                            if n == TAPS_BY + 2:
                                dve.wait_ge(A["mean"], 1)
                                for j in range(CT):
                                    dve.scalar_tensor_tensor(out=cv[:, j, :], in0=ps[:, 4, :], scalar=-1.0 / AW,
                                                             in1=cv[:, j, :], op0=ALU.mult,
                                                             op1=ALU.add).then_inc(A["centred"], 1)
                        out_lo(TB - 1)

            c0 = FIRST["wo"]
            with nc.Block() as block:
                @block.sync
                def _(sp):
                    stream(sp, "wo", load=True, keep_last=1)

                @block.scalar
                def _(act):
                    for j in range(CT):
                        act.wait_ge(A["scaled"], j + 1)
                        act.activation(lsq[:, j, :], cv[:, j, :], ACT.Silu, bias=v("ln_b", j)).then_inc(A["silu"], 1)
                    act.activation(warm[:], ones[:, 0:1], ACT.Sqrt)
                    stream(act, "wo", hi=True, keep_last=1)

                @block.vector
                def _(dve):
                    dve.wait_ge(A["std"], 1)
                    dve.reciprocal(lrs[:], lrs[:]).then_inc(A["rstd"], 1)
                    dve.wait_ge(A["rstd"], 1)
                    for j in range(CT):
                        dve.scalar_tensor_tensor(out=cv[:, j, :], in0=cv[:, j, :], scalar=v("ln_g", j),
                                                 in1=lrs[:], op0=ALU.mult, op1=ALU.mult).then_inc(A["scaled"], 1)
                    for j in range(CT):
                        dve.wait_ge(A["silu"], j + 1)
                        dve.tensor_copy(hhi[:, CT + j, :], lsq[:, j, :]).then_inc(A["chi"], 1)
                        dve.wait_ge(A["chi"], j + 1)
                        dve.tensor_tensor(hlo[:, CT + j, :], lsq[:, j, :], hhi[:, CT + j, :].bitcast(F32),
                                          ALU.subtract).then_inc(A["clo"], 1)
                    stream(dve, "wo", lo=True, keep_last=1)

                @block.tensor
                def _(pe):
                    out_projection(pe, "wo", [(hhi, hlo), (hhi[:, CT:, :], hlo[:, CT:, :])], ready=(A["clo"], CT))
        boundary("mix_post", "g1", [(v("ffn_pre"), "sc2", "sh2", hhi, hlo)], panel=(FIRST["ffn_in"], 10))

        with ExitStack() as seg:
            fhi = sbuf(seg, "fhi", [P, FT, S], F32R)
            flo = sbuf(seg, "flo", [P, FT, S], F32R)
            fg = sbuf(seg, "fg", [P, 2, S])
            g_ready = sem("g_ready")
            prod_ready = sem("prod_ready")
            fhi_ready = sem("fhi_ready")
            flo_ready = sem("flo_ready")
            c0, q0, a0 = FIRST["ffn_in"], 10, 20
            parts = [(0, ADA_C2 - a0), (ADA_C2 - a0, FT)]
            with nc.Block() as block:
                @block.sync
                def _(sp):
                    pairs(sp, FT, lambda i, r: (load_panel(sp, c0 + r + 4, i), load_ada(sp, a0 + r + 2, i)))

                @block.gpsimd
                def _(pool):
                    for lo, hi in parts:
                        pairs(pool, hi - lo, lambda i, r, lo=lo: ada_multiply(pool, a0 + lo + r, i))

                @block.scalar
                def _(act):
                    def step(i, r):
                        pair = (q0 + r) % 2
                        act.wait_ge(panels_used, at(c0 + r + 1, i))
                        act.activation(fg[:, pair, :], ps[:, 2 * pair, :], ACT.Silu).then_inc(g_ready, 1)
                        split_hi(act, c0 + r + 2, i)
                    pairs(act, FT, step)

                @block.vector
                def _(dve):
                    def step(i, r):
                        ada_sum(dve, a0 + r, i)
                        pair = (q0 + r) % 2
                        t = r + i * 2
                        dve.wait_ge(g_ready, at(r + 1, i))
                        dve.tensor_tensor(fg[:, pair, :], ps[:, 2 * pair + 1, :], fg[:, pair, :],
                                          ALU.mult).then_inc(prod_ready, 1)
                        dve.wait_ge(prod_ready, at(r + 1, i))
                        dve.tensor_copy(fhi[:, bass.ds(t, 1), :], fg[:, pair, :]).then_inc(fhi_ready, 1)
                        dve.wait_ge(fhi_ready, at(r + 1, i))
                        dve.tensor_tensor(flo[:, bass.ds(t, 1), :], fg[:, pair, :],
                                          fhi[:, bass.ds(t, 1), :].bitcast(F32),
                                          ALU.subtract).then_inc(pair_free[pair], 1)
                        split_lo(dve, c0 + r + 2, i)
                    pairs(dve, FT, step)
                    read_mod(dve, 20, 42)

                @block.tensor
                def _(pe):
                    pairs(pe, FT - 1, lambda i, r: (in_panel(pe, c0 + 1 + r, q0 + 1 + r, i, (hhi, hlo), False),
                                                    ada_columns(pe, a0 + r, i)))
                    ada_columns(pe, a0 + FT - 1, 0)
            out_block("ffn_out", [(fhi, flo)])
        boundary("ffn_post", "g2", [(v("norm2", 0, KT), "msc", "msh", hhi, hlo)], panel=(FIRST["xbc"], 32))

        with ExitStack() as seg:
            xbc, _, y2lo = shared_sbuf(seg, ("xbc", [P, XT, S], F32),
                                       [("y_place", [P, MT, S], F32), ("y2lo", [P, XT - MT, S], F32R)])
            assert MH * TB == P
            dtq = sbuf(seg, "dtq", [P, P])
            acq = sbuf(seg, "acq", [P, P])
            state = sbuf(seg, "state", [P, MG, MI // MG])
            dt_seq = sem("dt_seq")
            x_stored = sem("x_stored")
            x_back = sem("x_back")
            G = {k: sem("g_" + k) for k in ("z", "gated", "sq", "ss", "std", "rs", "scaled", "hi", "lo")}
            c0, q0, a0 = FIRST["xbc"], 32, 42
            with ExitStack() as tmp:
                wd_raw = sbuf(tmp, "wd_raw", [P, KT, MH])
                wd_hi = sbuf(tmp, "wd_hi", [P, KT, P], F32R)
                wd_lo = sbuf(tmp, "wd_lo", [P, KT, P], F32R)
                dtt = sbuf(tmp, "dtt", [P, 4, P])
                one_row = sbuf(tmp, "one_row2", [P, P])
                aneg = sbuf(tmp, "aneg", [P, 2])
                tap0 = sem("tap0")
                taps = sem("taps")
                xs_ready = sem("xs_ready")
                with nc.Block() as block:
                    @block.sync
                    def _(sp):
                        sp.dma_start(wd_raw[:].rearrange("p k n -> p (k n)"), w_dt).then_inc(small_landed, 16)
                        sp.dma_start(x_kept, x[:]).then_inc(x_stored, 16)
                        pairs(sp, XT // 2 - 2, lambda i, r: (load_panel(sp, c0 + r + 4, i),
                                                             load_ada(sp, a0 + r + 2, i)))
                        for r in range(2):
                            load_panel(sp, c0 + r + 4, XT // 4 - 1)

                    @block.gpsimd
                    def _(pool):
                        pairs(pool, XT // 2, lambda i, r: ada_multiply(pool, a0 + r, i))

                    @block.scalar
                    def _(act):
                        act.activation(aneg[:, 0:1], v("a_log"), ACT.Exp).then_inc(dt_seq, 1)

                        def step(i, r):
                            pair = (q0 + r) % 2
                            act.wait_ge(panels_used, at(c0 + r + 1, i))
                            for b in range(2):
                                t = 2 * r + b + i * 4
                                bc = VEC["mconv_b"][0] + t
                                wc = VEC["mconv_w"][0] + t * MK + MK - 1
                                act.activation(xbc[:, bass.ds(t, 1), :], ps[:, 2 * pair + b, :], ACT.Identity,
                                               bias=vec[:, bass.ds(bc, 1)],
                                               scale=vec[:, bass.ds(wc, 1)]).then_inc(tap0, 1)
                            split_hi(act, c0 + r + 2, i)
                            act.wait_ge(taps, 6 * r + 6 + i * 12)
                            for half in (1, 0):
                                both = xbc[:, bass.ds(2 * r + i * 4, 2), half * 256:half * 256 + 256]
                                act.activation(both, both, ACT.Silu).then_inc(xs_ready, 1)
                        pairs(act, XT // 2, step)
                        small_exp(act, dtt, P, 24, 2)

                    @block.vector
                    def _(dve):
                        dve.memset(one_row[:], 1.0).then_inc(pad_ready, 1)
                        dve.wait_ge(small_landed, 32)
                        split_small(dve, wd_hi, wd_lo, wd_raw, MH, 4)

                        def step(i, r):
                            ada_sum(dve, a0 + r, i)
                            pair = (q0 + r) % 2
                            for s in range(1, MK):
                                for b in range(2):
                                    t = 2 * r + b + i * 4
                                    wc = VEC["mconv_w"][0] + t * MK + MK - 1 - s
                                    if s == 1:
                                        dve.wait_ge(tap0, 2 * r + b + 1 + i * 4)
                                    else:
                                        dve.wait_ge(taps, 6 * r + (s - 1) * 2 + b - 1 + i * 12)
                                    ins = dve.scalar_tensor_tensor(
                                        out=xbc[:, bass.ds(t, 1), s:S], in0=ps[:, 2 * pair + b, 0:S - s],
                                        scalar=vec[:, bass.ds(wc, 1)], in1=xbc[:, bass.ds(t, 1), s:S],
                                        op0=ALU.mult, op1=ALU.add)
                                    ins.then_inc(taps, 1)
                            dve.wait_ge(taps, 6 * r + 6 + i * 12)
                            dve.sem_inc(pair_free[pair], 1)
                            split_lo(dve, c0 + r + 2, i)
                        pairs(dve, XT // 2, step)
                        read_mod(dve, 42, 54)
                        last, then = log1p_exp(dve, dtt, P, v("dt_bias"), 17, 2, by_chunk=True)
                        dve.tensor_scalar(dtt[:, 2, :], dtt[:, 0, :], 0.0, None, ALU.max).then_inc(dt_seq, 1)
                        dve.wait_ge(dt_seq, 2)
                        dve.tensor_tensor(dtq[:], dtt[:, 2, :], dtt[:, 1, :], ALU.add).then_inc(dt_seq, 1)
                        dve.tensor_scalar(aneg[:, 1:2], aneg[:, 0:1], -1.0, None, ALU.mult).then_inc(dt_seq, 1)
                        dve.wait_ge(dt_seq, 4)
                        dve.tensor_scalar(dtt[:, 3, :], dtq[:], aneg[:, 1:2], None, ALU.mult).then_inc(dt_seq, 1)
                        dve.wait_ge(dt_seq, 5)
                        dve.tensor_tensor_scan(acq[:], one_row[:], dtt[:, 3, :], 0.0, ALU.mult,
                                               ALU.add).then_inc(dt_seq, 1)

                    @block.tensor
                    def _(pe):
                        small_projection(pe, wd_hi, wd_lo, 8)
                        pairs(pe, XT // 2 - 1,
                              lambda i, r: (in_panel(pe, c0 + 1 + r, q0 + 1 + r, i, (hhi, hlo), False),
                                            ada_columns(pe, a0 + r, i)))
                        ada_columns(pe, a0 + XT // 2 - 1, 0)

            GH = MH // MG
            HB = 4
            NB = MH // HB
            NN = TB * NB
            c0, q0, cm = FIRST["z"], 44, FIRST["m_out"]
            IN_LAYING = [4, 4, 4, 0]
            IN_BATCHES = [7, 7, 6, 0]
            LAYING_OUT, QUARTERS = [], []
            for c in range(TB):
                k = sum(IN_LAYING[:c]) + sum(IN_BATCHES[:c])
                LAYING_OUT.append(range(k, k + IN_LAYING[c]))
                for b in range(NB):
                    j = k + IN_LAYING[c] + b - (NB - IN_BATCHES[c])
                    QUARTERS.append(range(j, j + 1) if b >= NB - IN_BATCHES[c] else range(0))

            def taken_at(n):
                ks = (list(QUARTERS[n - 1]) if n > 0 else []) + (list(LAYING_OUT[n // NB]) if n % NB == 0 else [])
                return [k // 4 for k in ks if k % 4 == 3]

            def gate_part(e, g):
                z = x[:, 4 * g:4 * g + 4, :] if g < 2 else zb[:, 4 * g - 8:4 * g - 4, :]
                y = xbc[:, 4 * g:4 * g + 4, :]
                e.tensor_tensor(y, y, z, ALU.mult).then_inc(G["gated"], 1)

            def norm_part(dve, g):
                dve.wait_ge(G["std"], g + 1)
                dve.reciprocal(state[:, g, :], state[:, g, :]).then_inc(G["rs"], 1)
                dve.wait_ge(G["rs"], g + 1)
                for t in range(4 * g, 4 * g + 4):
                    dve.scalar_tensor_tensor(out=xbc[:, t, :], in0=xbc[:, t, :], scalar=v("m_norm", t),
                                             in1=state[:, g, :], op0=ALU.mult,
                                             op1=ALU.mult).then_inc(G["scaled"], 1)

            def lo_part(dve, g):
                for t in range(4 * g, 4 * g + 4):
                    hi, lo = hi_lo(t)
                    dve.wait_ge(G["hi"], t + 1)
                    dve.tensor_tensor(lo, xbc[:, t, :], hi.bitcast(F32), ALU.subtract).then_inc(G["lo"], 1)

            def hi_part(act, g):
                for t in range(4 * g, 4 * g + 4):
                    act.wait_ge(G["scaled"], t + 1)
                    act.activation(hi_lo(t)[0], xbc[:, t, :], ACT.Copy).then_inc(G["hi"], 1)

            with ExitStack() as tmp:
                zb, y2hi = shared_sbuf(tmp, ("zb", [P, KT, S], F32), [("y2hi", [P, KT, S], F32R)])

                def hi_lo(t):
                    if t < KT:
                        return hhi[:, t, :], hlo[:, t, :]
                    return y2hi[:, t - KT, :], y2lo[:, t - KT, :]

                xdt = ada_raw[:, 0, :, :].rearrange("p k n -> p (k n)").rearrange("p (h d) -> p h d", h=MH)
                xw = ada_raw[:, 1, :, :].rearrange("p k n -> p (k n)").rearrange("p (h d) -> p h d", h=MH)
                gsq = ada_raw[:, 1, :, :].rearrange("p k n -> p (k n)").rearrange("p (a s) -> p a s", a=4)
                btok = sbuf(tmp, "btok", [P, MG, MN])
                cb = sbuf(tmp, "cb", [P, MG, P])
                bc = sbuf(tmp, "bc", [P, 2, HB, P])
                seg_t = sbuf(tmp, "seg_t", [P, 2, HB, P])
                dec = sbuf(tmp, "dec", [P, 2, HB, P])
                ce = sbuf(tmp, "ce", [P, 2, HB, P])
                dtc = sbuf(tmp, "dtc", [P, TB, MH])
                acc_c = sbuf(tmp, "acc_c", [P, TB, MH])
                dend = sbuf(tmp, "dend", [P, TB, MH])
                wend = sbuf(tmp, "wend", [P, TB, MH])
                M = {k: sem("m_" + k) for k in ("cols", "cols_c", "wend0", "ends", "xdt", "xw", "bt", "btok",
                                                "cbm", "rows", "bc0", "bc1", "seg", "clip", "grow", "ce", "dec",
                                                "mat", "yd", "yskip", "st", "decay", "state")}

                with nc.Block() as block:
                    @block.sync
                    def _(sp):
                        for c in range(TB):
                            sp.dma_start(ac_rows[:, c * P:(c + 1) * P],
                                         acq[c * MH:(c + 1) * MH, :]).then_inc(M["rows"], 16)
                        sp.wait_ge(M["rows"], 16 * TB)
                        sp.wait_ge(x_stored, 16)
                        for n in range(NN):
                            c, b = n // NB, n % NB
                            if n >= 2:
                                sp.wait_ge(M["clip"], n - 1)
                                if n - 2 >= NB:
                                    sp.wait_ge(M["grow"], n - 1 - NB)
                            sp.dma_start(bc[:, n % 2, :, :],
                                         ac_rows[b * HB:(b + 1) * HB, c * P:(c + 1) * P].unsqueeze(0)
                                         .to_broadcast([P, HB, P])).then_inc(M[f"bc{n % 2}"], 16)
                            for p in taken_at(n - 2) if n >= 2 else ():
                                load_panel(sp, c0 + p + 4, 0)

                        sp.wait_ge(G["gated"], 2)
                        sp.dma_start(x[:], x_kept).then_inc(x_back, 16)
                        stream(sp, "m_out", load=True, keep_last=1)

                    @block.tensor
                    def _(pe):
                        pe.transpose(ps[:, 4, 0:P], dtq[:], ident)
                        pe.transpose(ps[:, 4, P:2 * P], acq[:], ident)
                        pe.matmul(ps[:, 4, 2 * P:3 * P], acq[:, P - 1:P].to_broadcast([P, P]), ident, start=True,
                                  stop=True).then_inc(M["cols"], 1)

                        def z_quarter(k):
                            p, b, k0 = k // 4, k // 2 % 2, 4 * (k % 2)
                            cp, qp = c0 + p, q0 + p
                            if k % 4 == 0:
                                pe.wait_ge(lo_split, cp + 1)
                                pe.wait_ge(pair_free[qp % 2], qp // 2 + 1)
                            for kt in range(k0, k0 + 4):
                                for j, (wt, part) in enumerate(PASSES):
                                    mm = pe.matmul(ps[:, 2 * (qp % 2) + b, :], wt[:, cp % 2, 2 * kt + b, :],
                                                   (hhi, hlo)[part][:, kt, :], start=(kt == 0 and j == 0),
                                                   stop=(kt == KT - 1 and j == 2))
                            if k % 4 == 3:
                                mm.then_inc(panels_used, 1)

                        def squares(g):
                            if g >= 2:
                                pe.wait_ge(G["std"], g - 1)
                            for t in range(4 * g, 4 * g + 4):
                                pe.wait_ge(G["sq"], t + 1)
                                pe.matmul(ps[:, 4 + g % 2, :], ones, gsq[:, t % 4, :], start=t % 4 == 0,
                                          stop=t % 4 == 3).then_inc(G["ss"], 1)

                        for c in range(TB):
                            w = slice(c * P, (c + 1) * P)
                            for k in LAYING_OUT[c][0:1]:
                                z_quarter(k)
                            if c == 0:
                                pe.wait_ge(M["cols_c"], 3)
                            else:
                                pe.wait_ge(M["state"], MG * c)
                            for r in range(4):
                                if r == 2:
                                    for k in LAYING_OUT[c][1:2]:
                                        z_quarter(k)
                                if r >= 2:
                                    pe.wait_ge(M["xdt"], 4 * c + r - 1)
                                for j in range(4):
                                    mm = pe.transpose(ps[:, 4 + r % 2, j * P:(j + 1) * P], xbc[:, 4 * r + j, w],
                                                      ident)
                                mm.then_inc(M["bt"], 1)
                            if c < TB - 1:
                                pe.wait_ge(M["xdt"], 4 * c + 3)
                                for g in range(MG):
                                    mm = pe.transpose(ps[:, 4, g * P:(g + 1) * P], xbc[:, MT + g, w], ident)
                                mm.then_inc(M["bt"], 1)
                            pe.wait_ge(M["xdt"], 4 * c + 4)
                            for g in range(MG):
                                mm = pe.matmul(ps[:, 5, g * P:(g + 1) * P], xbc[:, MT + g, w],
                                               xbc[:, MT + MG + g, w], start=True, stop=True)
                            mm.then_inc(M["bt"], 1)
                            for k in LAYING_OUT[c][2:4]:
                                z_quarter(k)
                            for g in range(MG):
                                gi = c * MG + g
                                for b in range(2):
                                    n = c * NB + g * 2 + b
                                    for k in QUARTERS[n]:
                                        z_quarter(k)
                                    pe.wait_ge(M["mat"], n + 1)
                                    if c:
                                        pe.wait_ge(M["ce"], n + 1 - NB)
                                    if b == 0 and gi >= 2:
                                        pe.wait_ge(M["yskip"], 4 * (gi - 1))
                                    for j in range(HB):
                                        hg = b * HB + j
                                        h = g * GH + hg
                                        o = HD * (h % 2)
                                        dst = ps[o:o + HD, 6 + gi % 2, hg // 2 * P:(hg // 2 + 1) * P]
                                        mm = pe.matmul(dst, xdt[:, h, :], dec[:, n % 2, j, :], start=True,
                                                       stop=c == 0)
                                        if c:
                                            mm = pe.matmul(dst, state[:, g, hg * HD:(hg + 1) * HD],
                                                           ce[:, n % 2, j, :], start=False, stop=True)
                                    mm.then_inc(M["yd"], 1)
                                if c == TB - 1 and 1 <= g < MG - 1:
                                    squares(g - 1)
                            if c < TB - 1:
                                pe.wait_ge(M["xw"], c + 1)
                                pe.wait_ge(M["btok"], c + 1)
                                pe.wait_ge(M["cbm"], c + 1)
                                for g in range(MG):
                                    n = c * MG + g
                                    if g >= 2:
                                        pe.wait_ge(M["state"], n - 1)
                                    pe.matmul(ps[:, 4 + g % 2, :], btok[:, g, :],
                                              xw[:, g * GH:(g + 1) * GH, :], start=True,
                                              stop=True).then_inc(M["st"], 1)

                        def m_panel(k):
                            half, g = divmod(k, MG)
                            cp = cm + k
                            pe.wait_ge(lo_split, cp + 1)
                            if k == MG:
                                pe.wait_ge(G["std"], MG)
                                pe.wait_ge(M["yskip"], 4 * MG * TB)
                            for j in range(4):
                                parts = hi_lo(4 * g + j)
                                if half == 0:
                                    pe.wait_ge(G["lo"], 4 * g + j + 1)
                                for f in range(4):
                                    for n, (wt, part) in enumerate(PASSES):
                                        mm = pe.matmul(ps[:, 4 * half + f, :], wt[:, cp % 2, 4 * j + f, :],
                                                       parts[part], start=(g == 0 and j == 0 and n == 0),
                                                       stop=(g == MG - 1 and j == 3 and n == 2),
                                                       skip_group_check=True)
                            mm.then_inc(panels_used, 1)
                        squares(MG - 2)
                        squares(MG - 1)
                        for k in range(2 * MG):
                            m_panel(k)

                    @block.scalar
                    def _(act):
                        act.wait_ge(M["cols_c"], 3)
                        act.wait_ge(M["wend0"], 1)
                        act.activation(dend[:], dend[:], ACT.Exp).then_inc(M["ends"], 1)
                        act.activation(wend[:], wend[:], ACT.Exp).then_inc(M["ends"], 1)

                        def take_z(p):
                            pair = (q0 + p) % 2
                            act.wait_ge(panels_used, c0 + p + 1)
                            if p == 0:
                                act.wait_ge(M["bc0"], 16)
                            dst = x[:, 2 * p:2 * p + 2, :] if p < 4 else zb[:, 2 * p - 8:2 * p - 6, :]
                            act.activation(dst, ps[:, 2 * pair:2 * pair + 2, :],
                                           ACT.Copy).then_inc(pair_free[pair], 1)
                            split_hi(act, c0 + p + 2, 0)

                        def silu_z(p):
                            dst = x[:, 2 * p:2 * p + 2, :] if p < 4 else zb[:, 2 * p - 8:2 * p - 6, :]
                            act.wait_ge(pair_free[(q0 + p) % 2], (q0 + p) // 2 + 2)
                            act.activation(dst, dst, ACT.Silu).then_inc(G["z"], 1)

                        def group_squares(g):
                            for t in range(4 * g, 4 * g + 4):
                                act.wait_ge(G["gated"], g + 1)
                                if t >= 4:
                                    act.wait_ge(G["ss"], t - 3)
                                act.activation(gsq[:, t % 4, :], xbc[:, t, :], ACT.Square).then_inc(G["sq"], 1)

                        def group_std(g):
                            act.wait_ge(G["ss"], 4 * g + 4)
                            act.activation(state[:, g, :], ps[:, 4 + g % 2, :], ACT.Sqrt, bias=eps[:, 0:1],
                                           scale=MG / MI).then_inc(G["std"], 1)

                        taken, turned = 0, 0
                        for c in range(TB):
                            if c:
                                for p in taken_at(c * NB) if c == TB - 1 else ():
                                    take_z(p)
                                    taken += 1
                                for p in range(turned, taken):
                                    silu_z(p)
                                turned = taken
                            if c < TB - 1:
                                act.wait_ge(M["bt"], 6 * c + 5)
                                if c:
                                    act.wait_ge(M["st"], MG * c)
                                act.activation(btok[:], ps[:, 4, :].rearrange("p (g t) -> p g t", g=MG),
                                               ACT.Copy).then_inc(M["btok"], 1)
                            for g in range(MG):
                                for b in range(2):
                                    n = c * NB + g * 2 + b
                                    if n >= 2:
                                        act.wait_ge(M["yd"], n - 1)
                                    if c:
                                        act.wait_ge(M[f"bc{n % 2}"], 16 * (n // 2 + 1))
                                        act.activation(ce[:, n % 2, :, :], bc[:, n % 2, :, :],
                                                       ACT.Exp).then_inc(M["grow"], 1)
                                    act.wait_ge(M["clip"], n + 1)
                                    act.activation(dec[:, n % 2, :, :], seg_t[:, n % 2, :, :],
                                                   ACT.Exp).then_inc(M["dec"], 1)
                                    for p in taken_at(n) if b or g or c < TB - 1 else ():
                                        take_z(p)
                                        taken += 1
                                if c == TB - 1 and g:
                                    group_squares(g - 1)
                        group_std(0)
                        group_std(1)
                        group_squares(MG - 1)
                        hi_part(act, 0)
                        group_std(2)
                        hi_part(act, 1)
                        group_std(3)
                        hi_part(act, 2)
                        split_hi(act, cm + 2, 0)
                        hi_part(act, 3)
                        for k in range(1, MT // 2 - 1):
                            split_hi(act, cm + k + 2, 0)

                    @block.gpsimd
                    def _(pool):
                        for n in range(NN):
                            c, b = n // NB, n % NB
                            pool.wait_ge(M["dec"], n + 1)
                            pool.wait_ge(M["cbm"], c + 1)
                            pool.tensor_tensor(dec[:, n % 2, :, :], dec[:, n % 2, :, :],
                                               cb[:, b // 2, :].unsqueeze(1).to_broadcast([P, HB, P]),
                                               ALU.mult).then_inc(M["mat"], 1)

                    @block.vector
                    def _(dve):
                        dve.wait_ge(M["cols"], 1)
                        for k, t in enumerate((dtc, acc_c, dend)):
                            dve.tensor_copy(t[:], ps[:, 4, k * P:(k + 1) * P].rearrange("p (c h) -> p c h", c=TB)
                                            ).then_inc(M["cols_c"], 1)
                        dve.wait_ge(M["cols_c"], 3)
                        dve.tensor_tensor(wend[:], dend[:], acc_c[:], ALU.subtract).then_inc(M["wend0"], 1)

                        def difference(n):
                            c, b = n // NB, n % NB
                            dve.wait_ge(M[f"bc{n % 2}"], 16 * (n // 2 + 1))
                            if n >= 2:
                                dve.wait_ge(M["dec"], n - 1)
                            dve.tensor_tensor(seg_t[:, n % 2, :, :], bc[:, n % 2, :, :],
                                              acc_c[:, c, b * HB:(b + 1) * HB].unsqueeze(2).to_broadcast([P, HB, P]),
                                              ALU.subtract).then_inc(M["seg"], 1)
                            dve.wait_ge(M["seg"], n + 1)
                            dve.tensor_scalar(seg_t[:, n % 2, :, :], seg_t[:, n % 2, :, :], 0.0, None,
                                              ALU.min).then_inc(M["clip"], 1)
                            if c:
                                dve.wait_ge(M["grow"], n + 1 - NB)
                                dve.tensor_tensor(ce[:, n % 2, :, :], ce[:, n % 2, :, :],
                                                  xbc[:, MT + MG + b // 2, c * P:(c + 1) * P].unsqueeze(1)
                                                  .to_broadcast([P, HB, P]), ALU.mult).then_inc(M["ce"], 1)

                        for c in range(TB):
                            w = slice(c * P, (c + 1) * P)
                            for r in range(4):
                                dve.wait_ge(M["bt"], 6 * c + r + 1)
                                if c:
                                    dve.wait_ge(M["yd"], NB * c)
                                    dve.wait_ge(M["xw"], c)
                                dve.tensor_tensor(xdt[:, 8 * r:8 * r + 8, :],
                                                  ps[:, 4 + r % 2, :].rearrange("p (h d) -> p h d", h=8),
                                                  dtc[:, c, 8 * r:8 * r + 8].unsqueeze(2).to_broadcast([P, 8, HD]),
                                                  ALU.mult).then_inc(M["xdt"], 1)
                            dve.wait_ge(M["bt"], 6 * c + (6 if c < TB - 1 else 5))
                            if c:
                                dve.wait_ge(M["mat"], NB * c)
                            dve.tensor_tensor(cb[:], ps[:, 5, :].rearrange("p (g t) -> p g t", g=MG),
                                              consts[:, CST["upper"], :].unsqueeze(1).to_broadcast([P, MG, P]),
                                              ALU.mult).then_inc(M["cbm"], 1)
                            difference(c * NB)
                            if c < TB - 1:
                                dve.wait_ge(M["xdt"], 4 * c + 4)
                                dve.wait_ge(M["ends"], 2)
                                if c:
                                    dve.wait_ge(M["st"], MG * c)
                                dve.tensor_tensor(xw[:], xdt[:],
                                                  wend[:, c, :].unsqueeze(2).to_broadcast([P, MH, HD]),
                                                  ALU.mult).then_inc(M["xw"], 1)
                            for g in range(MG):
                                gi = c * MG + g
                                for b in range(2):
                                    n = c * NB + g * 2 + b
                                    if n % NB < NB - 1:
                                        difference(n + 1)
                                    for p in taken_at(n):
                                        split_lo(dve, c0 + p + 2, 0)
                                dve.wait_ge(M["yd"], 2 * gi + 2)
                                for j in range(4):
                                    t = 4 * g + j
                                    dve.scalar_tensor_tensor(out=xbc[:, t, w], in0=xbc[:, t, w],
                                                             scalar=v("m_d", t),
                                                             in1=ps[:, 6 + gi % 2, j * P:(j + 1) * P],
                                                             op0=ALU.mult, op1=ALU.add).then_inc(M["yskip"], 1)
                                if c == TB - 1:
                                    dve.wait_ge(M["yskip"], 4 * gi + 4)
                                    dve.wait_ge(G["z"], 2 * g + 2)
                                    gate_part(dve, g)
                            if c < TB - 1:
                                for g in range(MG):
                                    n = c * MG + g
                                    dve.wait_ge(M["st"], n + 1)
                                    if c == 0:
                                        dve.tensor_copy(state[:, g, :], ps[:, 4 + g % 2, :]).then_inc(M["state"], 1)
                                    else:
                                        s3 = state[:, g, :].rearrange("p (h d) -> p h d", h=GH)
                                        dve.tensor_tensor(s3, s3, dend[:, c, g * GH:(g + 1) * GH].unsqueeze(2)
                                                          .to_broadcast([P, GH, HD]),
                                                          ALU.mult).then_inc(M["decay"], 1)
                                        dve.wait_ge(M["decay"], n - MG + 1)
                                        dve.tensor_tensor(state[:, g, :], state[:, g, :], ps[:, 4 + g % 2, :],
                                                          ALU.add).then_inc(M["state"], 1)
                        for g in range(MG):
                            if g == MG - 1:
                                split_lo(dve, cm + 2, 0)
                            norm_part(dve, g)
                            lo_part(dve, g)
                        for k in range(1, MT // 2 - 1):
                            split_lo(dve, cm + k + 2, 0)
                        dve.wait_ge(x_back, 16)

        with ExitStack() as seg:
            k2 = sbuf(seg, "k2", [P, KT, S])
            v2 = sbuf(seg, "v2", [P, TB, D])
            q2 = sbuf(seg, "q2", [P, KT, S])
            z2 = sbuf(seg, "z2", [P, KT, S])
            with ExitStack() as tmp:
                h2hi = sbuf(tmp, "h2hi", [P, KT, S], F32R)
                h2lo = sbuf(tmp, "h2lo", [P, KT, S], F32R)
                boundary(None, "mg", [(v("kv_norm"), "kvsc", "kvsh", hhi, hlo),
                                      (v("norm2", KT, KT), "ssc", "ssh", h2hi, h2lo)], room=z2,
                         panel=(FIRST["k2"], 52), count=2)
                c0, q0 = FIRST["k2"], 52
                segs = [("k2", False, (hhi, hlo)), ("v2", True, (hhi, hlo)), ("q2", False, (h2hi, h2lo)),
                        ("z2", False, (h2hi, h2lo))]
                with nc.Block() as block:
                    @block.sync
                    def _(sp):
                        for r in range(2):
                            load_ada(sp, NADA - 2 + r, 0)
                        stream(sp, "k2", load=True)
                        stream(sp, "v2", load=True)
                        stream(sp, "q2", load=True)
                        stream(sp, "z2", load=True)

                    @block.gpsimd
                    def _(pool):
                        for r in range(2):
                            ada_multiply(pool, NADA - 2 + r, 0)

                    @block.scalar
                    def _(act):
                        for s, (name, by_token, _) in enumerate(segs):
                            def step(i, r, s=s, name=name):
                                pair = (q0 + r) % 2
                                act.wait_ge(panels_used, at(c0 + 4 * s + r + 1, i))
                                bank = ps[:, 2 * pair:2 * pair + 2, :]
                                if name == "v2":
                                    act.activation(v2[:, :, bass.ds(r * 256 + i * 512, 256)],
                                                   bank.rearrange("p a (b c) -> p (a b) c", b=2),
                                                   ACT.Copy).then_inc(pair_free[pair], 1)
                                else:
                                    dst = {"k2": k2, "q2": q2, "z2": z2}[name]
                                    act.activation(dst[:, bass.ds(2 * r + i * 4, 2), :], bank,
                                                   ACT.Silu if name == "z2" else ACT.Copy,
                                                   scale=HD ** -0.5 if name == "q2" else 1.0
                                                   ).then_inc(pair_free[pair], 1)
                                if c0 + 4 * s + 4 + 2 <= NPAN:
                                    split_hi(act, c0 + 4 * s + r + 2, i)
                            pairs(act, 4, step)

                    @block.vector
                    def _(dve):
                        for r in range(2):
                            split_lo(dve, c0 + r + 2, 0)
                        for r in range(2):
                            ada_sum(dve, NADA - 2 + r, 0)
                        pairs(dve, 14, lambda i, r: split_lo(dve, c0 + r + 4, i))
                        read_mod(dve, NADA - 2, NADA)

                    @block.tensor
                    def _(pe):
                        for s, (_, by_token, src) in enumerate(segs):
                            if s == 1:
                                for r in range(2):
                                    ada_columns(pe, NADA - 2 + r, 0)
                            skip = 0 if s else 2
                            pairs(pe, 4 - skip, lambda i, r: in_panel(pe, c0 + 4 * s + skip + r,
                                                                      q0 + 4 * s + skip + r, i, src, by_token))

            NU = TB * H2
            with ExitStack() as tmp:
                sig = sbuf(tmp, "sig", [P, 2, S])
                keep = sbuf(tmp, "keep", [P, 2, S])
                rest = sbuf(tmp, "rest", [P, 2, S + 1])
                zero = sbuf(tmp, "zero", [P, S])
                am = sbuf(tmp, "am", [P, 2, S])
                amt = sbuf(tmp, "amt", [P, 2, S])
                o2 = sbuf(tmp, "o2", [P, 2, D])
                og = sbuf(tmp, "og", [P, 2, 4, P])
                B = {k: sem("b_" + k) for k in ("zero", "z_done", "sig", "keep", "rest", "am", "t_done", "amt",
                                                "pv_done", "o_ready", "ot_done", "og", "ohi", "olo")}
                units = [(qb, h) for qb in range(TB) for h in range(H2)]
                with nc.Block() as block:
                    @block.tensor
                    def _(pe):
                        def logits(n):
                            qb, h = units[n]
                            nk = (qb + 1) * P
                            r0 = HD * (h % 2)
                            if n >= 2:
                                pe.wait_ge(B["keep"], n - 1)
                            pe.matmul(ps[:, n % 2, 0:nk], q2[r0:r0 + HD, h // 2, qb * P:nk],
                                      k2[r0:r0 + HD, h // 2, 0:nk], start=True, stop=False)
                            pe.matmul(ps[:, n % 2, qb * P:nk], ident, consts[:, CST["neg_from"], :],
                                      start=False, stop=True).then_inc(B["z_done"], 1)

                        def turn(n):
                            qb, h = units[n]
                            pe.wait_ge(B["am"], n + 1)
                            if n >= 2:
                                pe.wait_ge(B["amt"], n - 1)
                            for kb in range(qb + 1):
                                mm = pe.transpose(ps[:, 2 + n % 2, kb * P:(kb + 1) * P],
                                                  am[:, n % 2, kb * P:(kb + 1) * P], ident)
                            mm.then_inc(B["t_done"], 1)

                        def values(n):
                            qb, h = units[n]
                            half = n // 8
                            pe.wait_ge(B["amt"], n + 1)
                            if n % 8 == 0 and half >= 2:
                                pe.wait_ge(B["o_ready"], half - 1)
                            for kb in range(qb + 1):
                                mm = pe.matmul(ps[:, 4 + half % 2, (h % 8) * HD:(h % 8 + 1) * HD],
                                               amt[:, n % 2, kb * P:(kb + 1) * P],
                                               v2[:, kb, h * HD:(h + 1) * HD], start=kb == 0, stop=kb == qb)
                            mm.then_inc(B["pv_done"], 1)

                        def turn_out(half):
                            pe.wait_ge(B["o_ready"], half + 1)
                            if half >= 2:
                                pe.wait_ge(B["og"], half - 1)
                            for t in range(4):
                                mm = pe.transpose(ps[:, 6 + half % 2, t * P:(t + 1) * P],
                                                  o2[:, half % 2, t * P:(t + 1) * P], ident)
                            mm.then_inc(B["ot_done"], 1)

                        for n in range(NU + 5):
                            if n < NU:
                                logits(n)
                            if 2 <= n <= NU + 1:
                                turn(n - 2)
                            if 3 <= n <= NU + 2:
                                values(n - 3)
                            if n >= 12 and (n - 4) % 8 == 0:
                                turn_out((n - 4) // 8 - 1)

                    @block.scalar
                    def _(act):
                        def take(n):
                            qb, h = units[n]
                            nk = (qb + 1) * P
                            act.wait_ge(B["t_done"], n + 1)
                            if n >= 2:
                                act.wait_ge(B["pv_done"], n - 1)
                            act.activation(amt[:, n % 2, 0:nk], ps[:, 2 + n % 2, 0:nk], ACT.Copy).then_inc(B["amt"], 1)

                        def out_take(half):
                            act.wait_ge(B["pv_done"], 8 * half + 8)
                            if half >= 2:
                                act.wait_ge(B["ot_done"], half - 1)
                            act.activation(o2[:, half % 2, 0:512], ps[:, 4 + half % 2, :],
                                           ACT.Copy).then_inc(B["o_ready"], 1)

                        def out_hi(half):
                            qb, t0 = half // 2, 4 * (half % 2)
                            act.wait_ge(B["og"], half + 1)
                            act.activation(hhi[:, t0:t0 + 4, qb * P:(qb + 1) * P], og[:, half % 2, :, :],
                                           ACT.Copy).then_inc(B["ohi"], 1)

                        for n in range(NU + 6):
                            if n < NU:
                                qb, h = units[n]
                                nk = (qb + 1) * P
                                act.wait_ge(B["z_done"], n + 1)
                                if n >= 2:
                                    act.wait_ge(B["am"], n - 1)
                                act.activation(sig[:, n % 2, 0:nk], ps[:, n % 2, 0:nk],
                                               ACT.Sigmoid).then_inc(B["sig"], 1)
                                act.activation(keep[:, n % 2, 0:nk], ps[:, n % 2, 0:nk], ACT.Sigmoid,
                                               scale=-1.0).then_inc(B["keep"], 1)
                            if 2 <= n <= NU + 1:
                                take(n - 2)
                            if n >= 11 and (n - 3) % 8 == 0:
                                out_take((n - 3) // 8 - 1)
                            if n >= 13 and (n - 5) % 8 == 0:
                                out_hi((n - 5) // 8 - 1)

                    @block.gpsimd
                    def _(pool):
                        for n, (qb, h) in enumerate(units):
                            nk = (qb + 1) * P
                            pool.wait_ge(B["rest"], n + 1)
                            if n >= 2:
                                pool.wait_ge(B["t_done"], n - 1)
                            pool.tensor_tensor(am[:, n % 2, 0:nk], sig[:, n % 2, 0:nk], rest[:, n % 2, 1:nk + 1],
                                               ALU.mult).then_inc(B["am"], 1)

                    @block.vector
                    def _(dve):
                        dve.memset(zero[:], 0.0).then_inc(B["zero"], 1)
                        dve.wait_ge(B["zero"], 1)

                        def out_gate(half):
                            qb, t0 = half // 2, 4 * (half % 2)
                            dve.wait_ge(B["ot_done"], half + 1)
                            if half >= 2:
                                dve.wait_ge(B["olo"], half - 1)
                            dve.tensor_tensor(og[:, half % 2, :, :],
                                              ps[:, 6 + half % 2, :].rearrange("p (t q) -> p t q", t=4),
                                              z2[:, t0:t0 + 4, qb * P:(qb + 1) * P], ALU.mult).then_inc(B["og"], 1)

                        def out_lo(half):
                            qb, t0 = half // 2, 4 * (half % 2)
                            dve.wait_ge(B["ohi"], half + 1)
                            dve.tensor_tensor(hlo[:, t0:t0 + 4, qb * P:(qb + 1) * P], og[:, half % 2, :, :],
                                              hhi[:, t0:t0 + 4, qb * P:(qb + 1) * P].bitcast(F32),
                                              ALU.subtract).then_inc(B["olo"], 1)
                        for n in range(NU + 7):
                            if n < NU:
                                qb, h = units[n]
                                nk = (qb + 1) * P
                                if n >= 2:
                                    dve.wait_ge(B["am"], n - 1)
                                dve.memset(rest[:, n % 2, nk:nk + 1], 1.0).then_inc(B["zero"], 1)
                                dve.wait_ge(B["keep"], n + 1)
                                dve.tensor_tensor_scan(rest[:, n % 2, 0:nk][:, ::-1], keep[:, n % 2, 0:nk][:, ::-1],
                                                       zero[:, 0:nk], 1.0, ALU.mult,
                                                       ALU.add).then_inc(B["rest"], 1)
                            if n >= 12 and (n - 4) % 8 == 0:
                                out_gate((n - 4) // 8 - 1)
                            if n >= 14 and (n - 6) % 8 == 0:
                                out_lo((n - 6) // 8 - 1)
            out_block("sb_out", [(hhi, hlo)])
        boundary(None, "sg", [], final=True)


def _tiles(a):
    return a.reshape(-1, P).T


def _in_panel(w):
    return w.reshape(KT, P, 2, P).transpose(1, 0, 2, 3).reshape(P, 2048)


def _in_panels(w):
    return [_in_panel(w[:, i:i + 256]) for i in range(0, w.shape[1], 256)]


def _paired_panels(a, b):
    return [_in_panel(np.concatenate([a[:, i:i + P], b[:, i:i + P]], 1)) for i in range(0, a.shape[1], P)]


def _out_panels(w):
    w = w.reshape(-1, 2, P, KT, P).transpose(0, 2, 1, 3, 4)
    return [p.reshape(P, 2048) for p in w]


def _half_panels(w):
    w = w.reshape(-1, 4, P, 2, 4, P).transpose(3, 0, 2, 1, 4, 5)
    return [p.reshape(P, 2048) for p in w.reshape(-1, P, 2048)]


def _padded(a):
    return np.concatenate([a, np.zeros(P - a.shape[0], a.dtype)])[:, None]


def _by_chunk(a):
    return np.tile(a, TB)[:, None]


def kernel(**inputs):
    import concourse.bacc as bacc
    from concourse.bass_utils import run_bass_kernel_spmd

    g = {k: np.asarray(a) for k, a in inputs.items()}
    w_in = g["w_in"][0]
    w_ffn = g["w_ffn_in"][0]
    m_in = g["m_in_w_2"][0]
    sb_in = g["sb_in_w_2"][0]
    a3 = 3 * AW
    weights = (_paired_panels(w_in[:, a3 + H1:a3 + H1 + AW], w_in[:, a3 + H1 + AW:])
               + _in_panels(w_in[:, 0:a3])
               + _out_panels(g["w_o"][0])
               + _paired_panels(w_ffn[:, 0:DFF], w_ffn[:, DFF:])
               + _out_panels(g["w_ffn_out"][0])
               + _in_panels(m_in[:, MI:MI + XT * P])
               + _in_panels(m_in[:, 0:MI])
               + _half_panels(g["m_out_w_2"][0])
               + _in_panels(g["kv_w_2"])
               + _in_panels(sb_in)
               + _out_panels(g["sb_out_w_2"][0]))
    ada_w = np.concatenate([g["ada_w"][0], g["ada_w_2"][0], g["kv_ada_w_2"], g["ada_w_2"][1]], 1)
    ada_b = np.concatenate([g["ada_b"][0], g["ada_b_2"][0], g["kv_ada_b_2"], g["ada_b_2"][1]])
    ada = [ada_w[:, i:i + 256].reshape(KT, P, 256).transpose(1, 0, 2).reshape(P, 2048)
           for i in range(0, ada_w.shape[1], 256)]
    vectors = dict(
        c=_tiles(g["c"]), c2=_tiles(g["c_2"]), ada_b=_tiles(ada_b), mix_pre=_tiles(g["mix_pre_g"]),
        mix_post=_tiles(g["mix_post_g"]), ffn_pre=_tiles(g["ffn_pre_g"]), ffn_post=_tiles(g["ffn_post_g"]),
        conv_w=g["conv_w"][0].reshape(CK, CT, P).transpose(2, 1, 0).reshape(P, CT * CK),
        conv_b=_tiles(g["conv_b"]), ln_g=_tiles(g["conv_ln_g"]), ln_b=_tiles(g["conv_ln_b"]),
        norm2=_tiles(g["norm_g_2"]),
        mconv_w=g["m_conv_w_2"][0].reshape(MK, XT, P).transpose(2, 1, 0).reshape(P, XT * MK),
        mconv_b=_tiles(g["m_conv_b_2"]), m_norm=_tiles(g["m_norm_g_2"]),
        m_d=_tiles(np.repeat(g["m_d_2"][0], HD)), kv_norm=_tiles(g["kv_norm_g_2"]),
        final=_tiles(g["final_g_2"]), b_f=_padded(g["b_f"][0]), dt_bias=_by_chunk(g["m_dt_bias_2"][0]),
        a_log=_by_chunk(g["m_a_log_2"][0]))
    i = np.arange(P)
    shapes = np.stack([np.eye(P), i[:, None] <= i[None, :], (i[None, :] > i[:, None]) * NEG,
                       (i[None, :] >= i[:, None]) * NEG, np.ones((P, P))], 1).astype(np.float32)
    arrays = {
        "x_in": g["x"][0].T.reshape(KT, P, S).transpose(1, 0, 2),
        "panels": np.stack(weights),
        "ada": np.stack(ada),
        "vecs": np.concatenate([vectors[k] for k in VEC], 1),
        "cst": shapes.reshape(P, 5 * P),
        "w_f": w_in[:, a3:a3 + H1].reshape(KT, P, H1).transpose(1, 0, 2).reshape(P, KT * H1),
        "w_dt": m_in[:, MI + XT * P:].reshape(KT, P, MH).transpose(1, 0, 2).reshape(P, KT * MH),
    }
    arrays = {k: np.ascontiguousarray(a) for k, a in arrays.items()}
    nc = bacc.Bacc("TRN2", target_bir_lowering=False, num_devices=1, dynamic_dma_scratch_size=1024)
    args = [nc.dram_tensor(k, a.shape, mybir.dt.from_np(a.dtype), kind="ExternalInput").ap()
            for k, a in arrays.items()]
    out = nc.dram_tensor("out", (KT, P, S), F32, kind="ExternalOutput").ap()
    scratch = [nc.dram_tensor("x_kept", (P, KT, S), F32, kind="Internal").ap(),
               nc.dram_tensor("ac_rows", (MH, S), F32, kind="Internal").ap()]
    build(nc, *args, *scratch, out)
    r = run_bass_kernel_spmd(nc, [arrays], core_ids=[0])
    return r.results[0]["out"].reshape(D, S).T.reshape(1, S, D)
```
